# Optimizing a Trainium2 kernel written in Bass

```python
import math
import jax, jax.numpy as jnp
from jax import lax
import numpy as np

D_MODEL = 2048
BATCH = 1
SEQ = 1024
DEPTH = 1
DEC_BATCH = 8
DEC_SEQ = 16
PAST_LEN = 512

CHUNK = 64
Q_BLOCK = 128
EPS = 1e-6
D_CONV = D_MODEL // 2
CONV_WIDTH = 3
D_ATTN = D_MODEL - D_CONV
N_HEADS = 8
HEAD_DIM = D_ATTN // (2 * N_HEADS)
V_DIM = 2 * HEAD_DIM
D_PROJ = 3 * D_CONV + 3 * D_ATTN
SPLITS = (D_CONV, 2 * D_CONV, 3 * D_CONV, 3 * D_CONV + D_ATTN, 3 * D_CONV + 2 * D_ATTN)
N_GROUPS = 4
EXPERTS_PER_GROUP = 8
N_EXPERTS = N_GROUPS * EXPERTS_PER_GROUP
TOP_K = 2
D_EXPERT = 512

kernel_name = "hymba_conv_diffattn_hiermoe_stream_step"

def rms_norm(x, g):
    xf = x.astype(jnp.float32)
    y = xf * lax.rsqrt(jnp.mean(xf * xf, axis=-1, keepdims=True) + EPS)
    return (y * g.astype(jnp.float32)).astype(x.dtype)

def diff_lambda(lq1, lk1, lq2, lk2, lam_init):
    f = jnp.float32
    return (jnp.exp(jnp.sum(lq1.astype(f) * lk1.astype(f)))
            - jnp.exp(jnp.sum(lq2.astype(f) * lk2.astype(f))) + lam_init)

def diff_attend(q, k, v, mask, lam):
    s = jnp.einsum('bqhmd,bkhmd->bmhqk', q, k).astype(jnp.float32) * (HEAD_DIM ** -0.5)
    if mask is not None:
        s = jnp.where(mask, s, -jnp.inf)
    p = jax.nn.softmax(s, axis=-1)
    a = p[:, 0] - lam * p[:, 1]
    return jnp.einsum('bhqk,bkhe->bqhe', a.astype(v.dtype), v)

def prompt_diff_attention(q, k, v, lam):
    B, T = q.shape[:2]
    nb = T // Q_BLOCK
    qb = q.reshape(B, nb, Q_BLOCK, N_HEADS, 2, HEAD_DIM).transpose(1, 0, 2, 3, 4, 5)
    k_chunk = jnp.arange(T) // CHUNK

    def one(args):
        i, qi = args
        q_chunk = (i * Q_BLOCK + jnp.arange(Q_BLOCK)) // CHUNK
        mask = k_chunk[None, :] <= q_chunk[:, None]
        return diff_attend(qi, k, v, mask, lam)

    o = lax.map(one, (jnp.arange(nb), qb))
    return o.transpose(1, 0, 2, 3, 4).reshape(B, T, N_HEADS, V_DIM)

def short_conv(b_gate, c_gate, x_in, prev, conv_w):
    u = c_gate * x_in
    u_ext = jnp.concatenate([prev, u], axis=1)
    T = u.shape[1]
    y = sum(conv_w[j] * u_ext[:, j:j + T] for j in range(CONV_WIDTH))
    return b_gate * y, u_ext[:, -(CONV_WIDTH - 1):]

def mixer_sublayer(x, conv_prev, k_past, v_past, norm_g, w_in, conv_w, lam, lam_init, head_norm, w_out):
    B, T = x.shape[:2]
    z = rms_norm(x, norm_g) @ w_in
    b_gate, c_gate, x_in, q, k, v = jnp.split(z, SPLITS, axis=-1)
    q = q.reshape(B, T, N_HEADS, 2, HEAD_DIM)
    k = k.reshape(B, T, N_HEADS, 2, HEAD_DIM)
    v = v.reshape(B, T, N_HEADS, V_DIM)
    a, conv_state = short_conv(b_gate, c_gate, x_in, conv_prev, conv_w)
    if k_past is None:
        o = prompt_diff_attention(q, k, v, lam)
    else:
        o = diff_attend(q, jnp.concatenate([k_past, k], axis=1),
                        jnp.concatenate([v_past, v], axis=1), None, lam)
    o = (rms_norm(o, head_norm) * (1.0 - lam_init)).reshape(B, T, D_ATTN)
    y = jnp.concatenate([a, o], axis=-1) @ w_out
    return x + y, k, v, conv_state

def hier_moe(h, w_rg, b_rg, w_re, b_re, w_ei, w_eo):
    B, T, D = h.shape
    n = B * T
    f32 = jnp.float32
    hf = h.reshape(n, D)
    lg = (hf @ w_rg).astype(f32) + b_rg.astype(f32)
    pg = jax.nn.softmax(lg, axis=-1)
    g = jnp.argmax(lg, axis=-1)
    gate_g = jnp.take_along_axis(pg, g[:, None], axis=-1)
    le = ((hf @ w_re).astype(f32) + b_re.astype(f32)).reshape(n, N_GROUPS, EXPERTS_PER_GROUP)
    le_g = jnp.take_along_axis(le, g[:, None, None], axis=1)[:, 0]
    top_v, top_i = lax.top_k(le_g, TOP_K)
    w_tok = gate_g * jax.nn.softmax(top_v, axis=-1)
    eid = (g[:, None] * EXPERTS_PER_GROUP + top_i).reshape(-1)
    tok = jnp.repeat(jnp.arange(n), TOP_K)
    order = jnp.argsort(eid)
    tok_s = tok[order]
    w_s = w_tok.reshape(-1)[order]
    sizes = jnp.bincount(eid, length=N_EXPERTS).astype(jnp.int32)
    xs = hf[tok_s]
    gu = lax.ragged_dot(xs, w_ei, sizes)
    gate, up = jnp.split(gu, 2, axis=-1)
    ys = lax.ragged_dot(jax.nn.silu(gate) * up, w_eo, sizes)
    y = jnp.zeros_like(hf).at[tok_s].add(ys * w_s[:, None].astype(ys.dtype))
    return y.reshape(B, T, D)

def setup_inputs(seed: int = 0) -> dict:
    key = jax.random.key(seed)
    ks = jax.random.split(key, 24)
    nrm = lambda k, s, sc: jax.random.normal(k, s, jnp.float32) * sc
    L = DEPTH
    return {
        "x_prompt": nrm(ks[0], (BATCH, SEQ, D_MODEL), 1.0),
        "x_sample": nrm(ks[1], (DEC_BATCH, DEC_SEQ, D_MODEL), 1.0),
        "cache_k": nrm(ks[2], (L, DEC_BATCH, PAST_LEN, N_HEADS, 2, HEAD_DIM), 1.0),
        "cache_v": nrm(ks[3], (L, DEC_BATCH, PAST_LEN, N_HEADS, V_DIM), 1.0),
        "state_conv": nrm(ks[4], (L, DEC_BATCH, CONV_WIDTH - 1, D_CONV), 1.0),
        "norm_mix": 1.0 + nrm(ks[5], (L, D_MODEL), 0.02),
        "w_in": nrm(ks[6], (L, D_MODEL, D_PROJ), D_MODEL ** -0.5),
        "conv_w": nrm(ks[7], (L, CONV_WIDTH, D_CONV), CONV_WIDTH ** -0.5),
        "lambda_q1": nrm(ks[8], (L, HEAD_DIM), 0.1),
        "lambda_k1": nrm(ks[9], (L, HEAD_DIM), 0.1),
        "lambda_q2": nrm(ks[10], (L, HEAD_DIM), 0.1),
        "lambda_k2": nrm(ks[11], (L, HEAD_DIM), 0.1),
        "head_norm": 1.0 + nrm(ks[12], (L, V_DIM), 0.02),
        "w_out": nrm(ks[13], (L, D_MODEL, D_MODEL), D_MODEL ** -0.5),
        "norm_ffn": 1.0 + nrm(ks[14], (L, D_MODEL), 0.02),
        "w_router_group": nrm(ks[15], (L, D_MODEL, N_GROUPS), D_MODEL ** -0.5),
        "b_router_group": nrm(ks[16], (L, N_GROUPS), 0.01),
        "w_router_expert": nrm(ks[17], (L, D_MODEL, N_EXPERTS), D_MODEL ** -0.5),
        "b_router_expert": nrm(ks[18], (L, N_EXPERTS), 0.01),
        "w_expert_in": nrm(ks[19], (L, N_EXPERTS, D_MODEL, 2 * D_EXPERT), D_MODEL ** -0.5),
        "w_expert_out": nrm(ks[20], (L, N_EXPERTS, D_EXPERT, D_MODEL), D_EXPERT ** -0.5),
        "norm_final": 1.0 + nrm(ks[21], (D_MODEL,), 0.02),
    }

def reference(x_prompt, x_sample, cache_k, cache_v, state_conv, norm_mix, w_in, conv_w,
              lambda_q1, lambda_k1, lambda_q2, lambda_k2, head_norm, w_out, norm_ffn,
              w_router_group, b_router_group, w_router_expert, b_router_expert,
              w_expert_in, w_expert_out, norm_final):
    hp, hs = x_prompt, x_sample
    kp_l, vp_l, cp_l, ks_l, vs_l, cs_l = [], [], [], [], [], []
    for l in range(DEPTH):
        lam_init = 0.8 - 0.6 * math.exp(-0.3 * l)
        lam = diff_lambda(lambda_q1[l], lambda_k1[l], lambda_q2[l], lambda_k2[l], lam_init)
        zero_conv = jnp.zeros((hp.shape[0], CONV_WIDTH - 1, D_CONV), hp.dtype)
        hp, kp, vp, cp = mixer_sublayer(hp, zero_conv, None, None, norm_mix[l], w_in[l], conv_w[l],
                                        lam, lam_init, head_norm[l], w_out[l])
        hp = hp + hier_moe(rms_norm(hp, norm_ffn[l]), w_router_group[l], b_router_group[l],
                           w_router_expert[l], b_router_expert[l], w_expert_in[l], w_expert_out[l])
        hs, ksn, vsn, csn = mixer_sublayer(hs, state_conv[l], cache_k[l], cache_v[l], norm_mix[l], w_in[l],
                                           conv_w[l], lam, lam_init, head_norm[l], w_out[l])
        hs = hs + hier_moe(rms_norm(hs, norm_ffn[l]), w_router_group[l], b_router_group[l],
                           w_router_expert[l], b_router_expert[l], w_expert_in[l], w_expert_out[l])
        kp_l.append(kp); vp_l.append(vp); cp_l.append(cp)
        ks_l.append(ksn); vs_l.append(vsn); cs_l.append(csn)
    y_prompt = rms_norm(hp, norm_final)
    y_sample = rms_norm(hs, norm_final)
    k_prompt = jnp.stack(kp_l)
    v_prompt = jnp.stack(vp_l)
    conv_prompt = jnp.stack(cp_l)
    k_sample = jnp.stack(ks_l)
    v_sample = jnp.stack(vs_l)
    conv_sample = jnp.stack(cs_l)
    return (y_prompt, y_sample, k_prompt, v_prompt, conv_prompt, k_sample, v_sample, conv_sample)


_drawn_inputs = setup_inputs


def setup_inputs(seed=0):
    import zlib

    import numpy as np

    out = dict(_drawn_inputs(seed))
    spreads = {}
    factors = {'lambda_k1': 6.625,
     'lambda_q2': 6.894,
     'head_norm': 9.5,
     'b_router_group': 15.372,
     'b_router_expert': 14.56,
     'norm_final': 7.59,
     'norm_ffn': 3.838}
    for name, (base, spread) in spreads.items():
        noise = np.random.default_rng([zlib.crc32(name.encode()), seed]).standard_normal(out[name].shape)
        drawn = base * np.exp(spread * noise) if base else spread * noise
        out[name] = __import__('jax').numpy.asarray(drawn.astype(out[name].dtype))
    for name, factor in factors.items():
        out[name] = (out[name] * factor).astype(out[name].dtype)
    return out
```

```python
from contextlib import ExitStack

import numpy as np
import concourse.bass as bass
from concourse import mybir

F32 = mybir.dt.float32
F32R = mybir.dt.float32r
I32 = mybir.dt.int32
U32 = mybir.dt.uint32
ALU = mybir.AluOpType
ACT = mybir.ActivationFunctionType
AX = mybir.AxisListType
ds = bass.ds

P = 128
D = 2048
PROMPT = 1024
STREAMS = 8
NEW = 16
PAST = 512
TOK = PROMPT + STREAMS * NEW
NT = TOK // P
KT = D // P
HALF = KT // 2
NB = 3
BLK = TOK // NB
DC = D // 2
CH = DC // P
HEADS = 8
DH = 64
VD = 128
SCALE = DH ** -0.5
LAM_INIT = 0.8 - 0.6
EPS = 1e-6
MASKED = -1e30
GROUPS = 4
PER = 8
EXPERTS = GROUPS * PER
TOPK = 2
DE = 512
NR = GROUPS + EXPERTS
MAXT = TOPK * NT + EXPERTS - 1
BIG = 1e30
NO_ROW = 1 << 20
U = 2 * D


class Ctx:

    def __init__(self, nc, io):
        self.nc, self.io, self.in_use = nc, io, []
        self.passed = nc.alloc_semaphore("passed")

    def sem(self, name):
        self.in_use.append(self.nc.alloc_semaphore(name))
        return self.in_use[-1]

    def clear_semaphores(self):
        self.nc.clear_and_free_semaphores(self.in_use)
        self.nc.all_engine_barrier()
        self.in_use = []

    def start_at_one(self, eng, *sems):
        for sem in sems:
            eng.sem_inc(sem, 1)

    def hold(self, eng):
        eng.sem_inc(self.passed, 1)

    def sems(self, name, n):
        return [self.sem(f"{name}{i}") for i in range(n)]


def phase_norm(c, hT_hi, hT_lo):
    nc, io, sem = c.nc, c.io, c.sem
    SL = 3
    with ExitStack() as mem:
        x = mem.enter_context(nc.sbuf_tensor("n_x", [P, SL, D], F32))
        g = mem.enter_context(nc.sbuf_tensor("n_g", [P, D], F32))
        ssq = mem.enter_context(nc.sbuf_tensor("n_ssq", [P, SL], F32))
        rstd = mem.enter_context(nc.sbuf_tensor("n_rstd", [P, SL], F32))
        small = mem.enter_context(nc.sbuf_tensor("n_small", [19, DC], F32))
        junk = mem.enter_context(nc.psum_tensor("n_junk", [P, D], F32))
        tp = mem.enter_context(nc.psum_tensor("n_tp", [P, 4, 512], F32))
        x_loaded = c.sems("n_x_loaded", SL)
        x_done = c.sems("n_x_done", SL)
        g_loaded, squared, ms_done = sem("n_g_loaded"), sem("n_squared"), sem("n_ms_done")
        small_loaded, small_turned, small_kept = sem("n_small_loaded"), sem("n_small_turned"), sem("n_small_kept")
        rstd_done, h_ready, turned = sem("n_rstd_done"), sem("n_h_ready"), sem("n_turned")
        hi_done, lo_done, ident0, ident_ready = sem("n_hi_done"), sem("n_lo_done"), sem("n_ident0"), sem("n_ident_ready")
        lam_loaded, lam_step = sem("n_lam_loaded"), sem("n_lam_step")
        lam_exp = sem("n_lam_exp")
        lamb = mem.enter_context(nc.sbuf_tensor("n_lamb", [P, 4, DH], F32))
        lw = mem.enter_context(nc.sbuf_tensor("n_lw", [P, 8], F32))
        with nc.Block() as block:

            @block.sync
            def _(sp):
                sp.dma_start(g[:], io.norm_mix.to_broadcast([P, D])).then_inc(g_loaded, 16)
                with sp.Fori(0, NT // SL) as i:
                    for s in range(SL):
                        sp.wait_ge(x_done[s], i + 1)
                        sp.dma_start(x[:, s, :], io.x[ds((i * SL + s) * P, P), :]).then_inc(x_loaded[s], 16)
                sp.dma_start(small[:], io.small).then_inc(small_loaded, 16)
                sp.dma_start(lamb[:].rearrange("p a b -> p (a b)"), io.lam.to_broadcast([P, 4 * DH])).then_inc(lam_loaded, 16)
                sp.dma_start(c.hn[:], io.head_norm.to_broadcast([P, VD])).then_inc(lam_loaded, 16)

            @block.gpsimd
            def _(pool):
                pool.memset(c.ident[:], 0.0).then_inc(ident0, 1)
                pool.wait_ge(ident0, 1)
                pool.affine_select(out=c.ident[:], in_=c.ident[:], compare_op=ALU.not_equal, fill=1.0, base=0,
                                   pattern=[[-1, P]], channel_multiplier=1).then_inc(ident_ready, 1)
                pool.memset(c.eps[:], EPS).then_inc(ident_ready, 1)

            @block.scalar
            def _(act):
                def root(s, t):
                    act.activation(junk[:], x[:, s, :], ACT.Square, accum_out=ssq[:, s:s + 1]).then_inc(squared, 1)
                    act.wait_ge(squared, t + 1)
                    act.activation(ssq[:, s:s + 1], ssq[:, s:s + 1], ACT.Sqrt, bias=c.eps[:], scale=1.0 / D).then_inc(ms_done, 1)

                act.wait_ge(ident_ready, 2)
                act.wait_ge(x_loaded[0], 16)
                root(0, 0)

                def keep_hi(t, n):
                    for q in range(4):
                        act.wait_ge(turned, 4 * n + q + 1)
                        act.activation(hT_hi[:, 4 * q:4 * q + 4, ds(t * P, P)],
                                       tp[:, q, :].rearrange("p (a b) -> p a b", a=4), ACT.Copy).then_inc(hi_done, 1)

                with act.Fori(0, NT // SL - 1) as i:
                    for s in range(SL):
                        nx = (s + 1) % SL
                        act.wait_ge(x_loaded[nx], 16 * (i + 1 + (s == SL - 1)))
                        act.wait_ge(rstd_done, i * SL + s + 1)
                        root(nx, i * SL + s + 1)
                        keep_hi(i * SL + s, i * SL + s)
                for s in range(SL):
                    t = NT - SL + s
                    if s < SL - 1:
                        act.wait_ge(x_loaded[s + 1], 16 * (NT // SL))
                        act.wait_ge(rstd_done, t + 1)
                        root(s + 1, t + 1)
                    keep_hi(t, t)
                act.wait_ge(lam_step, 2)
                act.activation(lw[:, 2:4], lw[:, 0:2], ACT.Exp).then_inc(lam_exp, 1)

            @block.vector
            def _(dve):
                dve.wait_ge(g_loaded, 16)
                with dve.Fori(0, NT // SL) as i:
                    for s in range(SL):
                        t = i * SL + s
                        dve.wait_ge(ms_done, t + 1)
                        dve.reciprocal(rstd[:, s:s + 1], ssq[:, s:s + 1]).then_inc(rstd_done, 1)
                        dve.wait_ge(rstd_done, t + 1)
                        dve.scalar_tensor_tensor(x[:, s, :], x[:, s, :], rstd[:, s:s + 1], g[:], ALU.mult,
                                                 ALU.mult).then_inc(h_ready, 1)
                        for q in range(4):
                            dve.wait_ge(hi_done, 4 * t + q + 1)
                            dve.tensor_tensor(hT_lo[:, 4 * q:4 * q + 4, ds(t * P, P)],
                                              tp[:, q, :].rearrange("p (a b) -> p a b", a=4),
                                              hT_hi[:, 4 * q:4 * q + 4, ds(t * P, P)], ALU.subtract).then_inc(lo_done, 1)
                dve.wait_ge(small_turned, 1)
                dve.tensor_copy(c.taps[:], tp[:, 0, 0:CH * 19].rearrange("p (a b) -> p a b", a=CH)).then_inc(small_kept, 1)
                dve.wait_ge(lam_loaded, 32)
                lv = lamb[:].rearrange("p (m a) d -> p m a d", m=2)
                dve.tensor_tensor(lv[:, :, 0, :], lv[:, :, 0, :], lv[:, :, 1, :], ALU.mult).then_inc(lam_step, 1)
                dve.wait_ge(lam_step, 1)
                dve.tensor_reduce(lw[:, 0:2], lv[:, :, 0, :], AX.X, ALU.add).then_inc(lam_step, 1)
                dve.wait_ge(lam_exp, 1)
                dve.scalar_tensor_tensor(c.neglam[:], lw[:, 3:4], -LAM_INIT, lw[:, 2:3], ALU.add, ALU.subtract).then_inc(lam_step, 1)
                dve.tensor_scalar(c.hn[:], c.hn[:], 1.0 - LAM_INIT, None, ALU.mult).then_inc(lam_step, 1)

            @block.tensor
            def _(pe):
                c.start_at_one(pe, *x_done, lo_done)
                pe.wait_ge(ident_ready, 1)
                with pe.Fori(0, NT // SL) as i:
                    for s in range(SL):
                        t = i * SL + s
                        pe.wait_ge(h_ready, t + 1)
                        for q in range(4):
                            pe.wait_ge(lo_done, 4 * t + 1)
                            for j in range(4):
                                k = 4 * q + j
                                mm = pe.transpose(tp[:, q, j * P:(j + 1) * P], x[:, s, k * P:(k + 1) * P], c.ident[:])
                            mm.then_inc(turned, 1)
                        pe.wait_ge(turned, 4 * t + 4)
                        pe.sem_inc(x_done[s], 1)
                pe.wait_ge(small_loaded, 16)
                pe.wait_ge(lo_done, 4 * NT + 1)
                for j in range(CH):
                    mm = pe.transpose(tp[:, 0, j * 19:(j + 1) * 19], small[:, j * P:(j + 1) * P], c.ident[0:19, 0:19])
                mm.then_inc(small_turned, 1)


def weight_chunks(c, tag, w_raw, w_hi, w_lo):
    loaded, split = c.sems(f"{tag}_w_loaded", 2), c.sems(f"{tag}_w_split", 2)
    hi_done, half0_used = c.sem(f"{tag}_w_hi_done"), c.sem(f"{tag}_half0_used")
    z_done, z_kept = c.sems(f"{tag}_z_done", NB), c.sems(f"{tag}_z_kept", NB)

    def load(sp, n, w_cols):
        for half in range(2):
            sp.wait_ge(split[half], n + 1)
            c.hold(sp)
            sp.dma_start(w_raw[:, half * HALF:(half + 1) * HALF, :], w_cols(half)).then_inc(loaded[half], 16)

    def split_chunk(pool, n):
        for half in range(2):
            part = slice(half * HALF, (half + 1) * HALF)
            pool.wait_ge(loaded[half], 16 * (n + 1))
            pool.wait_ge(half0_used if half == 0 else z_done[NB - 1], n + 1)
            c.hold(pool)
            pool.tensor_copy(w_hi[:, part, :], w_raw[:, part, :]).then_inc(hi_done, 1)
            pool.wait_ge(hi_done, 2 * n + half + 1)
            pool.tensor_tensor(w_lo[:, part, :], w_raw[:, part, :], w_hi[:, part, :], ALU.subtract).then_inc(split[half], 1)

    def products(pe, n, half, z, x_hi, x_lo):
        pe.wait_ge(split[half], n + 2)
        for b in range(NB):
            if half == 0:
                pe.wait_ge(z_kept[b], n + 1)
            cols = slice(b * BLK, (b + 1) * BLK)
            for j in range(HALF):
                k = half * HALF + j
                xk = k % x_hi.shape[1]
                out = z[:, b, 0:BLK]
                pe.matmul(out, w_hi[:, k, :], x_hi[:, xk, cols], start=(k == 0), stop=False)
                pe.matmul(out, w_hi[:, k, :], x_lo[:, xk, cols], start=False, stop=False)
                mm = pe.matmul(out, w_lo[:, k, :], x_hi[:, xk, cols], start=False, stop=(k == KT - 1))
            if half == 1:
                mm.then_inc(z_done[b], 1)
        if half == 0:
            mm.then_inc(half0_used, 1)

    return load, split_chunk, products, z_done, z_kept, (*split, half0_used, *z_done, *z_kept)


def phase_project(c, hT_hi, hT_lo):
    nc, io, sem = c.nc, c.io, c.sem
    NCONV = 3 * CH
    with ExitStack() as mem:
        def sb(name, shape, dt=F32):
            return mem.enter_context(nc.sbuf_tensor(name, shape, dt))

        w_raw = sb("p_w_raw", [P, KT, P])
        w_hi = sb("p_w_hi", [P, KT, P], F32R)
        w_lo = sb("p_w_lo", [P, KT, P], F32R)
        e = sb("p_e", [P, TOK])
        xs = sb("p_xs", [P, TOK])
        up = sb("p_up", [P, 2 + PROMPT])
        us = sb("p_us", [P, STREAMS, 2 + NEW])
        tail = sb("p_tail", [P, CH, 2 + 2 * STREAMS])
        rows = sb("p_rows", [P, NT, P])
        tail_rows = sb("p_tail_rows", [2 + 2 * STREAMS, DC])
        z = mem.enter_context(nc.psum_tensor("p_z", [P, NB, 512], F32))
        tp = mem.enter_context(nc.psum_tensor("p_tp", [P, NB, 512], F32))
        load, split_chunk, products, z_done, z_kept, first_counts = weight_chunks(c, "p", w_raw, w_hi, w_lo)
        zeroed, step = sem("p_zeroed"), sem("p_conv_step")
        e_ready, e_stored = sem("p_e_ready"), sem("p_e_stored")
        e_turned, rows_ready, rows_stored = sem("p_e_turned"), sem("p_rows_ready"), sem("p_rows_stored")
        tail_turned, tail_kept, tail_stored = sem("p_tail_turned"), sem("p_tail_kept"), sem("p_tail_stored")

        w = io.w_in.rearrange("(h k p) n -> h p k n", h=2, p=P)
        NQ = NCONV + CH
        N = NQ + 2 * CH
        tr = slice(0, 3 * P)

        with nc.Block() as block:

            @block.sync
            def _(sp):
                with sp.Fori(0, CH) as t:
                    for r, kind in enumerate((2, 1, 0)):
                        load(sp, t * 3 + r, lambda half: w[half, :, :, ds(t * P + kind * DC, P)])
                with sp.Fori(0, 3 * CH) as t:
                    load(sp, t + NCONV, lambda half: w[half, :, :, ds(t * P + 3 * DC, P)])

            @block.gpsimd
            def _(pool):
                pool.memset(up[:, 0:2], 0.0).then_inc(zeroed, 1)
                with pool.Fori(0, N) as n:
                    split_chunk(pool, n)

            @block.tensor
            def _(pe):
                c.start_at_one(pe, *first_counts, e_stored, rows_stored, rows_ready)
                def turn_back(m):
                    pe.wait_ge(e_ready, m + 1 + 2 * CH)
                    for b in range(NB):
                        for j in range(NB):
                            mm = pe.transpose(tp[:, b, j * P:(j + 1) * P], e[:, (b * NB + j) * P:(b * NB + j + 1) * P],
                                              c.ident[:])
                        mm.then_inc(e_turned, 1)

                with pe.Fori(0, NQ) as n:
                    products(pe, n, 0, z, hT_hi, hT_lo)
                    products(pe, n, 1, z, hT_hi, hT_lo)
                products(pe, NQ, 0, z, hT_hi, hT_lo)
                products(pe, NQ, 1, z, hT_hi, hT_lo)
                with pe.Fori(1, 2 * CH) as m:
                    products(pe, m + NQ, 0, z, hT_hi, hT_lo)
                    pe.wait_ge(rows_ready, m)
                    turn_back(m - 1)
                    products(pe, m + NQ, 1, z, hT_hi, hT_lo)
                pe.wait_ge(rows_ready, 2 * CH)
                turn_back(2 * CH - 1)
                pe.wait_ge(rows_ready, 2 * CH + 1)
                for j in range(CH):
                    mm = pe.transpose(tp[0:2 + 2 * STREAMS, j // 4, (j % 4) * P:(j % 4 + 1) * P], tail[:, j, :], c.ident[:])
                mm.then_inc(tail_turned, 1)

            @block.vector
            def _(dve):
                cut = PROMPT - 2 * BLK
                ys = xs[:, PROMPT:TOK].rearrange("p (s r) -> p s r", s=STREAMS)
                es = slice(2, 2 + NEW)
                STEPS = 10
                dve.wait_ge(zeroed, 1)
                with dve.Fori(0, CH) as t:
                    for b in range(NB):
                        dve.wait_ge(z_done[b], t * 3 + 2)
                        dve.tensor_copy(xs[:, b * BLK:(b + 1) * BLK], z[:, b, 0:BLK]).then_inc(z_kept[b], 1)
                    dve.tensor_copy(us[:, :, 0:2], c.taps[:, ds(t, 1), 0:2 * STREAMS].rearrange(
                        "p a (s r) -> p (a s) r", s=STREAMS)).then_inc(step, 1)
                    dve.wait_ge(z_kept[2], t * 3 + 2)
                    for b in range(2):
                        dve.wait_ge(z_done[b], t * 3 + 2 + 1)
                        dve.tensor_tensor(up[:, 2 + b * BLK:2 + (b + 1) * BLK], z[:, b, 0:BLK],
                                          xs[:, b * BLK:(b + 1) * BLK], ALU.mult).then_inc(z_kept[b], 1)
                    dve.wait_ge(z_done[2], t * 3 + 2 + 1)
                    dve.tensor_tensor(up[:, 2 + 2 * BLK:2 + PROMPT], z[:, 2, 0:cut], xs[:, 2 * BLK:PROMPT],
                                      ALU.mult).then_inc(step, 1)
                    dve.tensor_tensor(us[:, :, es], z[:, 2, cut:BLK].rearrange("p (s r) -> p s r", s=STREAMS), ys,
                                      ALU.mult).then_inc(z_kept[2], 1)
                    dve.wait_ge(z_kept[2], t * 3 + 2 + 1)
                    dve.wait_ge(z_kept[1], t * 3 + 2 + 1)
                    dve.wait_ge(step, t * STEPS + 2)
                    dve.tensor_copy(tail[:, ds(t, 1), 0:2].rearrange("p a b -> p (a b)"), up[:, PROMPT:PROMPT + 2]).then_inc(step, 1)
                    dve.tensor_copy(tail[:, ds(t, 1), 2:2 + 2 * STREAMS].rearrange("p a (s r) -> p (a s) r", s=STREAMS),
                                    us[:, :, NEW:NEW + 2]).then_inc(step, 1)
                    def tap(j):
                        return c.taps[:, ds(t, 1), 2 * STREAMS + j:2 * STREAMS + j + 1].rearrange("p a b -> p (a b)")
                    dve.tensor_scalar(xs[:, 0:PROMPT], up[:, 0:PROMPT], tap(0), None, ALU.mult).then_inc(step, 1)
                    dve.tensor_scalar(ys, us[:, :, 0:NEW], tap(0), None, ALU.mult).then_inc(step, 1)
                    for j in (1, 2):
                        dve.wait_ge(step, t * STEPS + 4 + 2 * j)
                        dve.scalar_tensor_tensor(xs[:, 0:PROMPT], up[:, j:j + PROMPT], tap(j), xs[:, 0:PROMPT], ALU.mult,
                                                 ALU.add).then_inc(step, 1)
                        dve.scalar_tensor_tensor(ys, us[:, :, j:j + NEW], tap(j), ys, ALU.mult, ALU.add).then_inc(step, 1)
                    dve.wait_ge(step, t * STEPS + STEPS)
                    dve.wait_ge(e_stored, 16 * t + 1)
                    for b in range(NB):
                        dve.wait_ge(z_done[b], t * 3 + 3 + 1)
                        dve.tensor_tensor(e[:, b * BLK:(b + 1) * BLK], z[:, b, 0:BLK], xs[:, b * BLK:(b + 1) * BLK],
                                          ALU.mult).then_inc(z_kept[b], 1)
                    dve.wait_ge(z_kept[2], t * 3 + 3 + 1)
                    dve.sem_inc(e_ready, 1)
                with dve.Fori(0, CH) as t:
                    dve.wait_ge(e_stored, 16 * (t + CH) + 1)
                    for b in range(NB):
                        dve.wait_ge(z_done[b], t + NCONV + 2)
                        dve.tensor_scalar(e[:, b * BLK:(b + 1) * BLK], z[:, b, 0:BLK], SCALE, None, ALU.mult).then_inc(z_kept[b], 1)
                    dve.wait_ge(z_kept[2], t + NCONV + 2)
                    dve.sem_inc(e_ready, 1)

                def keep_rows(m):
                    dve.wait_ge(rows_stored, 16 * m + 1)
                    for b in range(NB):
                        dve.wait_ge(e_turned, NB * m + b + 1)
                        cp = dve.tensor_copy(rows[:, b * NB:(b + 1) * NB, :],
                                             tp[:, b, tr].rearrange("p (a q) -> p a q", a=NB))
                    cp.then_inc(rows_ready, 1)

                def keep_e(m, stored):
                    dve.wait_ge(e_stored, stored + 1)
                    for b in range(NB):
                        dve.wait_ge(z_done[b], m + NQ + 2)
                        dve.tensor_copy(e[:, b * BLK:(b + 1) * BLK], z[:, b, 0:BLK]).then_inc(z_kept[b], 1)
                    dve.wait_ge(z_kept[2], m + NQ + 2)
                    dve.sem_inc(e_ready, 1)

                keep_e(0, 16 * 2 * CH)
                with dve.Fori(1, CH + 1) as m:
                    keep_rows(m - 1)
                    keep_e(m, (m + 2 * CH) * 16)
                with dve.Fori(CH + 1, 2 * CH) as m:
                    keep_rows(m - 1)
                    keep_e(m, 16 * 3 * CH)
                keep_rows(2 * CH - 1)
                dve.wait_ge(tail_turned, 1)
                dve.tensor_copy(tail_rows[:].rearrange("p (a q) -> p a q", a=2), tp[0:2 + 2 * STREAMS, 0:2, :]).then_inc(tail_kept, 1)

            @block.scalar
            def _(act):
                with act.Fori(0, 2 * CH) as t:
                    act.wait_ge(e_ready, t + 1)
                    act.dma_start(io.chunks[ds(t, 1), :, :].rearrange("a p n -> (a p) n"), e[:]).then_inc(e_stored, 16)

                def store_rows(dram, m, done):
                    act.wait_ge(rows_ready, done + 2)
                    act.dma_start(dram.rearrange("(t p) n -> p t n", p=P)[:, :, ds(m * P, P)], rows[:]).then_inc(rows_stored, 16)

                with act.Fori(0, CH) as m:
                    act.wait_ge(e_ready, m + 2 * CH + 1)
                    act.dma_start(io.chunks[ds(m + 2 * CH, 1), :, :].rearrange("a p n -> (a p) n"), e[:]).then_inc(e_stored, 16)
                    store_rows(io.k_all, m, m)
                with act.Fori(0, CH) as m:
                    store_rows(io.v_all, m, m + CH)
                act.wait_ge(tail_kept, 1)
                act.dma_start(io.conv_all, tail_rows[:]).then_inc(tail_stored, 16)
                act.wait_ge(tail_stored, 16)
                act.wait_ge(rows_stored, 16 * 2 * CH + 1)
                act.wait_ge(e_stored, 16 * 3 * CH + 1)


def head_norm(c, dve, o, square, ssq, rstd, step, n, root_ready):
    dve.wait_ge(root_ready, n + 1)
    dve.reciprocal(rstd[:], ssq[:]).then_inc(step, 1)
    dve.wait_ge(step, 4 * n + 3)
    dve.tensor_tensor(o[:], o[:], rstd[:].unsqueeze(2).to_broadcast([P, HEADS, VD]), ALU.mult).then_inc(step, 1)
    dve.wait_ge(step, 4 * n + 4)


def norm_sums(c, dve, o, square, ssq, step, n):
    dve.tensor_tensor(square[:], o[:], o[:], ALU.mult).then_inc(step, 1)
    dve.wait_ge(step, 4 * n + 1)
    dve.tensor_reduce(ssq[:], square[:], AX.X, ALU.add).then_inc(step, 1)


def phase_attend(c, a_hi, a_lo, o_hi, o_lo):
    nc, io, sem = c.nc, c.io, c.sem
    QT = PROMPT // P
    with ExitStack() as mem:
        def sb(name, shape, dt=F32):
            return mem.enter_context(nc.sbuf_tensor(name, shape, dt))

        q = sb("a_q", [P, 2, PROMPT])
        k = sb("a_k", [P, 2, PROMPT])
        v = sb("a_v", [P, 2, QT, VD])
        pr = sb("a_pr", [P, 2, 2, PROMPT])
        at = sb("a_at", [P, 2, PROMPT])
        o = sb("a_o", [P, 2, QT, VD])
        nb, l, rl = (sb(f"a_{n}", [P, 2, 2]) for n in ("nb", "l", "rl"))
        cf = sb("a_cf", [P, 1])
        mask_q, mask_k = sb("a_mask_q", [P, P]), sb("a_mask_k", [P, P // 2])
        ssq, rstd = sb("a_ssq", [P, QT]), sb("a_rstd", [P, QT])
        a_raw = sb("a_raw", [P, TOK])
        square = a_raw[:, 0:QT * VD].rearrange("p (a b) -> p a b", a=QT)
        s_ps = mem.enter_context(nc.psum_tensor("a_s", [P, 2, PROMPT], F32))
        t_ps = mem.enter_context(nc.psum_tensor("a_t", [P, 2, 512], F32))
        o_ps = mem.enter_context(nc.psum_tensor("a_o_ps", [P, 2, 512], F32))
        head_loaded, head_used = c.sems("a_head_loaded", 2), c.sems("a_head_used", 2)
        scores_done, exp_done, bias_ready = c.sems("a_scores_done", 2), c.sems("a_exp_done", 2), c.sems("a_bias_ready", 2)
        step, mixed, mask_step = sem("a_step"), sem("a_mixed"), sem("a_mask_step")
        turned, t_kept = c.sems("a_turned", 2), c.sems("a_t_kept", 2)
        at_ready, pv_done, o_kept = sem("a_at_ready"), sem("a_pv_done"), sem("a_o_kept")
        sums_ready, root_ready, rstd_ready, scaled, normed = (sem(f"a_{n}") for n in ("sums_ready", "root_ready", "rstd_ready", "scaled", "normed"))
        squared, out_hi, out_done = sem("a_squared"), sem("a_out_hi"), sem("a_out_done")
        raw_loaded, split_hi, split_lo = sem("a_raw_loaded"), sem("a_split_hi"), sem("a_split_lo")
        STEPS = 2

        TURNS = {7: (0, 1), 0: (2,), 1: (3,), 2: (4,), "out": (5, 6), 3: (7,), 4: (8, 9), 5: (10, 11), 6: (12, 13),
                 "last out": (2, 3)}
        OUT_STEP = 3

        def bank_use(h, turn):
            missing = 1 if isinstance(h, int) and h == 0 and turn < TURNS["out"][0] else 2
            return turn % 2, 7 * h + turn // 2 - missing

        def blocks(i, n):
            return range(4 * n, min(4 * n + 4, i + 1))

        def pair(body, eng):
            body(0, True)
            with eng.Fori(1, HEADS // 2) as it:
                body(it, False)

        with nc.Block() as block:

            @block.gpsimd
            def _(pool):
                pool.memset(mask_k[:], 1.0).then_inc(mask_step, 1)
                pool.memset(mask_q[:], 0.0).then_inc(mask_step, 1)
                pool.wait_ge(mask_step, 2)
                for m in range(2):
                    pool.memset(mask_q[m * DH:m * DH + 1, 0:P // 2], MASKED).then_inc(mask_step, 1)
                with pool.Fori(0, HEADS // 2) as it:
                    for s in range(2):
                        h = 2 * it + s
                        pool.wait_ge(o_kept, QT * (h + 1))
                        pool.wait_ge(split_lo, h + 1)
                        pool.tensor_tensor(square, o[:, s], o[:, s], ALU.mult).then_inc(squared, 1)
                        pool.wait_ge(rstd_ready, h + 1)
                        pool.tensor_tensor(o[:, s], o[:, s], rstd[:].unsqueeze(2).to_broadcast([P, QT, VD]), ALU.mult).then_inc(scaled, 1)
                        pool.wait_ge(scaled, h + 1)
                        pool.tensor_tensor(o[:, s], o[:, s], c.hn[:].unsqueeze(1).to_broadcast([P, QT, VD]), ALU.mult).then_inc(normed, 1)
                        pool.dma_start(a_raw[:], io.chunks[ds(h, 1), :, :].rearrange("a p n -> (a p) n")).then_inc(raw_loaded, 16)
                        pool.wait_ge(raw_loaded, 16 * (h + 1))
                        c.hold(pool)
                        hi = a_hi[:, ds(h, 1), :].rearrange("p a b -> p (a b)")
                        pool.tensor_copy(hi, a_raw[:]).then_inc(split_hi, 1)
                        pool.wait_ge(split_hi, h + 1)
                        pool.tensor_tensor(a_lo[:, ds(h, 1), :].rearrange("p a b -> p (a b)"), a_raw[:], hi, ALU.subtract).then_inc(split_lo, 1)

            @block.sync
            def _(sp):
                with sp.Fori(0, HEADS // 2) as it:
                    for s in range(2):
                        h = 2 * it + s
                        sp.wait_ge(head_used[s], it + 1)
                        c.hold(sp)
                        sp.dma_start(q[:, s, :], io.chunks[ds(h + CH, 1), :, 0:PROMPT].rearrange("a p n -> (a p) n")).then_inc(head_loaded[s], 16)
                        sp.dma_start(k[:, s, :], io.chunks[ds(h + 2 * CH, 1), :, 0:PROMPT].rearrange("a p n -> (a p) n")).then_inc(head_loaded[s], 16)
                        sp.dma_start(v[:, s, :, :], io.v_all[0:PROMPT, ds(h * VD, VD)].rearrange("(t p) e -> p t e", p=P)).then_inc(head_loaded[s], 16)

            @block.tensor
            def _(pe):
                c.start_at_one(pe, *head_used, *exp_done, *t_kept, split_lo)

                def scores(s, i, g):
                    w = P * (i + 1)
                    for m in range(2):
                        part = slice(m * DH, (m + 1) * DH)
                        pe.wait_ge(exp_done[m], g + 1)
                        for b in range(0, P * (i + 1), 512):
                            e = min(b + 512, P * (i + 1))
                            mm = pe.matmul(s_ps[:, m, b:e], q[part, s, i * P:(i + 1) * P], k[part, s, b:e], start=True, stop=e < w)
                        mm = pe.matmul(s_ps[:, m, w - P // 2:w], mask_q[part, :], mask_k[part, :], start=False, stop=True)
                        mm.then_inc(scores_done[m], 1)

                def turn(i, h, g):
                    pe.wait_ge(mixed, g + 1)
                    for n, at_turn in enumerate(TURNS[i]):
                        bank, before = bank_use(h, at_turn)
                        pe.wait_ge(t_kept[bank], before + 1)
                        for j in blocks(i, n):
                            mm = pe.transpose(t_ps[:, bank, (j % 4) * P:(j % 4 + 1) * P], pr[:, i % 2, 0, j * P:(j + 1) * P],
                                              c.ident[:])
                        mm.then_inc(turned[bank], 1)

                def weigh(s, i, g):
                    pe.wait_ge(at_ready, g + 1)
                    for j in range(i + 1):
                        mm = pe.matmul(o_ps[:, i % 2, 0:VD], at[:, i % 2, j * P:(j + 1) * P], v[:, s, j, :], start=(j == 0), stop=(j == i))
                    mm.then_inc(pv_done, 1)

                def turn_out(h, s, turns=TURNS["out"]):
                    pe.wait_ge(normed, h)
                    for n, at_turn in enumerate(turns):
                        bank, before = bank_use(h, at_turn)
                        pe.wait_ge(t_kept[bank], before + 1)
                        for j in range(4):
                            mm = pe.transpose(t_ps[:, bank, j * P:(j + 1) * P], o[:, s, 4 * n + j, :], c.ident[:])
                        mm.then_inc(turned[bank], 1)

                def body(it, first):
                    for s in range(2):
                        h = 2 * it + s
                        start = first and s == 0
                        pe.wait_ge(head_loaded[s], 48 * (it + 1))
                        for i in range(QT):
                            g = h * QT + i
                            scores(s, i, g)
                            if not (start and i < 2):
                                weigh(s if i >= 2 else 1 - s, (i - 2) % QT, g - 2)
                            if i == 1 and not start:
                                pe.wait_ge(pv_done, g - 1)
                                pe.sem_inc(head_used[1 - s], 1)
                            if not (start and i == 0):
                                turn((i - 1) % QT, h, g - 1)
                            if i == OUT_STEP and not start:
                                turn_out(h, 1 - s)

                pe.wait_ge(mask_step, 4)
                pair(body, pe)
                n = HEADS * QT
                weigh(1, QT - 2, n - 2)
                turn(QT - 1, HEADS, n - 1)
                weigh(1, QT - 1, n - 1)
                turn_out(HEADS, 1, TURNS["last out"])

            @block.vector
            def _(dve):
                def bias(i, g):
                    for m in range(2):
                        dve.wait_ge(scores_done[m], g + 1)
                        dve.tensor_reduce(nb[:, i % 2, m:m + 1], s_ps[:, m, 0:P * (i + 1)], AX.X, ALU.max,
                                          negate=True).then_inc(bias_ready[m], 1)

                def mix(i, g, kept):
                    w, s = P * (i + 1), i % 2
                    if kept:
                        dve.wait_ge(o_kept, g - 1)
                    for m in range(2):
                        dve.wait_ge(exp_done[m], g + 2)
                    dve.reciprocal(rl[:, s, :], l[:, s, :]).then_inc(step, 1)
                    dve.wait_ge(step, STEPS * g + 1)
                    dve.tensor_scalar(cf[:], rl[:, s, 1:2], l[:, s, 0:1], c.neglam[:], ALU.mult, ALU.mult).then_inc(step, 1)
                    dve.wait_ge(step, STEPS * g + 2)
                    dve.scalar_tensor_tensor(pr[:, s, 0, 0:w], pr[:, s, 1, 0:w], cf[:], pr[:, s, 0, 0:w], ALU.mult, ALU.add).then_inc(mixed, 1)

                def keep_o(i, g, s, turned_out=None):
                    dve.wait_ge(pv_done, g + 1)
                    if turned_out is not None:
                        dve.wait_ge(out_done, turned_out)
                    dve.tensor_scalar(o[:, s, i, :], o_ps[:, i % 2, 0:VD], rl[:, i % 2, 0:1], None, ALU.mult).then_inc(o_kept, 1)

                def sums(h):
                    dve.wait_ge(squared, h)
                    dve.tensor_reduce(ssq[:], square, AX.X, ALU.add).then_inc(sums_ready, 1)

                def inverse(h):
                    dve.wait_ge(root_ready, h)
                    dve.reciprocal(rstd[:], ssq[:]).then_inc(rstd_ready, 1)

                def out_lo(h, turns=TURNS["out"]):
                    for n, at_turn in enumerate(turns):
                        bank, _ = bank_use(0, at_turn)
                        part = slice(n * 512, (n + 1) * 512)
                        dve.wait_ge(out_hi, 2 * h - 1 + n)
                        dve.tensor_tensor(o_lo[:, ds(h - 1, 1), part].rearrange("p a b -> p (a b)"), t_ps[:, bank, :],
                                          o_hi[:, ds(h - 1, 1), part].rearrange("p a b -> p (a b)"), ALU.subtract).then_inc(t_kept[bank], 1)

                def body(it, first):
                    for s in range(2):
                        h = 2 * it + s
                        start = first and s == 0
                        for i in range(QT):
                            g = h * QT + i
                            bias(i, g)
                            if not (start and i < 2):
                                keep_o((i - 2) % QT, g - 2, s if i >= 2 else 1 - s, h - 1 if i == 2 and not first else None)
                            if i == OUT_STEP and not start:
                                inverse(h)
                            mix(i, g, not (start and i < 2))
                            if not start:
                                if i == 2:
                                    sums(h)
                                if i == OUT_STEP + 1:
                                    out_lo(h)

                pair(body, dve)
                n = HEADS * QT
                keep_o(QT - 2, n - 2, 1)
                keep_o(QT - 1, n - 1, 1)
                sums(HEADS)
                inverse(HEADS)
                out_lo(HEADS, TURNS["last out"])

            @block.scalar
            def _(act):
                def exponentials(i, g):
                    w, s = P * (i + 1), i % 2
                    for m in range(2):
                        act.wait_ge(bias_ready[m], g + 1)
                        act.activation(pr[:, s, m, 0:w], s_ps[:, m, 0:w], ACT.Exp, bias=nb[:, s, m:m + 1],
                                       accum_out=l[:, s, m:m + 1]).then_inc(exp_done[m], 1)

                def keep_at(i, h):
                    for n, at_turn in enumerate(TURNS[i]):
                        bank, before = bank_use(h, at_turn)
                        act.wait_ge(turned[bank], before + 1)
                        w = P * len(blocks(i, n))
                        act.activation(at[:, i % 2, n * 512:n * 512 + w], t_ps[:, bank, 0:w], ACT.Copy).then_inc(t_kept[bank], 1)
                    act.wait_ge(t_kept[bank], before + 2)
                    act.sem_inc(at_ready, 1)

                def root(h):
                    act.wait_ge(sums_ready, h)
                    act.activation(ssq[:], ssq[:], ACT.Sqrt, bias=c.eps[:], scale=1.0 / VD).then_inc(root_ready, 1)

                def keep_out(h, turns=TURNS["out"]):
                    for n, at_turn in enumerate(turns):
                        bank, before = bank_use(h, at_turn)
                        act.wait_ge(turned[bank], before + 1)
                        act.activation(o_hi[:, ds(h - 1, 1), n * 512:(n + 1) * 512].rearrange("p a b -> p (a b)"),
                                       t_ps[:, bank, :], ACT.Copy).then_inc(out_hi, 1)
                    act.wait_ge(out_hi, 2 * h)
                    act.sem_inc(out_done, 1)

                def body(it, first):
                    for s in range(2):
                        h = 2 * it + s
                        start = first and s == 0
                        for i in range(QT):
                            g = h * QT + i
                            exponentials(i, g)
                            if not (start and i == 0):
                                keep_at((i - 1) % QT, h)
                            if not start:
                                if i == 2:
                                    root(h)
                                if i == OUT_STEP:
                                    keep_out(h)

                pair(body, act)
                keep_at(QT - 1, HEADS)
                root(HEADS)
                keep_out(HEADS, TURNS["last out"])


def phase_decode(c, o_hi, o_lo):
    nc, io, sem = c.nc, c.io, c.sem
    HG = 4
    KEYS = PAST + NEW
    PT = PAST // P
    with ExitStack() as mem:
        def sb(name, shape, dt=F32):
            return mem.enter_context(nc.sbuf_tensor(name, shape, dt))

        k = sb("d_k", [P, PT, DC])
        v = sb("d_v", [P, PT, DC])
        vn = sb("d_vn", [NEW, DC])
        kT = sb("d_kT", [P, HEADS, KEYS])
        qs = sb("d_q", [P, HEADS, P])
        qx = sb("d_qx", [P, HG, P])
        pr = sb("d_pr", [P, KEYS])
        mixer, mixl = sb("d_mixer", [P, HG * NEW]), sb("d_mixl", [P, HG * NEW])
        at = sb("d_at", [P, PT + 1, HG * NEW])
        orow = sb("d_orow", [NEW, DC])
        nb, l, rl = (sb(f"d_{n}", [P, 1]) for n in ("nb", "l", "rl"))
        ssq, rstd = sb("d_ssq", [P, HEADS]), sb("d_rstd", [P, HEADS])
        o = k[:, 0, :].rearrange("p (a b) -> p a b", a=HEADS)
        square = k[:, 1, :].rearrange("p (a b) -> p a b", a=HEADS)
        t_ps = mem.enter_context(nc.psum_tensor("d_t", [P, 2, 512], F32))
        s_ps = mem.enter_context(nc.psum_tensor("d_s", [P, 1024], F32))
        at_ps = mem.enter_context(nc.psum_tensor("d_at_ps", [P, 512], F32))
        o_ps = mem.enter_context(nc.psum_tensor("d_o_ps", [P, 512], F32))
        k_loaded, v_loaded, kn_loaded, q_loaded = sem("d_k_loaded"), sem("d_v_loaded"), sem("d_kn_loaded"), sem("d_q_loaded")
        k_turned, kT_ready = sem("d_k_turned"), c.sems("d_kT_ready", 2)
        qx_zeroed, qx_ready, mixer_step = sem("d_qx_zeroed"), sem("d_qx_ready"), sem("d_mixer_step")
        scores_done, step, exp_done, mixl_ready = sem("d_scores_done"), sem("d_step"), sem("d_exp_done"), sem("d_mixl_ready")
        at_done, at_kept, o_done, o_kept, o_stored = sem("d_at_done"), sem("d_at_kept"), sem("d_o_done"), sem("d_o_kept"), sem("d_o_stored")
        bias_ready = sem("d_bias_ready")
        o_loaded, nstep, root_ready, normed = sem("d_o_loaded"), sem("d_nstep"), sem("d_root_ready"), sem("d_normed")
        o_turned, hi_kept, lo_kept = sem("d_o_turned"), sem("d_hi_kept"), sem("d_lo_kept")
        G = HEADS // HG

        with nc.Block() as block:

            @block.sync
            def _(sp):
                sp.dma_start(qs[:], io.chunks[CH:2 * CH, :, PROMPT:TOK].rearrange("h p n -> p h n")).then_inc(q_loaded, 16)
                with sp.Fori(0, STREAMS) as b:
                    sp.wait_ge(k_turned, HEADS * b + 1)
                    sp.dma_start(k[:], io.cache_k[ds(b, 1), :, :].rearrange("a (t p) n -> p (a t) n", p=P)).then_inc(k_loaded, 16)
                    sp.wait_ge(scores_done, G * b + 1)
                    sp.dma_start(kT[:, :, PAST:KEYS], io.chunks[2 * CH:3 * CH, :, ds(b * NEW + PROMPT, NEW)].rearrange(
                        "h p n -> p h n")).then_inc(kn_loaded, 16)
                    sp.wait_ge(o_done, G * b + 1)
                    sp.dma_start(v[:], io.cache_v[ds(b, 1), :, :].rearrange("a (t p) n -> p (a t) n", p=P)).then_inc(v_loaded, 16)
                    sp.dma_start(vn[:], io.v_all[ds(b * NEW + PROMPT, NEW), :]).then_inc(v_loaded, 16)
                sp.wait_ge(o_stored, 16 * STREAMS + 1)
                sp.dma_start(k[:, 0, :], io.o_new).then_inc(o_loaded, 16)

            @block.gpsimd
            def _(pool):
                pool.memset(qx[:], 0.0).then_inc(qx_zeroed, 1)

            @block.tensor
            def _(pe):
                c.start_at_one(pe, k_turned, scores_done, o_done, *kT_ready, exp_done, at_kept, o_kept, at_done, o_stored)
                with pe.Fori(0, STREAMS) as b:
                    pe.wait_ge(k_loaded, 16 * (b + 1))
                    for h in range(HEADS):
                        pe.wait_ge(kT_ready[h % 2], b * (HEADS // 2) + h // 2 + 1)
                        for t in range(PT):
                            mm = pe.transpose(t_ps[:, h % 2, t * P:(t + 1) * P], k[:, t, h * VD:(h + 1) * VD], c.ident[:])
                        mm.then_inc(k_turned, 1)
                    for hg in range(G):
                        n = b * G + hg
                        pe.wait_ge(qx_ready, n + 1)
                        pe.wait_ge(exp_done, n + 1)
                        if hg == 0:
                            pe.wait_ge(kT_ready[0], b * (HEADS // 2) + HEADS // 2 + 1)
                            pe.wait_ge(kT_ready[1], b * (HEADS // 2) + HEADS // 2 + 1)
                            pe.wait_ge(kn_loaded, 16 * (b + 1))
                        for j in range(HG):
                            pe.matmul(s_ps[:, 0:PAST], qx[:, j, :], kT[:, hg * HG + j, 0:PAST], start=(j == 0), stop=(j == HG - 1))
                        for j in range(HG):
                            mm = pe.matmul(s_ps[:, PAST:KEYS], qx[:, j, :], kT[:, hg * HG + j, PAST:KEYS], start=(j == 0), stop=(j == HG - 1))
                        mm.then_inc(scores_done, 1)
                        pe.wait_ge(mixl_ready, n + 1)
                        pe.wait_ge(at_kept, n + 1)
                        for t in range(PT + 1):
                            w = min(P, KEYS - t * P)
                            mm = pe.matmul(at_ps[0:w, t * HG * NEW:(t + 1) * HG * NEW], pr[:, t * P:t * P + w], mixl[:],
                                           start=True, stop=True)
                        mm.then_inc(at_done, 1)
                        pe.wait_ge(at_kept, n + 2)
                        pe.wait_ge(o_kept, n + 1)
                        if hg == 0:
                            pe.wait_ge(v_loaded, 32 * (b + 1))
                        for j in range(HG):
                            cols = slice((hg * HG + j) * VD, (hg * HG + j + 1) * VD)
                            for t in range(PT + 1):
                                w = min(P, KEYS - t * P)
                                rhs = v[:, t, cols] if t < PT else vn[:, cols]
                                mm = pe.matmul(o_ps[0:NEW, j * VD:(j + 1) * VD], at[0:w, t, j * NEW:(j + 1) * NEW], rhs,
                                               start=(t == 0), stop=(t == PT))
                        mm.then_inc(o_done, 1)
                pe.wait_ge(normed, 1)
                for h in range(HEADS):
                    mm = pe.transpose(s_ps[:, h * P:(h + 1) * P], o[:, h, :], c.ident[:])
                mm.then_inc(o_turned, 1)

            @block.vector
            def _(dve):
                idv = c.ident[:].rearrange("p (h m q) -> p h m q", h=HG, m=2)
                mv = mixer[:].rearrange("p (h q) -> p h q", h=HG)
                dve.tensor_scalar(mv, idv[:, :, 1, :], c.neglam[:], None, ALU.mult).then_inc(mixer_step, 1)
                dve.wait_ge(mixer_step, 1)
                dve.tensor_tensor(mv, mv, idv[:, :, 0, :], ALU.add).then_inc(mixer_step, 1)
                dve.wait_ge(mixer_step, 2)
                dve.wait_ge(qx_zeroed, 1)
                dve.wait_ge(q_loaded, 16)
                qv = qx[:].rearrange("p h (g m q) -> p h g m q", g=HG, m=2)

                def spread_queries(b, hg, n):
                    dve.wait_ge(scores_done, n + 1)
                    for j in range(HG):
                        for m in range(2):
                            part = slice(m * DH, (m + 1) * DH)
                            cp = dve.tensor_copy(qx[part, j, (2 * j + m) * NEW:(2 * j + m + 1) * NEW],
                                                 qs[part, hg * HG + j, ds(b * NEW, NEW)])
                    cp.then_inc(qx_ready, 1)

                with dve.Fori(0, STREAMS) as b:
                    spread_queries(b, 0, b * G)
                    for h in range(1, HEADS, 2):
                        dve.wait_ge(k_turned, b * HEADS + h + 2)
                        if h == 1:
                            dve.wait_ge(scores_done, b * G + 1)
                        dve.tensor_copy(kT[:, h, 0:PAST], t_ps[:, 1, :]).then_inc(kT_ready[1], 1)
                    for hg in range(G):
                        n = b * G + hg
                        dve.wait_ge(scores_done, n + 2)
                        dve.tensor_reduce(nb[:], s_ps[:, 0:KEYS], AX.X, ALU.max, negate=True).then_inc(bias_ready, 1)
                        if hg == 0:
                            spread_queries(b, 1, n + 1)
                        dve.wait_ge(exp_done, n + 2)
                        dve.reciprocal(rl[:], l[:]).then_inc(step, 1)
                        dve.wait_ge(step, n + 1)
                        dve.tensor_scalar(mixl[:], mixer[:], rl[:], None, ALU.mult).then_inc(mixl_ready, 1)
                        dve.wait_ge(at_done, n + 2)
                        w = PT * HG * NEW
                        dve.tensor_copy(at[:, 0:PT, :].rearrange("p a b -> p (a b)"), at_ps[:, 0:w])
                        dve.tensor_copy(at[0:NEW, PT, :], at_ps[0:NEW, w:w + HG * NEW]).then_inc(at_kept, 1)
                dve.wait_ge(o_loaded, 16)
                norm_sums(c, dve, o, square, ssq, nstep, 0)
                head_norm(c, dve, o, square, ssq, rstd, nstep, 0, root_ready)
                dve.tensor_tensor(o[:], o[:], c.hn[:].unsqueeze(1).to_broadcast([P, HEADS, VD]), ALU.mult).then_inc(normed, 1)
                dve.wait_ge(hi_kept, 1)
                dve.tensor_tensor(o_lo[:, :, PROMPT:TOK], s_ps[:].rearrange("p (h n) -> p h n", h=HEADS),
                                  o_hi[:, :, PROMPT:TOK], ALU.subtract).then_inc(lo_kept, 1)
                dve.wait_ge(lo_kept, 1)

            @block.scalar
            def _(act):
                with act.Fori(0, STREAMS) as b:
                    for h in range(0, HEADS, 2):
                        act.wait_ge(k_turned, b * HEADS + h + 2)
                        if h == 0:
                            act.wait_ge(scores_done, b * G + 1)
                        act.activation(kT[:, h, 0:PAST], t_ps[:, 0, :], ACT.Copy).then_inc(kT_ready[0], 1)
                    for hg in range(G):
                        n = b * G + hg
                        act.wait_ge(bias_ready, n + 1)
                        act.wait_ge(at_done, n + 1)
                        act.activation(pr[:], s_ps[:, 0:KEYS], ACT.Exp, bias=nb[:], accum_out=l[:]).then_inc(exp_done, 1)
                        act.wait_ge(o_done, n + 2)
                        if hg == 0:
                            act.wait_ge(o_stored, 16 * b + 1)
                        act.activation(orow[:, hg * 512:(hg + 1) * 512], o_ps[0:NEW, :], ACT.Copy).then_inc(o_kept, 1)
                    act.wait_ge(o_kept, G * (b + 1) + 1)
                    act.dma_start(io.o_new[ds(b * NEW, NEW), :], orow[:]).then_inc(o_stored, 16)
                act.wait_ge(nstep, 2)
                act.activation(ssq[:], ssq[:], ACT.Sqrt, bias=c.eps[:], scale=1.0 / VD).then_inc(root_ready, 1)
                act.wait_ge(o_turned, 1)
                act.activation(o_hi[:, :, PROMPT:TOK], s_ps[:].rearrange("p (h n) -> p h n", h=HEADS), ACT.Copy).then_inc(hi_kept, 1)


def phase_mix_out(c, a_hi, a_lo, o_hi, o_lo):
    nc, io, sem = c.nc, c.io, c.sem
    with ExitStack() as mem:
        def sb(name, shape, dt=F32):
            return mem.enter_context(nc.sbuf_tensor(name, shape, dt))

        w_raw = sb("m_w_raw", [P, KT, P])
        w_hi = sb("m_w_hi", [P, KT, P], F32R)
        w_lo = sb("m_w_lo", [P, KT, P], F32R)
        e = sb("m_e", [P, TOK])
        x = sb("m_x", [P, NT, P])
        rows = sb("m_rows", [P, NT, P])
        z = mem.enter_context(nc.psum_tensor("m_z", [P, NB, 512], F32))
        tp = mem.enter_context(nc.psum_tensor("m_tp", [P, NB, 512], F32))
        load, split_chunk, products, z_done, z_kept, first_counts = weight_chunks(c, "m", w_raw, w_hi, w_lo)
        e_ready, e_turned = sem("m_e_ready"), sem("m_e_turned")
        x_loaded, rows_ready, rows_stored = sem("m_x_loaded"), sem("m_rows_ready"), sem("m_rows_stored")
        w = io.w_out.rearrange("(h k p) n -> h p k n", h=2, p=P)
        x_cols = io.x.rearrange("(t p) n -> p t n", p=P)
        x1_cols = io.x1.rearrange("(t p) n -> p t n", p=P)

        with nc.Block() as block:

            @block.sync
            def _(sp):
                with sp.Fori(0, KT) as n:
                    load(sp, n, lambda half: w[half, :, :, ds(n * P, P)])

            @block.gpsimd
            def _(pool):
                with pool.Fori(0, KT) as n:
                    split_chunk(pool, n)

            @block.tensor
            def _(pe):
                c.start_at_one(pe, *first_counts, rows_stored, rows_ready)
                def turn_back(m):
                    pe.wait_ge(e_ready, m + 1)
                    pe.wait_ge(rows_ready, m + 1)
                    for b in range(NB):
                        for j in range(NB):
                            mm = pe.transpose(tp[:, b, j * P:(j + 1) * P], e[:, (b * NB + j) * P:(b * NB + j + 1) * P],
                                              c.ident[:])
                        mm.then_inc(e_turned, 1)

                products(pe, 0, 0, z, a_hi, a_lo)
                products(pe, 0, 1, z, o_hi, o_lo)
                with pe.Fori(1, KT) as n:
                    products(pe, n, 0, z, a_hi, a_lo)
                    turn_back(n - 1)
                    products(pe, n, 1, z, o_hi, o_lo)
                turn_back(KT - 1)

            @block.vector
            def _(dve):
                def keep_e(n):
                    for b in range(NB):
                        dve.wait_ge(z_done[b], n + 2)
                        dve.tensor_copy(e[:, b * BLK:(b + 1) * BLK], z[:, b, 0:BLK]).then_inc(z_kept[b], 1)
                    dve.wait_ge(z_kept[2], n + 2)
                    dve.sem_inc(e_ready, 1)

                def add_rows(m):
                    dve.wait_ge(x_loaded, 16 * (m + 1))
                    dve.wait_ge(rows_stored, 16 * m + 1)
                    for b in range(NB):
                        dve.wait_ge(e_turned, NB * m + b + 1)
                        add = dve.tensor_tensor(rows[:, b * NB:(b + 1) * NB, :],
                                                tp[:, b, 0:NB * P].rearrange("p (a q) -> p a q", a=NB),
                                                x[:, b * NB:(b + 1) * NB, :], ALU.add)
                    add.then_inc(rows_ready, 1)

                keep_e(0)
                with dve.Fori(1, KT) as n:
                    add_rows(n - 1)
                    keep_e(n)
                add_rows(KT - 1)

            @block.scalar
            def _(act):
                with act.Fori(0, KT) as n:
                    act.wait_ge(rows_ready, n + 1)
                    act.dma_start(x[:], x_cols[:, :, ds(n * P, P)]).then_inc(x_loaded, 16)
                    act.wait_ge(rows_ready, n + 2)
                    act.dma_start(x1_cols[:, :, ds(n * P, P)], rows[:]).then_inc(rows_stored, 16)
                act.wait_ge(rows_stored, 16 * KT + 1)


def phase_route(c):
    nc, io, sem = c.nc, c.io, c.sem
    SL = 3
    NP = TOPK * NT
    with ExitStack() as mem:
        def sb(name, shape, dt=F32):
            return mem.enter_context(nc.sbuf_tensor(name, shape, dt))

        x = sb("r_x", [P, SL, D])
        g = sb("r_g", [P, D])
        xT = sb("r_xT", [P, KT, P])
        wr = sb("r_w", [P, KT, NR])
        br = sb("r_b", [P, NR])
        ssq, rstd = sb("r_ssq", [P, SL]), sb("r_rstd", [P, SL])
        junk = sb("r_junk", [P, D])
        lg = sb("r_lg", [P, NT, NR])
        tri, ones = sb("r_tri", [P, P]), sb("r_ones", [P, P])
        ints = sb("r_ints", [P, 64], I32)
        nums = sb("r_nums", [P, 64])
        thr_i, thr = sb("r_thr_i", [P, NT], I32), sb("r_thr", [P, NT])
        gm, gs, m1, m2, e1, e2, ex, wsum = (sb(f"r_{n}", [P, NT]) for n in ("gm", "gs", "m1", "m2", "e1", "e2", "ex", "wsum"))
        d4, x4, oh4 = (sb(f"r_{n}", [P, NT, GROUPS]) for n in ("d4", "x4", "oh4"))
        le, eq, oh1, oh2, both, carry, place = (sb(f"r_{n}", [P, NT, EXPERTS]) for n in ("le", "eq", "oh1", "oh2", "both", "carry", "place"))
        count, tiles, end, start = (sb(f"r_{n}", [P, EXPERTS]) for n in ("count", "tiles", "end", "start"))
        over = sb("r_over", [P, EXPERTS, NT])
        pos_f, pos = sb("r_pos_f", [P, NP]), sb("r_pos", [P, NP], U32)
        rows = sb("r_rows", [P, NP, 4], I32)
        empty = sb("r_empty", [P, MAXT + 1, 4], I32)
        done_by = sb("r_done_by", [1, MAXT + 1, EXPERTS])
        tile_f = sb("r_tile_f", [1, MAXT + 1])
        tp = mem.enter_context(nc.psum_tensor("r_tp", [P, 4, 512], F32))
        lg_ps = mem.enter_context(nc.psum_tensor("r_lg_ps", [P, 512], F32))
        cum_ps = mem.enter_context(nc.psum_tensor("r_cum", [P, 2, 512], F32))
        x_loaded, x_turned, h_stored = c.sems("r_x_loaded", SL), c.sems("r_x_turned", SL), c.sems("r_h_stored", SL)
        params, squared, root_done, rstd_done = sem("r_params"), sem("r_squared"), sem("r_root_done"), sem("r_rstd_done")
        h_ready, turned, kept_a, kept_v = sem("r_h_ready"), sem("r_turned"), sem("r_kept_a"), sem("r_kept_v")
        logits_done, logits_kept = sem("r_logits_done"), sem("r_logits_kept")
        consts, step, gaps_ready, exps_done = sem("r_consts"), sem("r_step"), sem("r_gaps_ready"), sem("r_exps_done")
        chosen, summed = sem("r_chosen"), sem("r_summed")
        emptied, slots_ready, slots_stored = sem("r_emptied"), sem("r_slots_ready"), sem("r_slots_stored")

        with nc.Block() as block:

            @block.sync
            def _(sp):
                sp.dma_start(g[:], io.norm_ffn.to_broadcast([P, D])).then_inc(params, 16)
                sp.dma_start(wr[:], io.w_router.rearrange("(k p) n -> p k n", p=P)).then_inc(params, 16)
                sp.dma_start(br[:], io.b_router.to_broadcast([P, NR])).then_inc(params, 16)
                with sp.Fori(0, NT // SL) as i:
                    for s in range(SL):
                        sp.wait_ge(x_turned[s], i + 1)
                        c.hold(sp)
                        sp.wait_ge(h_stored[s], 16 * i + 1)
                        c.hold(sp)
                        sp.dma_start(x[:, s, :], io.x1[ds((i * SL + s) * P, P), :]).then_inc(x_loaded[s], 16)

            @block.gpsimd
            def _(pool):
                pool.memset(tri[:], 1.0).then_inc(consts, 1)
                pool.memset(ones[:], 1.0).then_inc(consts, 1)
                pool.memset(empty[:], 0).then_inc(consts, 1)
                pool.memset(rows[:], 0).then_inc(consts, 1)
                pool.iota(ints[:], pattern=[[1, 64]], base=0, channel_multiplier=0).then_inc(consts, 1)
                pool.iota(thr_i[:], pattern=[[P, NT]], base=0, channel_multiplier=0).then_inc(consts, 1)
                pool.wait_ge(consts, 6)
                pool.affine_select(out=tri[:], in_=tri[:], compare_op=ALU.is_gt, fill=0.0, base=0, pattern=[[1, P]],
                                   channel_multiplier=-1).then_inc(consts, 1)
                pool.memset(empty[:, :, 1:2], NO_ROW).then_inc(consts, 1)
                for k in range(TOPK):
                    pool.iota(rows[:, k * NT:(k + 1) * NT, 0], pattern=[[P, NT]], base=0, channel_multiplier=1).then_inc(consts, 1)
                    pool.iota(rows[:, k * NT:(k + 1) * NT, 1], pattern=[[P, NT]], base=k * TOK, channel_multiplier=1).then_inc(consts, 1)
                pool.wait_ge(consts, 12)
                pool.dma_start(io.slots.rearrange("(p t) f -> p (t f)", p=P), empty[:].rearrange("p t f -> p (t f)")).then_inc(emptied, 16)
                pool.wait_ge(emptied, 16)
                pool.wait_ge(slots_ready, 1)
                for n in range(NP):
                    pool.indirect_dma_start(out=io.slots, out_offset=bass.IndirectOffsetOnAxis(ap=pos[:, n:n + 1], axis=0),
                                            in_=rows[:, n, :], in_offset=None).then_inc(slots_stored, 16)
                pool.wait_ge(slots_stored, 16 * NP)

            @block.scalar
            def _(act):
                def root(s, t):
                    act.activation(junk[:], x[:, s, :], ACT.Square, accum_out=ssq[:, s:s + 1]).then_inc(squared, 1)
                    act.wait_ge(squared, t + 1)
                    act.activation(ssq[:, s:s + 1], ssq[:, s:s + 1], ACT.Sqrt, bias=c.eps[:], scale=1.0 / D).then_inc(root_done, 1)

                with act.Fori(0, NT // SL) as i:
                    for s in range(SL):
                        t = i * SL + s
                        act.wait_ge(x_loaded[s], 16 * (i + 1))
                        act.wait_ge(rstd_done, t + 1)
                        root(s, t)
                        act.wait_ge(h_ready, t + 1)
                        act.dma_start(io.h2[ds(t * P, P), :], x[:, s, :]).then_inc(h_stored[s], 16)
                        for q in (0, 2):
                            act.wait_ge(turned, 4 * t + q + 1)
                            act.activation(xT[:, 4 * q:4 * q + 4, :], tp[:, q, :].rearrange("p (a b) -> p a b", a=4),
                                           ACT.Copy).then_inc(kept_a, 1)
                act.wait_ge(gaps_ready, 1)
                act.activation(x4[:], d4[:], ACT.Exp).then_inc(exps_done, 1)
                act.wait_ge(gaps_ready, 2)
                act.activation(ex[:], wsum[:], ACT.Exp).then_inc(exps_done, 1)
                for s in range(SL):
                    act.wait_ge(h_stored[s], 16 * (NT // SL) + 1)

            @block.tensor
            def _(pe):
                c.start_at_one(pe, *x_turned, *h_stored, rstd_done, logits_kept)
                pe.wait_ge(params, 48)
                with pe.Fori(0, NT // SL) as i:
                    for s in range(SL):
                        t = i * SL + s
                        pe.wait_ge(h_ready, t + 1)
                        for q in range(4):
                            for j in range(4):
                                k = 4 * q + j
                                mm = pe.transpose(tp[:, q, j * P:(j + 1) * P], x[:, s, k * P:(k + 1) * P], c.ident[:])
                            mm.then_inc(turned, 1)
                        pe.wait_ge(turned, 4 * t + 4)
                        pe.sem_inc(x_turned[s], 1)
                        pe.wait_ge(kept_a, 2 * t + 2)
                        pe.wait_ge(kept_v, 2 * t + 2)
                        pe.wait_ge(logits_kept, t + 1)
                        for k in range(KT):
                            mm = pe.matmul(lg_ps[:, 0:NR], xT[:, k, :], wr[:, k, :], start=(k == 0), stop=(k == KT - 1))
                        mm.then_inc(logits_done, 1)
                pe.wait_ge(chosen, 1)
                pe.wait_ge(consts, 7)
                n = NT * EXPERTS
                pe.matmul(cum_ps[:, 0, 0:n], tri[:], both[:].rearrange("p t e -> p (t e)"), start=True, stop=True)
                pe.matmul(cum_ps[:, 1, 0:n], ones[:], both[:].rearrange("p t e -> p (t e)"), start=True, stop=True).then_inc(summed, 1)

            @block.vector
            def _(dve):
                dve.wait_ge(params, 48)
                with dve.Fori(0, NT // SL) as i:
                    for s in range(SL):
                        t = i * SL + s
                        dve.wait_ge(root_done, t + 1)
                        dve.reciprocal(rstd[:, s:s + 1], ssq[:, s:s + 1]).then_inc(rstd_done, 1)
                        dve.wait_ge(rstd_done, t + 2)
                        dve.scalar_tensor_tensor(x[:, s, :], x[:, s, :], rstd[:, s:s + 1], g[:], ALU.mult, ALU.mult).then_inc(h_ready, 1)
                        for q in (1, 3):
                            dve.wait_ge(turned, 4 * t + q + 1)
                            dve.tensor_copy(xT[:, 4 * q:4 * q + 4, :], tp[:, q, :].rearrange("p (a b) -> p a b", a=4)).then_inc(kept_v, 1)
                        dve.wait_ge(logits_done, t + 1)
                        dve.tensor_tensor(lg[:, ds(t, 1), :].rearrange("p a b -> p (a b)"), lg_ps[:, 0:NR], br[:], ALU.add).then_inc(logits_kept, 1)

                steps = [0]

                def then(ins):
                    steps[0] += 1
                    ins.then_inc(step, 1)
                    dve.wait_ge(step, steps[0])

                def tt(out, a, b, op):
                    then(dve.tensor_tensor(out, a, b, op))

                def over_last(v, n):
                    return v.unsqueeze(2).to_broadcast([P, NT, n])

                def over_tiles(v, n):
                    return v.unsqueeze(1).to_broadcast([P, NT, n])

                dve.wait_ge(logits_kept, NT + 1)
                dve.wait_ge(consts, 12)
                then(dve.tensor_copy(nums[:], ints[:]))
                then(dve.tensor_copy(thr[:], thr_i[:]))
                e_no = nums[:, 0:EXPERTS]

                def first_best(best, index, onehot, scores, n):
                    then(dve.tensor_reduce(best, scores, AX.X, ALU.max))
                    tt(onehot, scores, over_last(best, n), ALU.is_equal)
                    then(dve.tensor_scalar(onehot, onehot, -64.0, 64.0, ALU.mult, ALU.add))
                    tt(onehot, onehot, over_tiles(e_no[:, 0:n], n), ALU.add)
                    then(dve.tensor_reduce(index, onehot, AX.X, ALU.min))
                    tt(onehot, over_tiles(e_no[:, 0:n], n), over_last(index, n), ALU.is_equal)

                first_best(gm[:], e1[:], oh4[:], lg[:, :, 0:GROUPS], GROUPS)
                dve.tensor_tensor(d4[:], lg[:, :, 0:GROUPS], over_last(gm[:], GROUPS), ALU.subtract).then_inc(gaps_ready, 1)
                then(dve.tensor_scalar(oh4[:], oh4[:], -1.0, BIG, ALU.add, ALU.mult))
                tt(le[:].rearrange("p t (g e) -> p t g e", g=GROUPS), lg[:, :, GROUPS:NR].rearrange("p t (g e) -> p t g e", g=GROUPS),
                   oh4[:].unsqueeze(3).to_broadcast([P, NT, GROUPS, PER]), ALU.add)
                first_best(m1[:], e1[:], oh1[:], le[:], EXPERTS)
                then(dve.scalar_tensor_tensor(le[:], oh1[:], -2 * BIG, le[:], ALU.mult, ALU.add))
                first_best(m2[:], e2[:], oh2[:], le[:], EXPERTS)
                dve.tensor_tensor(wsum[:], m2[:], m1[:], ALU.subtract).then_inc(gaps_ready, 1)
                dve.tensor_tensor(both[:], oh1[:], oh2[:], ALU.add).then_inc(chosen, 1)
                dve.wait_ge(exps_done, 2)
                then(dve.tensor_reduce(gs[:], x4[:], AX.X, ALU.add))
                then(dve.tensor_scalar(wsum[:], ex[:], 1.0, None, ALU.add))
                tt(gs[:], gs[:], wsum[:], ALU.mult)
                wv = rows[:].bitcast(F32)
                then(dve.reciprocal(gs[:], gs[:]))
                then(dve.tensor_copy(wv[:, 0:NT, 2], gs[:]))
                tt(wv[:, NT:NP, 2], gs[:], ex[:], ALU.mult)
                dve.wait_ge(summed, 1)
                before = cum_ps[:, 0, 0:NT * EXPERTS].rearrange("p (t e) -> p t e", t=NT)
                total = cum_ps[:, 1, 0:NT * EXPERTS].rearrange("p (t e) -> p t e", t=NT)
                then(dve.memset(carry[:, 0, :], 0.0))
                for t in range(1, NT):
                    tt(carry[:, t, :], carry[:, t - 1, :], total[:, t - 1, :], ALU.add)
                tt(count[:], carry[:, NT - 1, :], total[:, NT - 1, :], ALU.add)
                tt(over[:], count[:].unsqueeze(2).to_broadcast([P, EXPERTS, NT]), thr[:].unsqueeze(1).to_broadcast([P, EXPERTS, NT]), ALU.is_gt)
                then(dve.tensor_reduce(tiles[:], over[:], AX.X, ALU.add))
                then(dve.tensor_tensor_scan(end[:], ones[:, 0:EXPERTS], tiles[:], 0.0, ALU.mult, ALU.add))
                tt(start[:], end[:], tiles[:], ALU.subtract)
                then(dve.tensor_scalar(start[:], start[:], float(P), None, ALU.mult))
                tt(place[:], carry[:], before, ALU.add)
                tt(place[:], place[:], over_tiles(start[:], EXPERTS), ALU.add)
                tt(eq[:], place[:], oh1[:], ALU.mult)
                then(dve.tensor_reduce(pos_f[:, 0:NT], eq[:], AX.X, ALU.add))
                tt(eq[:], place[:], oh2[:], ALU.mult)
                then(dve.tensor_reduce(pos_f[:, NT:NP], eq[:], AX.X, ALU.add))
                dve.tensor_copy(pos[:], pos_f[:]).then_inc(slots_ready, 1)
                ends = end[0:1, :].unsqueeze(1).to_broadcast([1, MAXT + 1, EXPERTS])
                tt(done_by[:], ends, nums[0:1, 0:MAXT + 1].unsqueeze(2).to_broadcast([1, MAXT + 1, EXPERTS]), ALU.is_le)
                then(dve.tensor_reduce(tile_f[:], done_by[:], AX.X, ALU.add))
                then(dve.tensor_scalar(c.tile_expert[:], tile_f[:], EXPERTS - 1.0, None, ALU.min))
                then(dve.tensor_copy(c.tile_count[:], end[0:1, EXPERTS - 1:EXPERTS]))


def phase_experts(c):
    nc, io, sem = c.nc, c.io, c.sem
    UIN, UOUT = 8, 4
    UN = UIN + UOUT
    RAW, SPL = 6, 4
    AHEAD = 4
    with ExitStack() as mem:
        def sb(name, shape, dt=F32):
            return mem.enter_context(nc.sbuf_tensor(name, shape, dt))

        raw = sb("e_raw", [P, RAW, D])
        w_hi = sb("e_w_hi", [P, SPL, D], F32R)
        w_lo = sb("e_w_lo", [P, SPL, D], F32R)
        x = sb("e_x", [P, D])
        xT_hi, xT_lo = sb("e_xT_hi", [P, KT, P], F32R), sb("e_xT_lo", [P, KT, P], F32R)
        sg, act_rows = sb("e_sg", [P, DE]), sb("e_act", [P, DE])
        aT_hi, aT_lo = sb("e_aT_hi", [P, UOUT, P], F32R), sb("e_aT_lo", [P, UOUT, P], F32R)
        y = sb("e_y", [P, D])
        table = sb("e_table", [P, MAXT + 1, 4], I32)
        gather_idx, row_idx = sb("e_gather_idx", [P, 1], I32), sb("e_row_idx", [P, 1], I32)
        wcol = sb("e_wcol", [P, 1])
        gu_ps = mem.enter_context(nc.psum_tensor("e_gu", [P, 2, 512], F32))
        t_ps = mem.enter_context(nc.psum_tensor("e_t", [P, 2, 512], F32))
        y_ps = mem.enter_context(nc.psum_tensor("e_y_ps", [P, 4, 512], F32))
        table_loaded = sem("e_table_loaded")
        raw_loaded, lo_done = c.sems("e_raw_loaded", RAW), c.sems("e_lo_done", RAW)
        hi_done, used = sem("e_hi_done"), c.sems("e_used", SPL)
        idx_ready, row_idx_ready = sem("e_idx_ready"), sem("e_row_idx_ready")
        x_loaded, turned, t_hi, t_kept = sem("e_x_loaded"), sem("e_turned"), sem("e_t_hi"), c.sems("e_t_kept", 2)
        gu_done, silu_done, act_ready = sem("e_gu_done"), sem("e_silu_done"), sem("e_act_ready")
        y_done, y_kept_a, y_kept_v, y_stored = sem("e_y_done"), sem("e_y_kept_a"), sem("e_y_kept_v"), sem("e_y_stored")
        y_free = sem("e_y_free")
        w_in = io.w_ei.rearrange("e (u a p) n -> e u p a n", a=2, p=P)
        w_out = io.w_eo.rearrange("e (u p) n -> e u p n", p=P)

        def tiles(eng, body):
            count = eng.value_load(c.tile_count[0:1, 0:1], min_val=1, max_val=MAXT)
            with eng.Fori(0, MAXT) as t:
                with eng.If(t < count):
                    body(t)
            return count

        with nc.Block() as block:

            @block.sync
            def _(sp):
                def load(t, ex, u):
                    r = u % RAW
                    sp.wait_ge(lo_done[r], 2 * t + u // RAW + 1)
                    if u < UIN:
                        sp.dma_start(raw[:, r, :].rearrange("p (a n) -> p a n", a=2),
                                     w_in[ds(ex, 1), u, :, :, :].rearrange("e p a n -> (e p) a n")).then_inc(raw_loaded[r], 16)
                    else:
                        sp.dma_start(raw[:, r, :], w_out[ds(ex, 1), u - UIN, :, :].rearrange("e p n -> (e p) n")).then_inc(raw_loaded[r], 16)

                sp.dma_start(table[:], io.slots.rearrange("(t p) f -> p t f", p=P)).then_inc(table_loaded, 16)
                ex0 = sp.value_load(c.tile_expert[0:1, 0:1], min_val=0, max_val=EXPERTS - 1)
                for u in range(AHEAD):
                    load(0, ex0, u)

                def body(t):
                    ex = sp.value_load(c.tile_expert[0:1, ds(t, 1)], min_val=0, max_val=EXPERTS - 1)
                    for u in range(AHEAD, UN):
                        load(t, ex, u)
                    nx = sp.value_load(c.tile_expert[0:1, ds(t + 1, 1)], min_val=0, max_val=EXPERTS - 1)
                    for u in range(AHEAD):
                        load(t + 1, nx, u)

                tiles(sp, body)

            @block.gpsimd
            def _(pool):
                def gather(t):
                    pool.wait_ge(idx_ready, t + 1)
                    c.hold(pool)
                    pool.indirect_dma_start(out=x[:], out_offset=None, in_=io.h2, in_offset=bass.IndirectOffsetOnAxis(
                        ap=gather_idx[:].bitcast(U32), axis=0)).then_inc(x_loaded, 16)

                gather(0)

                def body(t):
                    pool.wait_ge(turned, 5 * t + 4)
                    gather(t + 1)
                    pool.wait_ge(row_idx_ready, t + 1)
                    pool.wait_ge(y_kept_a, 2 * t + 2 + 1)
                    pool.wait_ge(y_kept_v, 2 * t + 2 + 1)
                    c.hold(pool)
                    pool.indirect_dma_start(out=io.expert_rows, out_offset=bass.IndirectOffsetOnAxis(ap=row_idx[:].bitcast(U32), axis=0),
                                            in_=y[:], in_offset=None, bounds_check=TOPK * TOK - 1, oob_is_err=False).then_inc(y_stored, 16)
                    pool.wait_ge(y_stored, 16 * t + 16)
                    pool.sem_inc(y_free, 1)

                count = tiles(pool, body)
                pool.wait_ge(y_stored, count * 16)
                pool.wait_ge(x_loaded, count * 16 + 16)

            @block.tensor
            def _(pe):
                c.start_at_one(pe, *lo_done, act_ready, y_kept_a, y_kept_v, *used, y_free)
                def turn_first_rows():
                    pe.wait_ge(x_loaded, 16)
                    for q in range(4):
                        if q >= 2:
                            pe.wait_ge(t_kept[q % 2], 1)
                        for j in range(4):
                            k = 4 * q + j
                            mm = pe.transpose(t_ps[:, q % 2, j * P:(j + 1) * P], x[:, k * P:(k + 1) * P], c.ident[:])
                        mm.then_inc(turned, 1)

                turn_first_rows()

                def body(t):
                    pe.wait_ge(t_kept[0], 3 * t + 2)
                    pe.wait_ge(t_kept[1], 2 * t + 2)
                    pe.wait_ge(act_ready, t + 1)
                    for u in range(UIN):
                        r, s = u % RAW, u % SPL
                        pe.wait_ge(lo_done[r], 2 * t + u // RAW + 2)
                        for a in range(2):
                            k = 2 * u + a
                            for x_part, w_part, last in ((xT_hi, w_hi, False), (xT_hi, w_lo, False), (xT_lo, w_hi, True)):
                                for b in range(2):
                                    mm = pe.matmul(gu_ps[:, b, :], x_part[:, k, :], w_part[:, s, a * 1024 + b * 512:a * 1024 + b * 512 + 512],
                                                   start=(k == 0 and x_part is xT_hi and w_part is w_hi), stop=(k == KT - 1 and last))
                        mm.then_inc(used[s], 1)
                    pe.wait_ge(used[(UIN - 1) % SPL], 3 * t + 2 + 1)
                    pe.sem_inc(gu_done, 1)
                    pe.wait_ge(x_loaded, 16 * t + 32)
                    for q in range(4):
                        pe.wait_ge(t_kept[q % 2], (3 * t if q % 2 == 0 else 2 * t) + 2 + q // 2)
                        for j in range(4):
                            k = 4 * q + j
                            mm = pe.transpose(t_ps[:, q % 2, j * P:(j + 1) * P], x[:, k * P:(k + 1) * P], c.ident[:])
                        mm.then_inc(turned, 1)
                    pe.wait_ge(t_kept[0], 3 * t + 4)
                    pe.wait_ge(act_ready, t + 2)
                    for j in range(UOUT):
                        mm = pe.transpose(t_ps[:, 0, j * P:(j + 1) * P], act_rows[:, j * P:(j + 1) * P], c.ident[:])
                    mm.then_inc(turned, 1)
                    pe.wait_ge(t_kept[0], 3 * t + 5)
                    pe.wait_ge(y_kept_a, 2 * t + 1)
                    pe.wait_ge(y_kept_v, 2 * t + 1)
                    for u in range(UIN, UN):
                        r, s, k = u % RAW, u % SPL, u - UIN
                        pe.wait_ge(lo_done[r], 2 * t + u // RAW + 2)
                        for a_part, w_part, last in ((aT_hi, w_hi, False), (aT_hi, w_lo, False), (aT_lo, w_hi, True)):
                            for b in range(4):
                                mm = pe.matmul(y_ps[:, b, :], a_part[:, k, :], w_part[:, s, b * 512:(b + 1) * 512],
                                               start=(k == 0 and a_part is aT_hi and w_part is w_hi), stop=(k == UOUT - 1 and last))
                        mm.then_inc(used[s], 1)
                    pe.wait_ge(used[(UN - 1) % SPL], 3 * t + 3 + 1)
                    pe.sem_inc(y_done, 1)

                tiles(pe, body)

            @block.scalar
            def _(act):
                def split_hi(t, u):
                    r, s = u % RAW, u % SPL
                    act.wait_ge(raw_loaded[r], 32 * t + 16 * (u // RAW) + 16)
                    act.wait_ge(used[s], 3 * t + u // SPL + 1)
                    act.activation(w_hi[:, s, :], raw[:, r, :], ACT.Copy).then_inc(hi_done, 1)

                def keep_rows_hi(q, n):
                    act.wait_ge(turned, n)
                    act.activation(xT_hi[:, 4 * q:4 * q + 4, :], t_ps[:, q % 2, :].rearrange("p (a b) -> p a b", a=4), ACT.Copy).then_inc(t_hi, 1)

                for q in range(4):
                    keep_rows_hi(q, q + 1)
                for u in range(AHEAD):
                    split_hi(0, u)

                def body(t):
                    for u in range(AHEAD, UN):
                        split_hi(t, u)
                    act.wait_ge(gu_done, t + 1)
                    act.activation(sg[:], gu_ps[:, 0, :], ACT.Silu).then_inc(silu_done, 1)
                    for q in range(4):
                        keep_rows_hi(q, 5 * t + 5 + q)
                    act.wait_ge(turned, 5 * t + 9)
                    act.activation(aT_hi[:], t_ps[:, 0, :].rearrange("p (a b) -> p a b", a=UOUT), ACT.Copy).then_inc(t_hi, 1)
                    for u in range(AHEAD):
                        split_hi(t + 1, u)
                    act.wait_ge(y_done, t + 1)
                    act.wait_ge(y_free, t + 1)
                    act.wait_ge(row_idx_ready, t + 1)
                    for b in (0, 1):
                        act.activation(y[:, b * 512:(b + 1) * 512], y_ps[:, b, :], ACT.Copy, scale=wcol[:]).then_inc(y_kept_a, 1)

                tiles(act, body)

            @block.vector
            def _(dve):
                def split_lo(t, u):
                    r, s = u % RAW, u % SPL
                    dve.wait_ge(hi_done, UN * t + u + 1)
                    dve.tensor_tensor(w_lo[:, s, :], raw[:, r, :], w_hi[:, s, :], ALU.subtract).then_inc(lo_done[r], 1)

                def keep_rows_lo(q, n):
                    dve.wait_ge(t_hi, n)
                    dve.tensor_tensor(xT_lo[:, 4 * q:4 * q + 4, :], t_ps[:, q % 2, :].rearrange("p (a b) -> p a b", a=4),
                                      xT_hi[:, 4 * q:4 * q + 4, :], ALU.subtract).then_inc(t_kept[q % 2], 1)

                def field(t, f):
                    return table[:, ds(t, 1), f:f + 1].rearrange("p a b -> p (a b)")

                dve.wait_ge(table_loaded, 16)
                dve.tensor_copy(gather_idx[:], field(0, 0)).then_inc(idx_ready, 1)
                for q in range(4):
                    keep_rows_lo(q, q + 1)
                for u in range(AHEAD):
                    split_lo(0, u)

                def body(t):
                    dve.wait_ge(x_loaded, 16 * t + 16)
                    dve.tensor_copy(gather_idx[:], field(t + 1, 0)).then_inc(idx_ready, 1)
                    for u in range(AHEAD, UN):
                        split_lo(t, u)
                    dve.wait_ge(silu_done, t + 1)
                    dve.tensor_tensor(act_rows[:], sg[:], gu_ps[:, 1, :], ALU.mult).then_inc(act_ready, 1)
                    for q in range(4):
                        keep_rows_lo(q, 5 * t + 5 + q)
                    dve.wait_ge(t_hi, 5 * t + 9)
                    dve.tensor_tensor(aT_lo[:], t_ps[:, 0, :].rearrange("p (a b) -> p a b", a=UOUT), aT_hi[:], ALU.subtract).then_inc(t_kept[0], 1)
                    dve.wait_ge(y_free, t + 1)
                    dve.wait_ge(y_kept_a, 2 * t + 1)
                    dve.tensor_copy(row_idx[:], field(t, 1))
                    dve.tensor_copy(wcol[:].bitcast(I32), field(t, 2)).then_inc(row_idx_ready, 1)
                    for u in range(AHEAD):
                        split_lo(t + 1, u)
                    dve.wait_ge(y_done, t + 1)
                    dve.wait_ge(row_idx_ready, t + 1)
                    for b in (2, 3):
                        dve.tensor_scalar(y[:, b * 512:(b + 1) * 512], y_ps[:, b, :], wcol[:], None, ALU.mult).then_inc(y_kept_v, 1)

                tiles(dve, body)


def phase_final(c):
    nc, io, sem = c.nc, c.io, c.sem
    SL = 3
    with ExitStack() as mem:
        def sb(name, shape, dt=F32):
            return mem.enter_context(nc.sbuf_tensor(name, shape, dt))

        x, r0, r1 = (sb(f"f_{n}", [P, SL, D]) for n in ("x", "r0", "r1"))
        g, junk = sb("f_g", [P, D]), sb("f_junk", [P, D])
        ssq, rstd = sb("f_ssq", [P, SL]), sb("f_rstd", [P, SL])
        loaded, stored = c.sems("f_loaded", SL), c.sems("f_stored", SL)
        g_loaded, step, summed = sem("f_g_loaded"), sem("f_step"), sem("f_summed")
        squared, root_done, rstd_done, ready = sem("f_squared"), sem("f_root_done"), sem("f_rstd_done"), sem("f_ready")
        with nc.Block() as block:

            @block.sync
            def _(sp):
                sp.dma_start(g[:], io.norm_final.to_broadcast([P, D])).then_inc(g_loaded, 16)
                with sp.Fori(0, NT // SL) as i:
                    for s in range(SL):
                        t = i * SL + s
                        sp.wait_ge(stored[s], 16 * i + 1)
                        sp.dma_start(x[:, s, :], io.x1[ds(t * P, P), :]).then_inc(loaded[s], 16)
                        sp.dma_start(r0[:, s, :], io.expert_rows[ds(t * P, P), :]).then_inc(loaded[s], 16)
                        sp.dma_start(r1[:, s, :], io.expert_rows[ds(t * P + TOK, P), :]).then_inc(loaded[s], 16)

            @block.vector
            def _(dve):
                def add(s, i, t):
                    dve.wait_ge(loaded[s], 48 * (i + 1))
                    dve.tensor_tensor(r0[:, s, :], r0[:, s, :], r1[:, s, :], ALU.add).then_inc(step, 1)
                    dve.wait_ge(step, t + 1)
                    dve.tensor_tensor(x[:, s, :], x[:, s, :], r0[:, s, :], ALU.add).then_inc(summed, 1)

                def scale(s, t):
                    dve.wait_ge(root_done, t + 1)
                    dve.reciprocal(rstd[:, s:s + 1], ssq[:, s:s + 1]).then_inc(rstd_done, 1)
                    dve.wait_ge(rstd_done, t + 1)
                    dve.scalar_tensor_tensor(x[:, s, :], x[:, s, :], rstd[:, s:s + 1], g[:], ALU.mult, ALU.mult).then_inc(ready, 1)

                dve.wait_ge(g_loaded, 16)
                add(0, 0, 0)
                with dve.Fori(0, NT // SL - 1) as i:
                    for s in range(SL):
                        t = i * SL + s
                        add((s + 1) % SL, i + (s + 1) // SL, t + 1)
                        scale(s, t)
                for s in range(SL):
                    t = NT - SL + s
                    if s + 1 < SL:
                        add(s + 1, NT // SL - 1, t + 1)
                    scale(s, t)

            @block.scalar
            def _(act):
                c.start_at_one(act, *stored)
                with act.Fori(0, NT // SL) as i:
                    for s in range(SL):
                        t = i * SL + s
                        act.wait_ge(summed, t + 1)
                        act.activation(junk[:], x[:, s, :], ACT.Square, accum_out=ssq[:, s:s + 1]).then_inc(squared, 1)
                        act.wait_ge(squared, t + 1)
                        act.activation(ssq[:, s:s + 1], ssq[:, s:s + 1], ACT.Sqrt, bias=c.eps[:], scale=1.0 / D).then_inc(root_done, 1)
                        act.wait_ge(ready, t + 1)
                        act.dma_start(io.y_all[ds(t * P, P), :], x[:, s, :]).then_inc(stored[s], 16)
                for s in range(SL):
                    act.wait_ge(stored[s], 16 * (NT // SL) + 1)



class Dram:

    def __init__(self, x, cache_k, cache_v, small, norm_mix, w_in, lam, head_norm, w_out, norm_ffn, w_router, b_router,
                 w_ei, w_eo, norm_final, y_all, k_all, v_all, conv_all):
        self.x, self.cache_k, self.cache_v, self.small = x, cache_k, cache_v, small
        self.norm_mix, self.w_in, self.lam, self.head_norm, self.w_out = norm_mix, w_in, lam, head_norm, w_out
        self.norm_ffn, self.w_router, self.b_router, self.w_ei, self.w_eo = norm_ffn, w_router, b_router, w_ei, w_eo
        self.norm_final, self.y_all, self.k_all, self.v_all, self.conv_all = norm_final, y_all, k_all, v_all, conv_all


def build(nc, io):
    io.chunks = nc.dram_tensor("chunks", (3 * CH, P, TOK), F32).ap()
    io.o_new = nc.dram_tensor("o_new", (STREAMS * NEW, DC), F32).ap()
    io.x1 = nc.dram_tensor("x1", (TOK, D), F32).ap()
    io.h2 = nc.dram_tensor("h2", (TOK, D), F32).ap()
    io.slots = nc.dram_tensor("slots", ((MAXT + 1) * P, 4), I32).ap()
    io.expert_rows = nc.dram_tensor("expert_rows", (TOPK * TOK, D), F32).ap()
    with ExitStack() as stack:
        c = Ctx(nc, io)

        def sb(name, shape, dt=F32):
            return stack.enter_context(nc.sbuf_tensor(name, shape, dt))

        c.ident = sb("ident", [P, P])
        c.eps = sb("eps", [P, 1])
        c.taps = sb("taps", [P, CH, 2 * STREAMS + 3])
        c.neglam = sb("neglam", [P, 1])
        c.hn = sb("hn", [P, VD])
        c.tile_expert = sb("tile_expert", [1, MAXT + 1], I32)
        c.tile_count = sb("tile_count", [1, 1], I32)
        with ExitStack() as mem:
            hT_hi = mem.enter_context(nc.sbuf_tensor("hT_hi", [P, KT, TOK], F32R))
            hT_lo = mem.enter_context(nc.sbuf_tensor("hT_lo", [P, KT, TOK], F32R))
            phase_norm(c, hT_hi, hT_lo)
            phase_project(c, hT_hi, hT_lo)
        with ExitStack() as mem:
            def cat(name):
                return mem.enter_context(nc.sbuf_tensor(name, [P, CH, TOK], F32R))

            o_hi, o_lo = cat("o_hi"), cat("o_lo")
            phase_decode(c, o_hi, o_lo)
            a_hi, a_lo = cat("a_hi"), cat("a_lo")
            phase_attend(c, a_hi, a_lo, o_hi, o_lo)
            phase_mix_out(c, a_hi, a_lo, o_hi, o_lo)
        c.clear_semaphores()
        phase_route(c)
        phase_experts(c)
        phase_final(c)


def kernel(x_prompt, x_sample, cache_k, cache_v, state_conv, norm_mix, w_in, conv_w, lambda_q1, lambda_k1, lambda_q2,
           lambda_k2, head_norm, w_out, norm_ffn, w_router_group, b_router_group, w_router_expert, b_router_expert,
           w_expert_in, w_expert_out, norm_final):
    import concourse.bacc as bacc
    from concourse.bass_utils import run_bass_kernel_spmd

    a = np.asarray
    arrays = dict(
        x=np.concatenate([a(x_prompt)[0], a(x_sample).reshape(STREAMS * NEW, D)]),
        cache_k=a(cache_k).reshape(STREAMS, PAST, DC),
        cache_v=a(cache_v).reshape(STREAMS, PAST, DC),
        small=np.concatenate([a(state_conv).reshape(2 * STREAMS, DC), a(conv_w).reshape(3, DC)]),
        norm_mix=a(norm_mix).reshape(1, D),
        w_in=a(w_in)[0],
        lam=np.concatenate([a(v).reshape(1, DH) for v in (lambda_q1, lambda_k1, lambda_q2, lambda_k2)], axis=1),
        head_norm=a(head_norm).reshape(1, VD),
        w_out=a(w_out)[0],
        norm_ffn=a(norm_ffn).reshape(1, D),
        w_router=np.concatenate([a(w_router_group)[0], a(w_router_expert)[0]], axis=1),
        b_router=np.concatenate([a(b_router_group), a(b_router_expert)], axis=1),
        w_ei=a(w_expert_in)[0],
        w_eo=a(w_expert_out)[0],
        norm_final=a(norm_final).reshape(1, D),
    )
    nc = bacc.Bacc("TRN2", target_bir_lowering=False, num_devices=1)
    tensors = {}
    for name in arrays:
        arrays[name] = np.ascontiguousarray(arrays[name])
        tensors[name] = nc.dram_tensor(name, arrays[name].shape, F32, kind="ExternalInput").ap()
    outs = dict(y_all=(TOK, D), k_all=(TOK, DC), v_all=(TOK, DC), conv_all=(2 + 2 * STREAMS, DC))
    for name, shape in outs.items():
        tensors[name] = nc.dram_tensor(name, shape, F32, kind="ExternalOutput").ap()
    build(nc, Dram(**tensors))
    got = run_bass_kernel_spmd(nc, [arrays], core_ids=[0]).results[0]
    y, k, v, conv = (got[name] for name in outs)
    return (
        y[:PROMPT].reshape(1, PROMPT, D), y[PROMPT:].reshape(STREAMS, NEW, D),
        k[:PROMPT].reshape(1, 1, PROMPT, HEADS, 2, DH), v[:PROMPT].reshape(1, 1, PROMPT, HEADS, VD),
        conv[:2].reshape(1, 1, 2, DC),
        k[PROMPT:].reshape(1, STREAMS, NEW, HEADS, 2, DH), v[PROMPT:].reshape(1, STREAMS, NEW, HEADS, VD),
        conv[2:].reshape(1, STREAMS, 2, DC),
    )
```

```python
from contextlib import ExitStack

import numpy as np
import concourse.bass as bass
from concourse import mybir

F32 = mybir.dt.float32
F32R = mybir.dt.float32r
I32 = mybir.dt.int32
U32 = mybir.dt.uint32
ALU = mybir.AluOpType
ACT = mybir.ActivationFunctionType
AX = mybir.AxisListType
ds = bass.ds

P = 128
D = 2048
PROMPT = 1024
STREAMS = 8
NEW = 16
PAST = 512
TOK = PROMPT + STREAMS * NEW
NT = TOK // P
KT = D // P
HALF = KT // 2
NB = 3
BLK = TOK // NB
DC = D // 2
CH = DC // P
HEADS = 8
DH = 64
VD = 128
SCALE = DH ** -0.5
LAM_INIT = 0.8 - 0.6
EPS = 1e-6
MASKED = -1e30
GROUPS = 4
PER = 8
EXPERTS = GROUPS * PER
TOPK = 2
DE = 512
NR = GROUPS + EXPERTS
GROUP = 2 * P
MAXG = TOPK * TOK // GROUP + EXPERTS - 1
SLOT_GROUPS = MAXG + 3
BIG = 1e30
NO_ROW = 1 << 20
U = 2 * D


class Ctx:

    def __init__(self, nc, io):
        self.nc, self.io, self.in_use = nc, io, []
        self.passed = nc.alloc_semaphore("passed")

    def sem(self, name):
        self.in_use.append(self.nc.alloc_semaphore(name))
        return self.in_use[-1]

    def clear_semaphores(self):
        self.nc.clear_and_free_semaphores(self.in_use)
        self.nc.all_engine_barrier()
        self.in_use = []

    def start_at_one(self, eng, *sems):
        for sem in sems:
            eng.sem_inc(sem, 1)

    def hold(self, eng):
        eng.sem_inc(self.passed, 1)

    def sems(self, name, n):
        return [self.sem(f"{name}{i}") for i in range(n)]


def phase_norm(c, hT_hi, hT_lo):
    nc, io, sem = c.nc, c.io, c.sem
    SL = 3
    with ExitStack() as mem:
        x = mem.enter_context(nc.sbuf_tensor("n_x", [P, SL, D], F32))
        g = mem.enter_context(nc.sbuf_tensor("n_g", [P, D], F32))
        ssq = mem.enter_context(nc.sbuf_tensor("n_ssq", [P, SL], F32))
        rstd = mem.enter_context(nc.sbuf_tensor("n_rstd", [P, SL], F32))
        small = mem.enter_context(nc.sbuf_tensor("n_small", [19, DC], F32))
        junk = mem.enter_context(nc.psum_tensor("n_junk", [P, D], F32))
        tp = mem.enter_context(nc.psum_tensor("n_tp", [P, 4, 512], F32))
        x_loaded = c.sems("n_x_loaded", SL)
        x_done = c.sems("n_x_done", SL)
        g_loaded, squared, ms_done = sem("n_g_loaded"), sem("n_squared"), sem("n_ms_done")
        small_loaded, small_turned, small_kept = sem("n_small_loaded"), sem("n_small_turned"), sem("n_small_kept")
        rstd_done, h_ready, turned = sem("n_rstd_done"), sem("n_h_ready"), sem("n_turned")
        hi_done, lo_done, ident0, ident_ready = sem("n_hi_done"), sem("n_lo_done"), sem("n_ident0"), sem("n_ident_ready")
        lam_loaded, lam_step = sem("n_lam_loaded"), sem("n_lam_step")
        lam_exp = sem("n_lam_exp")
        lamb = mem.enter_context(nc.sbuf_tensor("n_lamb", [P, 4, DH], F32))
        lw = mem.enter_context(nc.sbuf_tensor("n_lw", [P, 8], F32))
        with nc.Block() as block:

            @block.sync
            def _(sp):
                sp.dma_start(g[:], io.norm_mix.to_broadcast([P, D])).then_inc(g_loaded, 16)
                with sp.Fori(0, NT // SL) as i:
                    for s in range(SL):
                        sp.wait_ge(x_done[s], i + 1)
                        sp.dma_start(x[:, s, :], io.x[ds((i * SL + s) * P, P), :]).then_inc(x_loaded[s], 16)
                sp.dma_start(small[:], io.small).then_inc(small_loaded, 16)
                sp.dma_start(lamb[:].rearrange("p a b -> p (a b)"), io.lam.to_broadcast([P, 4 * DH])).then_inc(lam_loaded, 16)
                sp.dma_start(c.hn[:], io.head_norm.to_broadcast([P, VD])).then_inc(lam_loaded, 16)

            @block.gpsimd
            def _(pool):
                pool.memset(c.ident[:], 0.0).then_inc(ident0, 1)
                pool.wait_ge(ident0, 1)
                pool.affine_select(out=c.ident[:], in_=c.ident[:], compare_op=ALU.not_equal, fill=1.0, base=0,
                                   pattern=[[-1, P]], channel_multiplier=1).then_inc(ident_ready, 1)
                pool.memset(c.eps[:], EPS).then_inc(ident_ready, 1)

            @block.scalar
            def _(act):
                def root(s, t):
                    act.activation(junk[:], x[:, s, :], ACT.Square, accum_out=ssq[:, s:s + 1]).then_inc(squared, 1)
                    act.wait_ge(squared, t + 1)
                    act.activation(ssq[:, s:s + 1], ssq[:, s:s + 1], ACT.Sqrt, bias=c.eps[:], scale=1.0 / D).then_inc(ms_done, 1)

                act.wait_ge(ident_ready, 2)
                act.wait_ge(x_loaded[0], 16)
                root(0, 0)

                def keep_hi(t, n):
                    for q in range(4):
                        act.wait_ge(turned, 4 * n + q + 1)
                        act.activation(hT_hi[:, 4 * q:4 * q + 4, ds(t * P, P)],
                                       tp[:, q, :].rearrange("p (a b) -> p a b", a=4), ACT.Copy).then_inc(hi_done, 1)

                with act.Fori(0, NT // SL - 1) as i:
                    for s in range(SL):
                        nx = (s + 1) % SL
                        act.wait_ge(x_loaded[nx], 16 * (i + 1 + (s == SL - 1)))
                        act.wait_ge(rstd_done, i * SL + s + 1)
                        root(nx, i * SL + s + 1)
                        keep_hi(i * SL + s, i * SL + s)
                for s in range(SL):
                    t = NT - SL + s
                    if s < SL - 1:
                        act.wait_ge(x_loaded[s + 1], 16 * (NT // SL))
                        act.wait_ge(rstd_done, t + 1)
                        root(s + 1, t + 1)
                    keep_hi(t, t)
                act.wait_ge(lam_step, 2)
                act.activation(lw[:, 2:4], lw[:, 0:2], ACT.Exp).then_inc(lam_exp, 1)

            @block.vector
            def _(dve):
                dve.wait_ge(g_loaded, 16)
                with dve.Fori(0, NT // SL) as i:
                    for s in range(SL):
                        t = i * SL + s
                        dve.wait_ge(ms_done, t + 1)
                        dve.reciprocal(rstd[:, s:s + 1], ssq[:, s:s + 1]).then_inc(rstd_done, 1)
                        dve.wait_ge(rstd_done, t + 1)
                        dve.scalar_tensor_tensor(x[:, s, :], x[:, s, :], rstd[:, s:s + 1], g[:], ALU.mult,
                                                 ALU.mult).then_inc(h_ready, 1)
                        for q in range(4):
                            dve.wait_ge(hi_done, 4 * t + q + 1)
                            dve.tensor_tensor(hT_lo[:, 4 * q:4 * q + 4, ds(t * P, P)],
                                              tp[:, q, :].rearrange("p (a b) -> p a b", a=4),
                                              hT_hi[:, 4 * q:4 * q + 4, ds(t * P, P)], ALU.subtract).then_inc(lo_done, 1)
                dve.wait_ge(small_turned, 1)
                dve.tensor_copy(c.taps[:], tp[:, 0, 0:CH * 19].rearrange("p (a b) -> p a b", a=CH)).then_inc(small_kept, 1)
                dve.wait_ge(lam_loaded, 32)
                lv = lamb[:].rearrange("p (m a) d -> p m a d", m=2)
                dve.tensor_tensor(lv[:, :, 0, :], lv[:, :, 0, :], lv[:, :, 1, :], ALU.mult).then_inc(lam_step, 1)
                dve.wait_ge(lam_step, 1)
                dve.tensor_reduce(lw[:, 0:2], lv[:, :, 0, :], AX.X, ALU.add).then_inc(lam_step, 1)
                dve.wait_ge(lam_exp, 1)
                dve.scalar_tensor_tensor(c.neglam[:], lw[:, 3:4], -LAM_INIT, lw[:, 2:3], ALU.add, ALU.subtract).then_inc(lam_step, 1)
                dve.tensor_scalar(c.hn[:], c.hn[:], 1.0 - LAM_INIT, None, ALU.mult).then_inc(lam_step, 1)

            @block.tensor
            def _(pe):
                c.start_at_one(pe, *x_done, lo_done)
                pe.wait_ge(ident_ready, 1)
                with pe.Fori(0, NT // SL) as i:
                    for s in range(SL):
                        t = i * SL + s
                        pe.wait_ge(h_ready, t + 1)
                        for q in range(4):
                            pe.wait_ge(lo_done, 4 * t + 1)
                            for j in range(4):
                                k = 4 * q + j
                                mm = pe.transpose(tp[:, q, j * P:(j + 1) * P], x[:, s, k * P:(k + 1) * P], c.ident[:])
                            mm.then_inc(turned, 1)
                        pe.wait_ge(turned, 4 * t + 4)
                        pe.sem_inc(x_done[s], 1)
                pe.wait_ge(small_loaded, 16)
                pe.wait_ge(lo_done, 4 * NT + 1)
                for j in range(CH):
                    mm = pe.transpose(tp[:, 0, j * 19:(j + 1) * 19], small[:, j * P:(j + 1) * P], c.ident[0:19, 0:19])
                mm.then_inc(small_turned, 1)


def weight_chunks(c, tag, w_raw, w_hi, w_lo):
    loaded, split = c.sems(f"{tag}_w_loaded", 2), c.sems(f"{tag}_w_split", 2)
    hi_done, half0_used = c.sem(f"{tag}_w_hi_done"), c.sem(f"{tag}_half0_used")
    z_done, z_kept = c.sems(f"{tag}_z_done", NB), c.sems(f"{tag}_z_kept", NB)

    def load(sp, n, w_cols):
        for half in range(2):
            sp.wait_ge(split[half], n + 1)
            c.hold(sp)
            sp.dma_start(w_raw[:, half * HALF:(half + 1) * HALF, :], w_cols(half)).then_inc(loaded[half], 16)

    def split_chunk(pool, n):
        for half in range(2):
            part = slice(half * HALF, (half + 1) * HALF)
            pool.wait_ge(loaded[half], 16 * (n + 1))
            pool.wait_ge(half0_used if half == 0 else z_done[NB - 1], n + 1)
            c.hold(pool)
            pool.tensor_copy(w_hi[:, part, :], w_raw[:, part, :]).then_inc(hi_done, 1)
            pool.wait_ge(hi_done, 2 * n + half + 1)
            pool.tensor_tensor(w_lo[:, part, :], w_raw[:, part, :], w_hi[:, part, :], ALU.subtract).then_inc(split[half], 1)

    def products(pe, n, half, z, x_hi, x_lo):
        pe.wait_ge(split[half], n + 2)
        for b in range(NB):
            if half == 0:
                pe.wait_ge(z_kept[b], n + 1)
            cols = slice(b * BLK, (b + 1) * BLK)
            for j in range(HALF):
                k = half * HALF + j
                xk = k % x_hi.shape[1]
                out = z[:, b, 0:BLK]
                pe.matmul(out, w_hi[:, k, :], x_hi[:, xk, cols], start=(k == 0), stop=False)
                pe.matmul(out, w_hi[:, k, :], x_lo[:, xk, cols], start=False, stop=False)
                mm = pe.matmul(out, w_lo[:, k, :], x_hi[:, xk, cols], start=False, stop=(k == KT - 1))
            if half == 1:
                mm.then_inc(z_done[b], 1)
        if half == 0:
            mm.then_inc(half0_used, 1)

    return load, split_chunk, products, z_done, z_kept, (*split, half0_used, *z_done, *z_kept)


def phase_project(c, hT_hi, hT_lo):
    nc, io, sem = c.nc, c.io, c.sem
    NCONV = 3 * CH
    with ExitStack() as mem:
        def sb(name, shape, dt=F32):
            return mem.enter_context(nc.sbuf_tensor(name, shape, dt))

        w_raw = sb("p_w_raw", [P, KT, P])
        w_hi = sb("p_w_hi", [P, KT, P], F32R)
        w_lo = sb("p_w_lo", [P, KT, P], F32R)
        e = sb("p_e", [P, TOK])
        xs = sb("p_xs", [P, TOK])
        up = sb("p_up", [P, 2 + PROMPT])
        us = sb("p_us", [P, STREAMS, 2 + NEW])
        tail = sb("p_tail", [P, CH, 2 + 2 * STREAMS])
        rows = sb("p_rows", [P, NT, P])
        tail_rows = sb("p_tail_rows", [2 + 2 * STREAMS, DC])
        z = mem.enter_context(nc.psum_tensor("p_z", [P, NB, 512], F32))
        tp = mem.enter_context(nc.psum_tensor("p_tp", [P, NB, 512], F32))
        load, split_chunk, products, z_done, z_kept, first_counts = weight_chunks(c, "p", w_raw, w_hi, w_lo)
        zeroed, step = sem("p_zeroed"), sem("p_conv_step")
        e_ready, e_stored = sem("p_e_ready"), sem("p_e_stored")
        e_turned, rows_ready, rows_stored = sem("p_e_turned"), sem("p_rows_ready"), sem("p_rows_stored")
        tail_turned, tail_kept, tail_stored = sem("p_tail_turned"), sem("p_tail_kept"), sem("p_tail_stored")

        w = io.w_in.rearrange("(h k p) n -> h p k n", h=2, p=P)
        NQ = NCONV + CH
        N = NQ + 2 * CH
        tr = slice(0, 3 * P)

        with nc.Block() as block:

            @block.sync
            def _(sp):
                with sp.Fori(0, CH) as t:
                    for r, kind in enumerate((2, 1, 0)):
                        load(sp, t * 3 + r, lambda half: w[half, :, :, ds(t * P + kind * DC, P)])
                with sp.Fori(0, 3 * CH) as t:
                    load(sp, t + NCONV, lambda half: w[half, :, :, ds(t * P + 3 * DC, P)])

            @block.gpsimd
            def _(pool):
                pool.memset(up[:, 0:2], 0.0).then_inc(zeroed, 1)
                with pool.Fori(0, N) as n:
                    split_chunk(pool, n)

            @block.tensor
            def _(pe):
                c.start_at_one(pe, *first_counts, e_stored, rows_stored, rows_ready)
                def turn_back(m):
                    pe.wait_ge(e_ready, m + 1 + 2 * CH)
                    for b in range(NB):
                        for j in range(NB):
                            mm = pe.transpose(tp[:, b, j * P:(j + 1) * P], e[:, (b * NB + j) * P:(b * NB + j + 1) * P],
                                              c.ident[:])
                        mm.then_inc(e_turned, 1)

                with pe.Fori(0, NQ) as n:
                    products(pe, n, 0, z, hT_hi, hT_lo)
                    products(pe, n, 1, z, hT_hi, hT_lo)
                products(pe, NQ, 0, z, hT_hi, hT_lo)
                products(pe, NQ, 1, z, hT_hi, hT_lo)
                with pe.Fori(1, 2 * CH) as m:
                    products(pe, m + NQ, 0, z, hT_hi, hT_lo)
                    pe.wait_ge(rows_ready, m)
                    turn_back(m - 1)
                    products(pe, m + NQ, 1, z, hT_hi, hT_lo)
                pe.wait_ge(rows_ready, 2 * CH)
                turn_back(2 * CH - 1)
                pe.wait_ge(rows_ready, 2 * CH + 1)
                for j in range(CH):
                    mm = pe.transpose(tp[0:2 + 2 * STREAMS, j // 4, (j % 4) * P:(j % 4 + 1) * P], tail[:, j, :], c.ident[:])
                mm.then_inc(tail_turned, 1)

            @block.vector
            def _(dve):
                cut = PROMPT - 2 * BLK
                ys = xs[:, PROMPT:TOK].rearrange("p (s r) -> p s r", s=STREAMS)
                es = slice(2, 2 + NEW)
                STEPS = 10
                dve.wait_ge(zeroed, 1)
                with dve.Fori(0, CH) as t:
                    for b in range(NB):
                        dve.wait_ge(z_done[b], t * 3 + 2)
                        dve.tensor_copy(xs[:, b * BLK:(b + 1) * BLK], z[:, b, 0:BLK]).then_inc(z_kept[b], 1)
                    dve.tensor_copy(us[:, :, 0:2], c.taps[:, ds(t, 1), 0:2 * STREAMS].rearrange(
                        "p a (s r) -> p (a s) r", s=STREAMS)).then_inc(step, 1)
                    dve.wait_ge(z_kept[2], t * 3 + 2)
                    for b in range(2):
                        dve.wait_ge(z_done[b], t * 3 + 2 + 1)
                        dve.tensor_tensor(up[:, 2 + b * BLK:2 + (b + 1) * BLK], z[:, b, 0:BLK],
                                          xs[:, b * BLK:(b + 1) * BLK], ALU.mult).then_inc(z_kept[b], 1)
                    dve.wait_ge(z_done[2], t * 3 + 2 + 1)
                    dve.tensor_tensor(up[:, 2 + 2 * BLK:2 + PROMPT], z[:, 2, 0:cut], xs[:, 2 * BLK:PROMPT],
                                      ALU.mult).then_inc(step, 1)
                    dve.tensor_tensor(us[:, :, es], z[:, 2, cut:BLK].rearrange("p (s r) -> p s r", s=STREAMS), ys,
                                      ALU.mult).then_inc(z_kept[2], 1)
                    dve.wait_ge(z_kept[2], t * 3 + 2 + 1)
                    dve.wait_ge(z_kept[1], t * 3 + 2 + 1)
                    dve.wait_ge(step, t * STEPS + 2)
                    dve.tensor_copy(tail[:, ds(t, 1), 0:2].rearrange("p a b -> p (a b)"), up[:, PROMPT:PROMPT + 2]).then_inc(step, 1)
                    dve.tensor_copy(tail[:, ds(t, 1), 2:2 + 2 * STREAMS].rearrange("p a (s r) -> p (a s) r", s=STREAMS),
                                    us[:, :, NEW:NEW + 2]).then_inc(step, 1)
                    def tap(j):
                        return c.taps[:, ds(t, 1), 2 * STREAMS + j:2 * STREAMS + j + 1].rearrange("p a b -> p (a b)")
                    dve.tensor_scalar(xs[:, 0:PROMPT], up[:, 0:PROMPT], tap(0), None, ALU.mult).then_inc(step, 1)
                    dve.tensor_scalar(ys, us[:, :, 0:NEW], tap(0), None, ALU.mult).then_inc(step, 1)
                    for j in (1, 2):
                        dve.wait_ge(step, t * STEPS + 4 + 2 * j)
                        dve.scalar_tensor_tensor(xs[:, 0:PROMPT], up[:, j:j + PROMPT], tap(j), xs[:, 0:PROMPT], ALU.mult,
                                                 ALU.add).then_inc(step, 1)
                        dve.scalar_tensor_tensor(ys, us[:, :, j:j + NEW], tap(j), ys, ALU.mult, ALU.add).then_inc(step, 1)
                    dve.wait_ge(step, t * STEPS + STEPS)
                    dve.wait_ge(e_stored, 16 * t + 1)
                    for b in range(NB):
                        dve.wait_ge(z_done[b], t * 3 + 3 + 1)
                        dve.tensor_tensor(e[:, b * BLK:(b + 1) * BLK], z[:, b, 0:BLK], xs[:, b * BLK:(b + 1) * BLK],
                                          ALU.mult).then_inc(z_kept[b], 1)
                    dve.wait_ge(z_kept[2], t * 3 + 3 + 1)
                    dve.sem_inc(e_ready, 1)
                with dve.Fori(0, CH) as t:
                    dve.wait_ge(e_stored, 16 * (t + CH) + 1)
                    for b in range(NB):
                        dve.wait_ge(z_done[b], t + NCONV + 2)
                        dve.tensor_scalar(e[:, b * BLK:(b + 1) * BLK], z[:, b, 0:BLK], SCALE, None, ALU.mult).then_inc(z_kept[b], 1)
                    dve.wait_ge(z_kept[2], t + NCONV + 2)
                    dve.sem_inc(e_ready, 1)

                def keep_rows(m):
                    dve.wait_ge(rows_stored, 16 * m + 1)
                    for b in range(NB):
                        dve.wait_ge(e_turned, NB * m + b + 1)
                        cp = dve.tensor_copy(rows[:, b * NB:(b + 1) * NB, :],
                                             tp[:, b, tr].rearrange("p (a q) -> p a q", a=NB))
                    cp.then_inc(rows_ready, 1)

                def keep_e(m, stored):
                    dve.wait_ge(e_stored, stored + 1)
                    for b in range(NB):
                        dve.wait_ge(z_done[b], m + NQ + 2)
                        dve.tensor_copy(e[:, b * BLK:(b + 1) * BLK], z[:, b, 0:BLK]).then_inc(z_kept[b], 1)
                    dve.wait_ge(z_kept[2], m + NQ + 2)
                    dve.sem_inc(e_ready, 1)

                keep_e(0, 16 * 2 * CH)
                with dve.Fori(1, CH + 1) as m:
                    keep_rows(m - 1)
                    keep_e(m, (m + 2 * CH) * 16)
                with dve.Fori(CH + 1, 2 * CH) as m:
                    keep_rows(m - 1)
                    keep_e(m, 16 * 3 * CH)
                keep_rows(2 * CH - 1)
                dve.wait_ge(tail_turned, 1)
                dve.tensor_copy(tail_rows[:].rearrange("p (a q) -> p a q", a=2), tp[0:2 + 2 * STREAMS, 0:2, :]).then_inc(tail_kept, 1)

            @block.scalar
            def _(act):
                with act.Fori(0, 2 * CH) as t:
                    act.wait_ge(e_ready, t + 1)
                    act.dma_start(io.chunks[ds(t, 1), :, :].rearrange("a p n -> (a p) n"), e[:]).then_inc(e_stored, 16)

                def store_rows(dram, m, done):
                    act.wait_ge(rows_ready, done + 2)
                    act.dma_start(dram.rearrange("(t p) n -> p t n", p=P)[:, :, ds(m * P, P)], rows[:]).then_inc(rows_stored, 16)

                with act.Fori(0, CH) as m:
                    act.wait_ge(e_ready, m + 2 * CH + 1)
                    act.dma_start(io.chunks[ds(m + 2 * CH, 1), :, :].rearrange("a p n -> (a p) n"), e[:]).then_inc(e_stored, 16)
                    store_rows(io.k_all, m, m)
                with act.Fori(0, CH) as m:
                    store_rows(io.v_all, m, m + CH)
                act.wait_ge(tail_kept, 1)
                act.dma_start(io.conv_all, tail_rows[:]).then_inc(tail_stored, 16)
                act.wait_ge(tail_stored, 16)
                act.wait_ge(rows_stored, 16 * 2 * CH + 1)
                act.wait_ge(e_stored, 16 * 3 * CH + 1)


def head_norm(c, dve, o, square, ssq, rstd, step, n, root_ready):
    dve.wait_ge(root_ready, n + 1)
    dve.reciprocal(rstd[:], ssq[:]).then_inc(step, 1)
    dve.wait_ge(step, 4 * n + 3)
    dve.tensor_tensor(o[:], o[:], rstd[:].unsqueeze(2).to_broadcast([P, HEADS, VD]), ALU.mult).then_inc(step, 1)
    dve.wait_ge(step, 4 * n + 4)


def norm_sums(c, dve, o, square, ssq, step, n):
    dve.tensor_tensor(square[:], o[:], o[:], ALU.mult).then_inc(step, 1)
    dve.wait_ge(step, 4 * n + 1)
    dve.tensor_reduce(ssq[:], square[:], AX.X, ALU.add).then_inc(step, 1)


def phase_attend(c, a_hi, a_lo, o_hi, o_lo):
    nc, io, sem = c.nc, c.io, c.sem
    QT = PROMPT // P
    with ExitStack() as mem:
        def sb(name, shape, dt=F32):
            return mem.enter_context(nc.sbuf_tensor(name, shape, dt))

        q = sb("a_q", [P, 2, PROMPT])
        k = sb("a_k", [P, 2, PROMPT])
        v = sb("a_v", [P, 2, QT, VD])
        pr = sb("a_pr", [P, 2, 2, PROMPT])
        at = sb("a_at", [P, 2, PROMPT])
        o = sb("a_o", [P, 2, QT, VD])
        nb, l, rl = (sb(f"a_{n}", [P, 2, 2]) for n in ("nb", "l", "rl"))
        cf = sb("a_cf", [P, 1])
        mask_q, mask_k = sb("a_mask_q", [P, P]), sb("a_mask_k", [P, P // 2])
        ssq, rstd = sb("a_ssq", [P, QT]), sb("a_rstd", [P, QT])
        a_raw = sb("a_raw", [P, TOK])
        square = a_raw[:, 0:QT * VD].rearrange("p (a b) -> p a b", a=QT)
        s_ps = mem.enter_context(nc.psum_tensor("a_s", [P, 2, PROMPT], F32))
        t_ps = mem.enter_context(nc.psum_tensor("a_t", [P, 2, 512], F32))
        o_ps = mem.enter_context(nc.psum_tensor("a_o_ps", [P, 2, 512], F32))
        head_loaded, head_used = c.sems("a_head_loaded", 2), c.sems("a_head_used", 2)
        scores_done, exp_done, bias_ready = c.sems("a_scores_done", 2), c.sems("a_exp_done", 2), c.sems("a_bias_ready", 2)
        step, mixed, mask_step = sem("a_step"), sem("a_mixed"), sem("a_mask_step")
        turned, t_kept = c.sems("a_turned", 2), c.sems("a_t_kept", 2)
        at_ready, pv_done, o_kept = sem("a_at_ready"), sem("a_pv_done"), sem("a_o_kept")
        sums_ready, root_ready, rstd_ready, scaled, normed = (sem(f"a_{n}") for n in ("sums_ready", "root_ready", "rstd_ready", "scaled", "normed"))
        squared, out_hi, out_done = sem("a_squared"), sem("a_out_hi"), sem("a_out_done")
        raw_loaded, split_hi, split_lo = sem("a_raw_loaded"), sem("a_split_hi"), sem("a_split_lo")
        STEPS = 2

        TURNS = {7: (0, 1), 0: (2,), 1: (3,), 2: (4,), "out": (5, 6), 3: (7,), 4: (8, 9), 5: (10, 11), 6: (12, 13),
                 "last out": (2, 3)}
        OUT_STEP = 3

        def bank_use(h, turn):
            missing = 1 if isinstance(h, int) and h == 0 and turn < TURNS["out"][0] else 2
            return turn % 2, 7 * h + turn // 2 - missing

        def blocks(i, n):
            return range(4 * n, min(4 * n + 4, i + 1))

        def pair(body, eng):
            body(0, True)
            with eng.Fori(1, HEADS // 2) as it:
                body(it, False)

        with nc.Block() as block:

            @block.gpsimd
            def _(pool):
                pool.memset(mask_k[:], 1.0).then_inc(mask_step, 1)
                pool.memset(mask_q[:], 0.0).then_inc(mask_step, 1)
                pool.wait_ge(mask_step, 2)
                for m in range(2):
                    pool.memset(mask_q[m * DH:m * DH + 1, 0:P // 2], MASKED).then_inc(mask_step, 1)
                with pool.Fori(0, HEADS // 2) as it:
                    for s in range(2):
                        h = 2 * it + s
                        pool.wait_ge(o_kept, QT * (h + 1))
                        pool.wait_ge(split_lo, h + 1)
                        pool.tensor_tensor(square, o[:, s], o[:, s], ALU.mult).then_inc(squared, 1)
                        pool.wait_ge(rstd_ready, h + 1)
                        pool.tensor_tensor(o[:, s], o[:, s], rstd[:].unsqueeze(2).to_broadcast([P, QT, VD]), ALU.mult).then_inc(scaled, 1)
                        pool.wait_ge(scaled, h + 1)
                        pool.tensor_tensor(o[:, s], o[:, s], c.hn[:].unsqueeze(1).to_broadcast([P, QT, VD]), ALU.mult).then_inc(normed, 1)
                        pool.dma_start(a_raw[:], io.chunks[ds(h, 1), :, :].rearrange("a p n -> (a p) n")).then_inc(raw_loaded, 16)
                        pool.wait_ge(raw_loaded, 16 * (h + 1))
                        c.hold(pool)
                        hi = a_hi[:, ds(h, 1), :].rearrange("p a b -> p (a b)")
                        pool.tensor_copy(hi, a_raw[:]).then_inc(split_hi, 1)
                        pool.wait_ge(split_hi, h + 1)
                        pool.tensor_tensor(a_lo[:, ds(h, 1), :].rearrange("p a b -> p (a b)"), a_raw[:], hi, ALU.subtract).then_inc(split_lo, 1)

            @block.sync
            def _(sp):
                with sp.Fori(0, HEADS // 2) as it:
                    for s in range(2):
                        h = 2 * it + s
                        sp.wait_ge(head_used[s], it + 1)
                        c.hold(sp)
                        sp.dma_start(q[:, s, :], io.chunks[ds(h + CH, 1), :, 0:PROMPT].rearrange("a p n -> (a p) n")).then_inc(head_loaded[s], 16)
                        sp.dma_start(k[:, s, :], io.chunks[ds(h + 2 * CH, 1), :, 0:PROMPT].rearrange("a p n -> (a p) n")).then_inc(head_loaded[s], 16)
                        sp.dma_start(v[:, s, :, :], io.v_all[0:PROMPT, ds(h * VD, VD)].rearrange("(t p) e -> p t e", p=P)).then_inc(head_loaded[s], 16)

            @block.tensor
            def _(pe):
                c.start_at_one(pe, *head_used, *exp_done, *t_kept, split_lo)

                def scores(s, i, g):
                    w = P * (i + 1)
                    for m in range(2):
                        part = slice(m * DH, (m + 1) * DH)
                        pe.wait_ge(exp_done[m], g + 1)
                        for b in range(0, P * (i + 1), 512):
                            e = min(b + 512, P * (i + 1))
                            mm = pe.matmul(s_ps[:, m, b:e], q[part, s, i * P:(i + 1) * P], k[part, s, b:e], start=True, stop=e < w)
                        mm = pe.matmul(s_ps[:, m, w - P // 2:w], mask_q[part, :], mask_k[part, :], start=False, stop=True)
                        mm.then_inc(scores_done[m], 1)

                def turn(i, h, g):
                    pe.wait_ge(mixed, g + 1)
                    for n, at_turn in enumerate(TURNS[i]):
                        bank, before = bank_use(h, at_turn)
                        pe.wait_ge(t_kept[bank], before + 1)
                        for j in blocks(i, n):
                            mm = pe.transpose(t_ps[:, bank, (j % 4) * P:(j % 4 + 1) * P], pr[:, i % 2, 0, j * P:(j + 1) * P],
                                              c.ident[:])
                        mm.then_inc(turned[bank], 1)

                def weigh(s, i, g):
                    pe.wait_ge(at_ready, g + 1)
                    for j in range(i + 1):
                        mm = pe.matmul(o_ps[:, i % 2, 0:VD], at[:, i % 2, j * P:(j + 1) * P], v[:, s, j, :], start=(j == 0), stop=(j == i))
                    mm.then_inc(pv_done, 1)

                def turn_out(h, s, turns=TURNS["out"]):
                    pe.wait_ge(normed, h)
                    for n, at_turn in enumerate(turns):
                        bank, before = bank_use(h, at_turn)
                        pe.wait_ge(t_kept[bank], before + 1)
                        for j in range(4):
                            mm = pe.transpose(t_ps[:, bank, j * P:(j + 1) * P], o[:, s, 4 * n + j, :], c.ident[:])
                        mm.then_inc(turned[bank], 1)

                def body(it, first):
                    for s in range(2):
                        h = 2 * it + s
                        start = first and s == 0
                        pe.wait_ge(head_loaded[s], 48 * (it + 1))
                        for i in range(QT):
                            g = h * QT + i
                            scores(s, i, g)
                            if not (start and i < 2):
                                weigh(s if i >= 2 else 1 - s, (i - 2) % QT, g - 2)
                            if i == 1 and not start:
                                pe.wait_ge(pv_done, g - 1)
                                pe.sem_inc(head_used[1 - s], 1)
                            if not (start and i == 0):
                                turn((i - 1) % QT, h, g - 1)
                            if i == OUT_STEP and not start:
                                turn_out(h, 1 - s)

                pe.wait_ge(mask_step, 4)
                pair(body, pe)
                n = HEADS * QT
                weigh(1, QT - 2, n - 2)
                turn(QT - 1, HEADS, n - 1)
                weigh(1, QT - 1, n - 1)
                turn_out(HEADS, 1, TURNS["last out"])

            @block.vector
            def _(dve):
                def bias(i, g):
                    for m in range(2):
                        dve.wait_ge(scores_done[m], g + 1)
                        dve.tensor_reduce(nb[:, i % 2, m:m + 1], s_ps[:, m, 0:P * (i + 1)], AX.X, ALU.max,
                                          negate=True).then_inc(bias_ready[m], 1)

                def mix(i, g, kept):
                    w, s = P * (i + 1), i % 2
                    if kept:
                        dve.wait_ge(o_kept, g - 1)
                    for m in range(2):
                        dve.wait_ge(exp_done[m], g + 2)
                    dve.reciprocal(rl[:, s, :], l[:, s, :]).then_inc(step, 1)
                    dve.wait_ge(step, STEPS * g + 1)
                    dve.tensor_scalar(cf[:], rl[:, s, 1:2], l[:, s, 0:1], c.neglam[:], ALU.mult, ALU.mult).then_inc(step, 1)
                    dve.wait_ge(step, STEPS * g + 2)
                    dve.scalar_tensor_tensor(pr[:, s, 0, 0:w], pr[:, s, 1, 0:w], cf[:], pr[:, s, 0, 0:w], ALU.mult, ALU.add).then_inc(mixed, 1)

                def keep_o(i, g, s, turned_out=None):
                    dve.wait_ge(pv_done, g + 1)
                    if turned_out is not None:
                        dve.wait_ge(out_done, turned_out)
                    dve.tensor_scalar(o[:, s, i, :], o_ps[:, i % 2, 0:VD], rl[:, i % 2, 0:1], None, ALU.mult).then_inc(o_kept, 1)

                def sums(h):
                    dve.wait_ge(squared, h)
                    dve.tensor_reduce(ssq[:], square, AX.X, ALU.add).then_inc(sums_ready, 1)

                def inverse(h):
                    dve.wait_ge(root_ready, h)
                    dve.reciprocal(rstd[:], ssq[:]).then_inc(rstd_ready, 1)

                def out_lo(h, turns=TURNS["out"]):
                    for n, at_turn in enumerate(turns):
                        bank, _ = bank_use(0, at_turn)
                        part = slice(n * 512, (n + 1) * 512)
                        dve.wait_ge(out_hi, 2 * h - 1 + n)
                        dve.tensor_tensor(o_lo[:, ds(h - 1, 1), part].rearrange("p a b -> p (a b)"), t_ps[:, bank, :],
                                          o_hi[:, ds(h - 1, 1), part].rearrange("p a b -> p (a b)"), ALU.subtract).then_inc(t_kept[bank], 1)

                def body(it, first):
                    for s in range(2):
                        h = 2 * it + s
                        start = first and s == 0
                        for i in range(QT):
                            g = h * QT + i
                            bias(i, g)
                            if not (start and i < 2):
                                keep_o((i - 2) % QT, g - 2, s if i >= 2 else 1 - s, h - 1 if i == 2 and not first else None)
                            if i == OUT_STEP and not start:
                                inverse(h)
                            mix(i, g, not (start and i < 2))
                            if not start:
                                if i == 2:
                                    sums(h)
                                if i == OUT_STEP + 1:
                                    out_lo(h)

                pair(body, dve)
                n = HEADS * QT
                keep_o(QT - 2, n - 2, 1)
                keep_o(QT - 1, n - 1, 1)
                sums(HEADS)
                inverse(HEADS)
                out_lo(HEADS, TURNS["last out"])

            @block.scalar
            def _(act):
                def exponentials(i, g):
                    w, s = P * (i + 1), i % 2
                    for m in range(2):
                        act.wait_ge(bias_ready[m], g + 1)
                        act.activation(pr[:, s, m, 0:w], s_ps[:, m, 0:w], ACT.Exp, bias=nb[:, s, m:m + 1],
                                       accum_out=l[:, s, m:m + 1]).then_inc(exp_done[m], 1)

                def keep_at(i, h):
                    for n, at_turn in enumerate(TURNS[i]):
                        bank, before = bank_use(h, at_turn)
                        act.wait_ge(turned[bank], before + 1)
                        w = P * len(blocks(i, n))
                        act.activation(at[:, i % 2, n * 512:n * 512 + w], t_ps[:, bank, 0:w], ACT.Copy).then_inc(t_kept[bank], 1)
                    act.wait_ge(t_kept[bank], before + 2)
                    act.sem_inc(at_ready, 1)

                def root(h):
                    act.wait_ge(sums_ready, h)
                    act.activation(ssq[:], ssq[:], ACT.Sqrt, bias=c.eps[:], scale=1.0 / VD).then_inc(root_ready, 1)

                def keep_out(h, turns=TURNS["out"]):
                    for n, at_turn in enumerate(turns):
                        bank, before = bank_use(h, at_turn)
                        act.wait_ge(turned[bank], before + 1)
                        act.activation(o_hi[:, ds(h - 1, 1), n * 512:(n + 1) * 512].rearrange("p a b -> p (a b)"),
                                       t_ps[:, bank, :], ACT.Copy).then_inc(out_hi, 1)
                    act.wait_ge(out_hi, 2 * h)
                    act.sem_inc(out_done, 1)

                def body(it, first):
                    for s in range(2):
                        h = 2 * it + s
                        start = first and s == 0
                        for i in range(QT):
                            g = h * QT + i
                            exponentials(i, g)
                            if not (start and i == 0):
                                keep_at((i - 1) % QT, h)
                            if not start:
                                if i == 2:
                                    root(h)
                                if i == OUT_STEP:
                                    keep_out(h)

                pair(body, act)
                keep_at(QT - 1, HEADS)
                root(HEADS)
                keep_out(HEADS, TURNS["last out"])


def phase_decode(c, o_hi, o_lo):
    nc, io, sem = c.nc, c.io, c.sem
    HG = 4
    KEYS = PAST + NEW
    PT = PAST // P
    with ExitStack() as mem:
        def sb(name, shape, dt=F32):
            return mem.enter_context(nc.sbuf_tensor(name, shape, dt))

        k = sb("d_k", [P, PT, DC])
        v = sb("d_v", [P, PT, DC])
        vn = sb("d_vn", [NEW, DC])
        kT = sb("d_kT", [P, HEADS, KEYS])
        qs = sb("d_q", [P, HEADS, P])
        qx = sb("d_qx", [P, HG, P])
        pr = sb("d_pr", [P, KEYS])
        mixer, mixl = sb("d_mixer", [P, HG * NEW]), sb("d_mixl", [P, HG * NEW])
        at = sb("d_at", [P, PT + 1, HG * NEW])
        orow = sb("d_orow", [NEW, DC])
        nb, l, rl = (sb(f"d_{n}", [P, 1]) for n in ("nb", "l", "rl"))
        ssq, rstd = sb("d_ssq", [P, HEADS]), sb("d_rstd", [P, HEADS])
        o = k[:, 0, :].rearrange("p (a b) -> p a b", a=HEADS)
        square = k[:, 1, :].rearrange("p (a b) -> p a b", a=HEADS)
        t_ps = mem.enter_context(nc.psum_tensor("d_t", [P, 2, 512], F32))
        s_ps = mem.enter_context(nc.psum_tensor("d_s", [P, 1024], F32))
        at_ps = mem.enter_context(nc.psum_tensor("d_at_ps", [P, 512], F32))
        o_ps = mem.enter_context(nc.psum_tensor("d_o_ps", [P, 512], F32))
        k_loaded, v_loaded, kn_loaded, q_loaded = sem("d_k_loaded"), sem("d_v_loaded"), sem("d_kn_loaded"), sem("d_q_loaded")
        k_turned, kT_ready = sem("d_k_turned"), c.sems("d_kT_ready", 2)
        qx_zeroed, qx_ready, mixer_step = sem("d_qx_zeroed"), sem("d_qx_ready"), sem("d_mixer_step")
        scores_done, step, exp_done, mixl_ready = sem("d_scores_done"), sem("d_step"), sem("d_exp_done"), sem("d_mixl_ready")
        at_done, at_kept, o_done, o_kept, o_stored = sem("d_at_done"), sem("d_at_kept"), sem("d_o_done"), sem("d_o_kept"), sem("d_o_stored")
        bias_ready = sem("d_bias_ready")
        o_loaded, nstep, root_ready, normed = sem("d_o_loaded"), sem("d_nstep"), sem("d_root_ready"), sem("d_normed")
        o_turned, hi_kept, lo_kept = sem("d_o_turned"), sem("d_hi_kept"), sem("d_lo_kept")
        G = HEADS // HG

        with nc.Block() as block:

            @block.sync
            def _(sp):
                sp.dma_start(qs[:], io.chunks[CH:2 * CH, :, PROMPT:TOK].rearrange("h p n -> p h n")).then_inc(q_loaded, 16)
                with sp.Fori(0, STREAMS) as b:
                    sp.wait_ge(k_turned, HEADS * b + 1)
                    sp.dma_start(k[:], io.cache_k[ds(b, 1), :, :].rearrange("a (t p) n -> p (a t) n", p=P)).then_inc(k_loaded, 16)
                    sp.wait_ge(scores_done, G * b + 1)
                    sp.dma_start(kT[:, :, PAST:KEYS], io.chunks[2 * CH:3 * CH, :, ds(b * NEW + PROMPT, NEW)].rearrange(
                        "h p n -> p h n")).then_inc(kn_loaded, 16)
                    sp.wait_ge(o_done, G * b + 1)
                    sp.dma_start(v[:], io.cache_v[ds(b, 1), :, :].rearrange("a (t p) n -> p (a t) n", p=P)).then_inc(v_loaded, 16)
                    sp.dma_start(vn[:], io.v_all[ds(b * NEW + PROMPT, NEW), :]).then_inc(v_loaded, 16)
                sp.wait_ge(o_stored, 16 * STREAMS + 1)
                sp.dma_start(k[:, 0, :], io.o_new).then_inc(o_loaded, 16)

            @block.gpsimd
            def _(pool):
                pool.memset(qx[:], 0.0).then_inc(qx_zeroed, 1)

            @block.tensor
            def _(pe):
                c.start_at_one(pe, k_turned, scores_done, o_done, *kT_ready, exp_done, at_kept, o_kept, at_done, o_stored)
                with pe.Fori(0, STREAMS) as b:
                    pe.wait_ge(k_loaded, 16 * (b + 1))
                    for h in range(HEADS):
                        pe.wait_ge(kT_ready[h % 2], b * (HEADS // 2) + h // 2 + 1)
                        for t in range(PT):
                            mm = pe.transpose(t_ps[:, h % 2, t * P:(t + 1) * P], k[:, t, h * VD:(h + 1) * VD], c.ident[:])
                        mm.then_inc(k_turned, 1)
                    for hg in range(G):
                        n = b * G + hg
                        pe.wait_ge(qx_ready, n + 1)
                        pe.wait_ge(exp_done, n + 1)
                        if hg == 0:
                            pe.wait_ge(kT_ready[0], b * (HEADS // 2) + HEADS // 2 + 1)
                            pe.wait_ge(kT_ready[1], b * (HEADS // 2) + HEADS // 2 + 1)
                            pe.wait_ge(kn_loaded, 16 * (b + 1))
                        for j in range(HG):
                            pe.matmul(s_ps[:, 0:PAST], qx[:, j, :], kT[:, hg * HG + j, 0:PAST], start=(j == 0), stop=(j == HG - 1))
                        for j in range(HG):
                            mm = pe.matmul(s_ps[:, PAST:KEYS], qx[:, j, :], kT[:, hg * HG + j, PAST:KEYS], start=(j == 0), stop=(j == HG - 1))
                        mm.then_inc(scores_done, 1)
                        pe.wait_ge(mixl_ready, n + 1)
                        pe.wait_ge(at_kept, n + 1)
                        for t in range(PT + 1):
                            w = min(P, KEYS - t * P)
                            mm = pe.matmul(at_ps[0:w, t * HG * NEW:(t + 1) * HG * NEW], pr[:, t * P:t * P + w], mixl[:],
                                           start=True, stop=True)
                        mm.then_inc(at_done, 1)
                        pe.wait_ge(at_kept, n + 2)
                        pe.wait_ge(o_kept, n + 1)
                        if hg == 0:
                            pe.wait_ge(v_loaded, 32 * (b + 1))
                        for j in range(HG):
                            cols = slice((hg * HG + j) * VD, (hg * HG + j + 1) * VD)
                            for t in range(PT + 1):
                                w = min(P, KEYS - t * P)
                                rhs = v[:, t, cols] if t < PT else vn[:, cols]
                                mm = pe.matmul(o_ps[0:NEW, j * VD:(j + 1) * VD], at[0:w, t, j * NEW:(j + 1) * NEW], rhs,
                                               start=(t == 0), stop=(t == PT))
                        mm.then_inc(o_done, 1)
                pe.wait_ge(normed, 1)
                for h in range(HEADS):
                    mm = pe.transpose(s_ps[:, h * P:(h + 1) * P], o[:, h, :], c.ident[:])
                mm.then_inc(o_turned, 1)

            @block.vector
            def _(dve):
                idv = c.ident[:].rearrange("p (h m q) -> p h m q", h=HG, m=2)
                mv = mixer[:].rearrange("p (h q) -> p h q", h=HG)
                dve.tensor_scalar(mv, idv[:, :, 1, :], c.neglam[:], None, ALU.mult).then_inc(mixer_step, 1)
                dve.wait_ge(mixer_step, 1)
                dve.tensor_tensor(mv, mv, idv[:, :, 0, :], ALU.add).then_inc(mixer_step, 1)
                dve.wait_ge(mixer_step, 2)
                dve.wait_ge(qx_zeroed, 1)
                dve.wait_ge(q_loaded, 16)
                qv = qx[:].rearrange("p h (g m q) -> p h g m q", g=HG, m=2)

                def spread_queries(b, hg, n):
                    dve.wait_ge(scores_done, n + 1)
                    for j in range(HG):
                        for m in range(2):
                            part = slice(m * DH, (m + 1) * DH)
                            cp = dve.tensor_copy(qx[part, j, (2 * j + m) * NEW:(2 * j + m + 1) * NEW],
                                                 qs[part, hg * HG + j, ds(b * NEW, NEW)])
                    cp.then_inc(qx_ready, 1)

                with dve.Fori(0, STREAMS) as b:
                    spread_queries(b, 0, b * G)
                    for h in range(1, HEADS, 2):
                        dve.wait_ge(k_turned, b * HEADS + h + 2)
                        if h == 1:
                            dve.wait_ge(scores_done, b * G + 1)
                        dve.tensor_copy(kT[:, h, 0:PAST], t_ps[:, 1, :]).then_inc(kT_ready[1], 1)
                    for hg in range(G):
                        n = b * G + hg
                        dve.wait_ge(scores_done, n + 2)
                        dve.tensor_reduce(nb[:], s_ps[:, 0:KEYS], AX.X, ALU.max, negate=True).then_inc(bias_ready, 1)
                        if hg == 0:
                            spread_queries(b, 1, n + 1)
                        dve.wait_ge(exp_done, n + 2)
                        dve.reciprocal(rl[:], l[:]).then_inc(step, 1)
                        dve.wait_ge(step, n + 1)
                        dve.tensor_scalar(mixl[:], mixer[:], rl[:], None, ALU.mult).then_inc(mixl_ready, 1)
                        dve.wait_ge(at_done, n + 2)
                        w = PT * HG * NEW
                        dve.tensor_copy(at[:, 0:PT, :].rearrange("p a b -> p (a b)"), at_ps[:, 0:w])
                        dve.tensor_copy(at[0:NEW, PT, :], at_ps[0:NEW, w:w + HG * NEW]).then_inc(at_kept, 1)
                dve.wait_ge(o_loaded, 16)
                norm_sums(c, dve, o, square, ssq, nstep, 0)
                head_norm(c, dve, o, square, ssq, rstd, nstep, 0, root_ready)
                dve.tensor_tensor(o[:], o[:], c.hn[:].unsqueeze(1).to_broadcast([P, HEADS, VD]), ALU.mult).then_inc(normed, 1)
                dve.wait_ge(hi_kept, 1)
                dve.tensor_tensor(o_lo[:, :, PROMPT:TOK], s_ps[:].rearrange("p (h n) -> p h n", h=HEADS),
                                  o_hi[:, :, PROMPT:TOK], ALU.subtract).then_inc(lo_kept, 1)
                dve.wait_ge(lo_kept, 1)

            @block.scalar
            def _(act):
                with act.Fori(0, STREAMS) as b:
                    for h in range(0, HEADS, 2):
                        act.wait_ge(k_turned, b * HEADS + h + 2)
                        if h == 0:
                            act.wait_ge(scores_done, b * G + 1)
                        act.activation(kT[:, h, 0:PAST], t_ps[:, 0, :], ACT.Copy).then_inc(kT_ready[0], 1)
                    for hg in range(G):
                        n = b * G + hg
                        act.wait_ge(bias_ready, n + 1)
                        act.wait_ge(at_done, n + 1)
                        act.activation(pr[:], s_ps[:, 0:KEYS], ACT.Exp, bias=nb[:], accum_out=l[:]).then_inc(exp_done, 1)
                        act.wait_ge(o_done, n + 2)
                        if hg == 0:
                            act.wait_ge(o_stored, 16 * b + 1)
                        act.activation(orow[:, hg * 512:(hg + 1) * 512], o_ps[0:NEW, :], ACT.Copy).then_inc(o_kept, 1)
                    act.wait_ge(o_kept, G * (b + 1) + 1)
                    act.dma_start(io.o_new[ds(b * NEW, NEW), :], orow[:]).then_inc(o_stored, 16)
                act.wait_ge(nstep, 2)
                act.activation(ssq[:], ssq[:], ACT.Sqrt, bias=c.eps[:], scale=1.0 / VD).then_inc(root_ready, 1)
                act.wait_ge(o_turned, 1)
                act.activation(o_hi[:, :, PROMPT:TOK], s_ps[:].rearrange("p (h n) -> p h n", h=HEADS), ACT.Copy).then_inc(hi_kept, 1)


def phase_mix_out(c, a_hi, a_lo, o_hi, o_lo):
    nc, io, sem = c.nc, c.io, c.sem
    with ExitStack() as mem:
        def sb(name, shape, dt=F32):
            return mem.enter_context(nc.sbuf_tensor(name, shape, dt))

        w_raw = sb("m_w_raw", [P, KT, P])
        w_hi = sb("m_w_hi", [P, KT, P], F32R)
        w_lo = sb("m_w_lo", [P, KT, P], F32R)
        e = sb("m_e", [P, TOK])
        x = sb("m_x", [P, NT, P])
        rows = sb("m_rows", [P, NT, P])
        z = mem.enter_context(nc.psum_tensor("m_z", [P, NB, 512], F32))
        tp = mem.enter_context(nc.psum_tensor("m_tp", [P, NB, 512], F32))
        load, split_chunk, products, z_done, z_kept, first_counts = weight_chunks(c, "m", w_raw, w_hi, w_lo)
        e_ready, e_turned = sem("m_e_ready"), sem("m_e_turned")
        x_loaded, rows_ready, rows_stored = sem("m_x_loaded"), sem("m_rows_ready"), sem("m_rows_stored")
        w = io.w_out.rearrange("(h k p) n -> h p k n", h=2, p=P)
        x_cols = io.x.rearrange("(t p) n -> p t n", p=P)
        x1_cols = io.x1.rearrange("(t p) n -> p t n", p=P)

        with nc.Block() as block:

            @block.sync
            def _(sp):
                with sp.Fori(0, KT) as n:
                    load(sp, n, lambda half: w[half, :, :, ds(n * P, P)])

            @block.gpsimd
            def _(pool):
                with pool.Fori(0, KT) as n:
                    split_chunk(pool, n)

            @block.tensor
            def _(pe):
                c.start_at_one(pe, *first_counts, rows_stored, rows_ready)
                def turn_back(m):
                    pe.wait_ge(e_ready, m + 1)
                    pe.wait_ge(rows_ready, m + 1)
                    for b in range(NB):
                        for j in range(NB):
                            mm = pe.transpose(tp[:, b, j * P:(j + 1) * P], e[:, (b * NB + j) * P:(b * NB + j + 1) * P],
                                              c.ident[:])
                        mm.then_inc(e_turned, 1)

                products(pe, 0, 0, z, a_hi, a_lo)
                products(pe, 0, 1, z, o_hi, o_lo)
                with pe.Fori(1, KT) as n:
                    products(pe, n, 0, z, a_hi, a_lo)
                    turn_back(n - 1)
                    products(pe, n, 1, z, o_hi, o_lo)
                turn_back(KT - 1)

            @block.vector
            def _(dve):
                def keep_e(n):
                    for b in range(NB):
                        dve.wait_ge(z_done[b], n + 2)
                        dve.tensor_copy(e[:, b * BLK:(b + 1) * BLK], z[:, b, 0:BLK]).then_inc(z_kept[b], 1)
                    dve.wait_ge(z_kept[2], n + 2)
                    dve.sem_inc(e_ready, 1)

                def add_rows(m):
                    dve.wait_ge(x_loaded, 16 * (m + 1))
                    dve.wait_ge(rows_stored, 16 * m + 1)
                    for b in range(NB):
                        dve.wait_ge(e_turned, NB * m + b + 1)
                        add = dve.tensor_tensor(rows[:, b * NB:(b + 1) * NB, :],
                                                tp[:, b, 0:NB * P].rearrange("p (a q) -> p a q", a=NB),
                                                x[:, b * NB:(b + 1) * NB, :], ALU.add)
                    add.then_inc(rows_ready, 1)

                keep_e(0)
                with dve.Fori(1, KT) as n:
                    add_rows(n - 1)
                    keep_e(n)
                add_rows(KT - 1)

            @block.scalar
            def _(act):
                with act.Fori(0, KT) as n:
                    act.wait_ge(rows_ready, n + 1)
                    act.dma_start(x[:], x_cols[:, :, ds(n * P, P)]).then_inc(x_loaded, 16)
                    act.wait_ge(rows_ready, n + 2)
                    act.dma_start(x1_cols[:, :, ds(n * P, P)], rows[:]).then_inc(rows_stored, 16)
                act.wait_ge(rows_stored, 16 * KT + 1)


def phase_route(c):
    nc, io, sem = c.nc, c.io, c.sem
    SL = 3
    NP = TOPK * NT
    with ExitStack() as mem:
        def sb(name, shape, dt=F32):
            return mem.enter_context(nc.sbuf_tensor(name, shape, dt))

        x = sb("r_x", [P, SL, D])
        g = sb("r_g", [P, D])
        xT = sb("r_xT", [P, KT, P])
        wr = sb("r_w", [P, KT, NR])
        br = sb("r_b", [P, NR])
        ssq, rstd = sb("r_ssq", [P, SL]), sb("r_rstd", [P, SL])
        junk = sb("r_junk", [P, D])
        lg = sb("r_lg", [P, NT, NR])
        tri, ones = sb("r_tri", [P, P]), sb("r_ones", [P, P])
        ints = sb("r_ints", [P, 64], I32)
        nums = sb("r_nums", [P, 64])
        thr_i, thr = sb("r_thr_i", [P, NT], I32), sb("r_thr", [P, NT])
        gm, gs, m1, m2, e1, e2, ex, wsum = (sb(f"r_{n}", [P, NT]) for n in ("gm", "gs", "m1", "m2", "e1", "e2", "ex", "wsum"))
        d4, x4, oh4 = (sb(f"r_{n}", [P, NT, GROUPS]) for n in ("d4", "x4", "oh4"))
        le, eq, oh1, oh2, both, carry, place = (sb(f"r_{n}", [P, NT, EXPERTS]) for n in ("le", "eq", "oh1", "oh2", "both", "carry", "place"))
        count, groups, end, start = (sb(f"r_{n}", [P, EXPERTS]) for n in ("count", "groups", "end", "start"))
        over = sb("r_over", [P, EXPERTS, NT])
        pos_f, pos = sb("r_pos_f", [P, NP]), sb("r_pos", [P, NP], U32)
        rows = sb("r_rows", [P, NP, 4], I32)
        empty = sb("r_empty", [P, 2 * SLOT_GROUPS, 4], I32)
        done_by, begun = (sb(f"r_{n}", [1, SLOT_GROUPS, EXPERTS]) for n in ("done_by", "begun"))
        first_slot, second_slots, group_f, paired = (sb(f"r_{n}", [1, SLOT_GROUPS]) for n in ("first_slot", "second_slots", "group_f", "paired"))
        slots_end = sb("r_slots_end", [1, EXPERTS])
        tp = mem.enter_context(nc.psum_tensor("r_tp", [P, 4, 512], F32))
        lg_ps = mem.enter_context(nc.psum_tensor("r_lg_ps", [P, 512], F32))
        cum_ps = mem.enter_context(nc.psum_tensor("r_cum", [P, 2, 512], F32))
        x_loaded, x_turned, h_stored = c.sems("r_x_loaded", SL), c.sems("r_x_turned", SL), c.sems("r_h_stored", SL)
        params, squared, root_done, rstd_done = sem("r_params"), sem("r_squared"), sem("r_root_done"), sem("r_rstd_done")
        h_ready, turned, kept_a, kept_v = sem("r_h_ready"), sem("r_turned"), sem("r_kept_a"), sem("r_kept_v")
        logits_done, logits_kept = sem("r_logits_done"), sem("r_logits_kept")
        consts, step, gaps_ready, exps_done = sem("r_consts"), sem("r_step"), sem("r_gaps_ready"), sem("r_exps_done")
        chosen, summed = sem("r_chosen"), sem("r_summed")
        emptied, slots_ready, slots_stored = sem("r_emptied"), sem("r_slots_ready"), sem("r_slots_stored")

        with nc.Block() as block:

            @block.sync
            def _(sp):
                sp.dma_start(g[:], io.norm_ffn.to_broadcast([P, D])).then_inc(params, 16)
                sp.dma_start(wr[:], io.w_router.rearrange("(k p) n -> p k n", p=P)).then_inc(params, 16)
                sp.dma_start(br[:], io.b_router.to_broadcast([P, NR])).then_inc(params, 16)
                with sp.Fori(0, NT // SL) as i:
                    for s in range(SL):
                        sp.wait_ge(x_turned[s], i + 1)
                        c.hold(sp)
                        sp.wait_ge(h_stored[s], 16 * i + 1)
                        c.hold(sp)
                        sp.dma_start(x[:, s, :], io.x1[ds((i * SL + s) * P, P), :]).then_inc(x_loaded[s], 16)

            @block.gpsimd
            def _(pool):
                pool.memset(tri[:], 1.0).then_inc(consts, 1)
                pool.memset(ones[:], 1.0).then_inc(consts, 1)
                pool.memset(empty[:], 0).then_inc(consts, 1)
                pool.memset(rows[:], 0).then_inc(consts, 1)
                pool.iota(ints[:], pattern=[[1, 64]], base=0, channel_multiplier=0).then_inc(consts, 1)
                pool.iota(thr_i[:], pattern=[[GROUP, NT]], base=0, channel_multiplier=0).then_inc(consts, 1)
                pool.wait_ge(consts, 6)
                pool.affine_select(out=tri[:], in_=tri[:], compare_op=ALU.is_gt, fill=0.0, base=0, pattern=[[1, P]],
                                   channel_multiplier=-1).then_inc(consts, 1)
                pool.memset(empty[:, :, 0:2], NO_ROW).then_inc(consts, 1)
                for k in range(TOPK):
                    pool.iota(rows[:, k * NT:(k + 1) * NT, 0], pattern=[[P, NT]], base=0, channel_multiplier=1).then_inc(consts, 1)
                    pool.iota(rows[:, k * NT:(k + 1) * NT, 1], pattern=[[P, NT]], base=k * TOK, channel_multiplier=1).then_inc(consts, 1)
                pool.wait_ge(consts, 12)
                pool.dma_start(io.slots.rearrange("(p t) f -> p (t f)", p=P), empty[:].rearrange("p t f -> p (t f)")).then_inc(emptied, 16)
                pool.wait_ge(emptied, 16)
                pool.wait_ge(slots_ready, 1)
                for n in range(NP):
                    pool.indirect_dma_start(out=io.slots, out_offset=bass.IndirectOffsetOnAxis(ap=pos[:, n:n + 1], axis=0),
                                            in_=rows[:, n, :], in_offset=None).then_inc(slots_stored, 16)
                pool.wait_ge(slots_stored, 16 * NP)

            @block.scalar
            def _(act):
                def root(s, t):
                    act.activation(junk[:], x[:, s, :], ACT.Square, accum_out=ssq[:, s:s + 1]).then_inc(squared, 1)
                    act.wait_ge(squared, t + 1)
                    act.activation(ssq[:, s:s + 1], ssq[:, s:s + 1], ACT.Sqrt, bias=c.eps[:], scale=1.0 / D).then_inc(root_done, 1)

                with act.Fori(0, NT // SL) as i:
                    for s in range(SL):
                        t = i * SL + s
                        act.wait_ge(x_loaded[s], 16 * (i + 1))
                        act.wait_ge(rstd_done, t + 1)
                        root(s, t)
                        act.wait_ge(h_ready, t + 1)
                        act.dma_start(io.h2[ds(t * P, P), :], x[:, s, :]).then_inc(h_stored[s], 16)
                        for q in (0, 2):
                            act.wait_ge(turned, 4 * t + q + 1)
                            act.activation(xT[:, 4 * q:4 * q + 4, :], tp[:, q, :].rearrange("p (a b) -> p a b", a=4),
                                           ACT.Copy).then_inc(kept_a, 1)
                act.wait_ge(gaps_ready, 1)
                act.activation(x4[:], d4[:], ACT.Exp).then_inc(exps_done, 1)
                act.wait_ge(gaps_ready, 2)
                act.activation(ex[:], wsum[:], ACT.Exp).then_inc(exps_done, 1)
                for s in range(SL):
                    act.wait_ge(h_stored[s], 16 * (NT // SL) + 1)

            @block.tensor
            def _(pe):
                c.start_at_one(pe, *x_turned, *h_stored, rstd_done, logits_kept)
                pe.wait_ge(params, 48)
                with pe.Fori(0, NT // SL) as i:
                    for s in range(SL):
                        t = i * SL + s
                        pe.wait_ge(h_ready, t + 1)
                        for q in range(4):
                            for j in range(4):
                                k = 4 * q + j
                                mm = pe.transpose(tp[:, q, j * P:(j + 1) * P], x[:, s, k * P:(k + 1) * P], c.ident[:])
                            mm.then_inc(turned, 1)
                        pe.wait_ge(turned, 4 * t + 4)
                        pe.sem_inc(x_turned[s], 1)
                        pe.wait_ge(kept_a, 2 * t + 2)
                        pe.wait_ge(kept_v, 2 * t + 2)
                        pe.wait_ge(logits_kept, t + 1)
                        for k in range(KT):
                            mm = pe.matmul(lg_ps[:, 0:NR], xT[:, k, :], wr[:, k, :], start=(k == 0), stop=(k == KT - 1))
                        mm.then_inc(logits_done, 1)
                pe.wait_ge(chosen, 1)
                pe.wait_ge(consts, 7)
                n = NT * EXPERTS
                pe.matmul(cum_ps[:, 0, 0:n], tri[:], both[:].rearrange("p t e -> p (t e)"), start=True, stop=True)
                pe.matmul(cum_ps[:, 1, 0:n], ones[:], both[:].rearrange("p t e -> p (t e)"), start=True, stop=True).then_inc(summed, 1)

            @block.vector
            def _(dve):
                dve.wait_ge(params, 48)
                with dve.Fori(0, NT // SL) as i:
                    for s in range(SL):
                        t = i * SL + s
                        dve.wait_ge(root_done, t + 1)
                        dve.reciprocal(rstd[:, s:s + 1], ssq[:, s:s + 1]).then_inc(rstd_done, 1)
                        dve.wait_ge(rstd_done, t + 2)
                        dve.scalar_tensor_tensor(x[:, s, :], x[:, s, :], rstd[:, s:s + 1], g[:], ALU.mult, ALU.mult).then_inc(h_ready, 1)
                        for q in (1, 3):
                            dve.wait_ge(turned, 4 * t + q + 1)
                            dve.tensor_copy(xT[:, 4 * q:4 * q + 4, :], tp[:, q, :].rearrange("p (a b) -> p a b", a=4)).then_inc(kept_v, 1)
                        dve.wait_ge(logits_done, t + 1)
                        dve.tensor_tensor(lg[:, ds(t, 1), :].rearrange("p a b -> p (a b)"), lg_ps[:, 0:NR], br[:], ALU.add).then_inc(logits_kept, 1)

                steps = [0]

                def then(ins):
                    steps[0] += 1
                    ins.then_inc(step, 1)
                    dve.wait_ge(step, steps[0])

                def tt(out, a, b, op):
                    then(dve.tensor_tensor(out, a, b, op))

                def over_last(v, n):
                    return v.unsqueeze(2).to_broadcast([P, NT, n])

                def over_tiles(v, n):
                    return v.unsqueeze(1).to_broadcast([P, NT, n])

                dve.wait_ge(logits_kept, NT + 1)
                dve.wait_ge(consts, 12)
                then(dve.tensor_copy(nums[:], ints[:]))
                then(dve.tensor_copy(thr[:], thr_i[:]))
                e_no = nums[:, 0:EXPERTS]

                def first_best(best, index, onehot, scores, n):
                    then(dve.tensor_reduce(best, scores, AX.X, ALU.max))
                    tt(onehot, scores, over_last(best, n), ALU.is_equal)
                    then(dve.tensor_scalar(onehot, onehot, -64.0, 64.0, ALU.mult, ALU.add))
                    tt(onehot, onehot, over_tiles(e_no[:, 0:n], n), ALU.add)
                    then(dve.tensor_reduce(index, onehot, AX.X, ALU.min))
                    tt(onehot, over_tiles(e_no[:, 0:n], n), over_last(index, n), ALU.is_equal)

                first_best(gm[:], e1[:], oh4[:], lg[:, :, 0:GROUPS], GROUPS)
                dve.tensor_tensor(d4[:], lg[:, :, 0:GROUPS], over_last(gm[:], GROUPS), ALU.subtract).then_inc(gaps_ready, 1)
                then(dve.tensor_scalar(oh4[:], oh4[:], -1.0, BIG, ALU.add, ALU.mult))
                tt(le[:].rearrange("p t (g e) -> p t g e", g=GROUPS), lg[:, :, GROUPS:NR].rearrange("p t (g e) -> p t g e", g=GROUPS),
                   oh4[:].unsqueeze(3).to_broadcast([P, NT, GROUPS, PER]), ALU.add)
                first_best(m1[:], e1[:], oh1[:], le[:], EXPERTS)
                then(dve.scalar_tensor_tensor(le[:], oh1[:], -2 * BIG, le[:], ALU.mult, ALU.add))
                first_best(m2[:], e2[:], oh2[:], le[:], EXPERTS)
                dve.tensor_tensor(wsum[:], m2[:], m1[:], ALU.subtract).then_inc(gaps_ready, 1)
                dve.tensor_tensor(both[:], oh1[:], oh2[:], ALU.add).then_inc(chosen, 1)
                dve.wait_ge(exps_done, 2)
                then(dve.tensor_reduce(gs[:], x4[:], AX.X, ALU.add))
                then(dve.tensor_scalar(wsum[:], ex[:], 1.0, None, ALU.add))
                tt(gs[:], gs[:], wsum[:], ALU.mult)
                wv = rows[:].bitcast(F32)
                then(dve.reciprocal(gs[:], gs[:]))
                then(dve.tensor_copy(wv[:, 0:NT, 2], gs[:]))
                tt(wv[:, NT:NP, 2], gs[:], ex[:], ALU.mult)
                dve.wait_ge(summed, 1)
                before = cum_ps[:, 0, 0:NT * EXPERTS].rearrange("p (t e) -> p t e", t=NT)
                total = cum_ps[:, 1, 0:NT * EXPERTS].rearrange("p (t e) -> p t e", t=NT)
                then(dve.memset(carry[:, 0, :], 0.0))
                for t in range(1, NT):
                    tt(carry[:, t, :], carry[:, t - 1, :], total[:, t - 1, :], ALU.add)
                tt(count[:], carry[:, NT - 1, :], total[:, NT - 1, :], ALU.add)
                tt(over[:], count[:].unsqueeze(2).to_broadcast([P, EXPERTS, NT]), thr[:].unsqueeze(1).to_broadcast([P, EXPERTS, NT]), ALU.is_gt)
                then(dve.tensor_reduce(groups[:], over[:], AX.X, ALU.add))
                then(dve.tensor_tensor_scan(end[:], ones[:, 0:EXPERTS], groups[:], 0.0, ALU.mult, ALU.add))
                tt(start[:], end[:], groups[:], ALU.subtract)
                then(dve.tensor_scalar(start[:], start[:], float(GROUP), None, ALU.mult))
                tt(place[:], carry[:], before, ALU.add)
                tt(place[:], place[:], over_tiles(start[:], EXPERTS), ALU.add)
                tt(eq[:], place[:], oh1[:], ALU.mult)
                then(dve.tensor_reduce(pos_f[:, 0:NT], eq[:], AX.X, ALU.add))
                tt(eq[:], place[:], oh2[:], ALU.mult)
                then(dve.tensor_reduce(pos_f[:, NT:NP], eq[:], AX.X, ALU.add))
                dve.tensor_copy(pos[:], pos_f[:]).then_inc(slots_ready, 1)
                def by_group(v):
                    return v.unsqueeze(2).to_broadcast([1, SLOT_GROUPS, EXPERTS])

                def by_expert(v):
                    return v.unsqueeze(1).to_broadcast([1, SLOT_GROUPS, EXPERTS])

                group_no = nums[0:1, 0:SLOT_GROUPS]
                tt(done_by[:], by_expert(end[0:1, :]), by_group(group_no), ALU.is_le)
                then(dve.tensor_reduce(group_f[:], done_by[:], AX.X, ALU.add))
                then(dve.tensor_scalar(c.group_expert[:], group_f[:], EXPERTS - 1.0, None, ALU.min))
                then(dve.tensor_copy(c.group_count[:], end[0:1, EXPERTS - 1:EXPERTS]))
                then(dve.tensor_scalar(first_slot[:], group_no, float(GROUP), None, ALU.mult))
                then(dve.tensor_scalar(second_slots[:], first_slot[:], float(P), None, ALU.add))
                tt(slots_end[:], start[0:1, :], count[0:1, :], ALU.add)
                tt(begun[:], by_expert(start[0:1, :]), by_group(first_slot[:]), ALU.is_le)
                tt(done_by[:], by_expert(slots_end[:]), by_group(second_slots[:]), ALU.is_gt)
                tt(begun[:], begun[:], done_by[:], ALU.mult)
                then(dve.tensor_reduce(paired[:], begun[:], AX.X, ALU.add))
                then(dve.tensor_tensor_scan(group_f[:], ones[0:1, 0:SLOT_GROUPS], paired[:], 0.0, ALU.mult, ALU.add))
                tt(group_f[:], group_f[:], paired[:], ALU.subtract)
                then(dve.tensor_copy(c.group_pairs[:], group_f[:]))


def phase_experts(c):
    nc, io, sem = c.nc, c.io, c.sem
    UIN, UOUT = 8, 4
    UN = UIN + UOUT
    KE = DE // P
    RAW, SPL = 6, 4
    AHEAD = 4
    with ExitStack() as mem:
        def sb(name, shape, dt=F32):
            return mem.enter_context(nc.sbuf_tensor(name, shape, dt))

        raw = sb("e_raw", [P, RAW, D])
        w_hi = sb("e_w_hi", [P, SPL, D], F32R)
        w_lo = sb("e_w_lo", [P, SPL, D], F32R)
        x = sb("e_x", [P, 2, D])
        xT_hi, xT_lo = sb("e_xT_hi", [P, 2, KT, P], F32R), sb("e_xT_lo", [P, 2, KT, P], F32R)
        sg, act_rows = sb("e_sg", [P, 2, DE]), sb("e_act", [P, 2, DE])
        aT_hi, aT_lo = sb("e_aT_hi", [P, 2, KE, P], F32R), sb("e_aT_lo", [P, 2, KE, P], F32R)
        y = sb("e_y", [P, 2, D])
        table = sb("e_table", [P, 2 * SLOT_GROUPS, 4], I32)
        gather_idx, row_idx = sb("e_gather_idx", [P, 2], I32), sb("e_row_idx", [P, 2], I32)
        wcol = sb("e_wcol", [P, 2])
        gu_ps = mem.enter_context(nc.psum_tensor("e_gu", [P, 4, 512], F32))
        t_ps = mem.enter_context(nc.psum_tensor("e_t", [P, 2, 512], F32))
        y_ps = mem.enter_context(nc.psum_tensor("e_y_ps", [P, 2, 512], F32))
        table_loaded, x_cleared = sem("e_table_loaded"), sem("e_x_cleared")
        raw_loaded, lo_done = c.sems("e_raw_loaded", RAW), c.sems("e_lo_done", RAW)
        hi_done, used = sem("e_hi_done"), c.sems("e_used", SPL)
        idx_ready, row_idx_ready = sem("e_idx_ready"), sem("e_row_idx_ready")
        x_loaded, x_turned, x_hi, x_kept = sem("e_x_loaded"), sem("e_x_turned"), sem("e_x_hi"), sem("e_x_kept")
        a_turned, a_hi, a_kept = sem("e_a_turned"), sem("e_a_hi"), sem("e_a_kept")
        silu_done, act_ready = sem("e_silu_done"), sem("e_act_ready")
        first_done, y_kept, y_stored = sem("e_first_done"), c.sems("e_y_kept", 2), sem("e_y_stored")
        y_free = sem("e_y_free")
        w_in = io.w_ei.rearrange("e (u a p) n -> e u p a n", a=2, p=P)
        w_out = io.w_eo.rearrange("e (k p) (b n) -> e b p k n", p=P, n=512)

        def groups(eng, body):
            count = eng.value_load(c.group_count[0:1, 0:1], min_val=1, max_val=MAXG)
            with eng.Fori(0, MAXG) as g:
                with eng.If(g < count):
                    body(g)
            return count

        def pairs(eng, g):
            return eng.value_load(c.group_pairs[0:1, ds(g, 1)], min_val=0, max_val=MAXG)

        def by_size(eng, before, after, part):
            with eng.If(before < after):
                part(2)
            with eng.If(before == after):
                part(1)

        with nc.Block() as block:

            @block.sync
            def _(sp):
                def load(g, ex, u):
                    r = u % RAW
                    sp.wait_ge(lo_done[r], 2 * g + u // RAW + 1)
                    if u < UIN:
                        sp.dma_start(raw[:, r, :].rearrange("p (a n) -> p a n", a=2),
                                     w_in[ds(ex, 1), u, :, :, :].rearrange("e p a n -> (e p) a n")).then_inc(raw_loaded[r], 16)
                    else:
                        sp.dma_start(raw[:, r, :].rearrange("p (k n) -> p k n", k=KE),
                                     w_out[ds(ex, 1), u - UIN, :, :, :].rearrange("e p k n -> (e p) k n")).then_inc(raw_loaded[r], 16)

                sp.dma_start(table[:], io.slots.rearrange("(t p) f -> p t f", p=P)).then_inc(table_loaded, 16)
                ex0 = sp.value_load(c.group_expert[0:1, 0:1], min_val=0, max_val=EXPERTS - 1)
                for u in range(AHEAD):
                    load(0, ex0, u)

                def body(g):
                    ex = sp.value_load(c.group_expert[0:1, ds(g, 1)], min_val=0, max_val=EXPERTS - 1)
                    for u in range(AHEAD, UN):
                        load(g, ex, u)
                    nx = sp.value_load(c.group_expert[0:1, ds(g + 1, 1)], min_val=0, max_val=EXPERTS - 1)
                    for u in range(AHEAD):
                        load(g + 1, nx, u)

                groups(sp, body)

            @block.gpsimd
            def _(pool):
                def gather_tile(r):
                    pool.indirect_dma_start(out=x[:, r, :], out_offset=None, in_=io.h2, in_offset=bass.IndirectOffsetOnAxis(
                        ap=gather_idx[:, r:r + 1].bitcast(U32), axis=0), bounds_check=TOK - 1, oob_is_err=False).then_inc(x_loaded, 16)

                def gather(g, before, after):
                    pool.wait_ge(idx_ready, g + 1)
                    c.hold(pool)
                    gather_tile(0)
                    with pool.If(before < after):
                        gather_tile(1)

                pool.memset(x[:], 0.0).then_inc(x_cleared, 1)
                pool.wait_ge(x_cleared, 1)
                p0, p1, p2 = (pairs(pool, g) for g in range(3))
                gather(0, p0, p1)
                pool.wait_ge(x_turned, 4 * p1 + 4)
                gather(1, p1, p2)

                def body(g):
                    here, nx, nx2, nx3 = (pairs(pool, g + i) for i in range(4))
                    pool.wait_ge(x_turned, 4 * (g + nx2 + 2))
                    gather(g + 2, nx2, nx3)

                    def scatter(n):
                        for eng in range(2):
                            pool.wait_ge(y_kept[eng], 2 * (g + here + n) + 1)
                        c.hold(pool)
                        for r in range(n):
                            pool.indirect_dma_start(out=io.expert_rows, out_offset=bass.IndirectOffsetOnAxis(
                                ap=row_idx[:, r:r + 1].bitcast(U32), axis=0), in_=y[:, r, :], in_offset=None,
                                bounds_check=TOPK * TOK - 1, oob_is_err=False).then_inc(y_stored, 16)

                    by_size(pool, here, nx, scatter)
                    pool.wait_ge(y_stored, 16 * (g + nx + 1))
                    pool.sem_inc(y_free, 1)

                count = groups(pool, body)
                all_pairs = pairs(pool, MAXG)
                pool.wait_ge(y_stored, 16 * (count + all_pairs))
                pool.wait_ge(x_loaded, 16 * (count + all_pairs + 2))

            @block.tensor
            def _(pe):
                c.start_at_one(pe, *lo_done, act_ready, *y_kept, *used, y_free)

                def turn_rows(tile, r, quads):
                    for q in quads:
                        if q >= 2:
                            pe.wait_ge(x_kept, 4 * tile + q - 1)
                        for j in range(4):
                            k = 4 * q + j
                            mm = pe.transpose(t_ps[:, q % 2, j * P:(j + 1) * P], x[:, r, k * P:(k + 1) * P], c.ident[:])
                        mm.then_inc(x_turned, 1)

                p1 = pairs(pe, 1)
                pe.wait_ge(x_loaded, 16 * p1 + 16)
                turn_rows(0, 0, range(4))
                with pe.If(p1 > 0):
                    pe.wait_ge(x_kept, 4)
                    turn_rows(1, 1, range(4))

                def body(g):
                    here, nx, nx2 = (pairs(pe, g + i) for i in range(3))

                    def gate_up(n):
                        pe.wait_ge(x_kept, 4 * (g + here + n))
                        pe.wait_ge(act_ready, g + here + 1)
                        for u in range(UIN):
                            s = u % SPL
                            pe.wait_ge(lo_done[u % RAW], 2 * g + u // RAW + 2)
                            for a in range(2):
                                k = 2 * u + a
                                for r in range(n):
                                    for x_part, w_part, last in ((xT_hi, w_hi, False), (xT_hi, w_lo, False), (xT_lo, w_hi, True)):
                                        for b in range(2):
                                            mm = pe.matmul(gu_ps[:, 2 * r + b, :], x_part[:, r, k, :],
                                                           w_part[:, s, a * 1024 + b * 512:a * 1024 + b * 512 + 512],
                                                           start=(k == 0 and x_part is xT_hi and w_part is w_hi), stop=(k == KT - 1 and last))
                            mm.then_inc(used[s], 1)
                        pe.wait_ge(x_loaded, 16 * (g + nx2 + 2))
                        tile = g + here + n
                        turn_rows(tile, 0, (0, 1))
                        for r in range(n):
                            pe.wait_ge(act_ready, g + here + r + 2)
                            pe.wait_ge(y_kept[r], 2 * (g + here) + 1)
                            for k in range(KE):
                                mm = pe.transpose(y_ps[:, r, k * P:(k + 1) * P], act_rows[:, r, k * P:(k + 1) * P], c.ident[:])
                            mm.then_inc(a_turned, 1)
                        turn_rows(tile, 0, (2, 3))

                    by_size(pe, here, nx, gate_up)
                    with pe.If(nx < nx2):
                        tile = g + nx + 2
                        pe.wait_ge(x_kept, 4 * tile)
                        turn_rows(tile, 1, range(4))

                    def out_rows(n):
                        for b in range(UOUT):
                            u = UIN + b
                            s = u % SPL
                            pe.wait_ge(lo_done[u % RAW], 2 * g + u // RAW + 2)
                            for r in range(n):
                                m = b * n + r
                                if b == 0:
                                    pe.wait_ge(a_kept, g + here + r + 1)
                                pe.wait_ge(y_kept[m % 2], 2 * (g + here) + m // 2 + 1)
                                for k in range(KE):
                                    for a_part, w_part, last in ((aT_hi, w_hi, False), (aT_hi, w_lo, False), (aT_lo, w_hi, True)):
                                        mm = pe.matmul(y_ps[:, m % 2, :], a_part[:, r, k, :], w_part[:, s, k * 512:(k + 1) * 512],
                                                       start=(k == 0 and a_part is aT_hi and w_part is w_hi), stop=(k == KE - 1 and last))
                                mm.then_inc(used[s] if r == n - 1 else first_done, 1)

                    by_size(pe, here, nx, out_rows)

                groups(pe, body)

            def unit_used(eng, g, u):
                eng.wait_ge(used[u % SPL], 3 * g + u // SPL + 2)

            def keep_y(eng, which, g, here, n, b, keep):
                for r in range(n):
                    m = b * n + r
                    if m % 2 == which:
                        if r == n - 1:
                            unit_used(eng, g, UIN + b)
                        else:
                            eng.wait_ge(first_done, 4 * here + b + 1)
                        keep(y[:, r, b * 512:(b + 1) * 512], y_ps[:, m % 2, :], wcol[:, r:r + 1]).then_inc(y_kept[which], 1)

            def quad(part, r, q):
                return part[:, r, 4 * q:4 * q + 4, :]

            def bank(ps, b):
                return ps[:, b, :].rearrange("p (a b) -> p a b", a=4)

            @block.scalar
            def _(act):
                def split_hi(g, u):
                    r, s = u % RAW, u % SPL
                    act.wait_ge(raw_loaded[r], 32 * g + 16 * (u // RAW) + 16)
                    act.wait_ge(used[s], 3 * g + u // SPL + 1)
                    act.activation(w_hi[:, s, :], raw[:, r, :], ACT.Copy).then_inc(hi_done, 1)

                def keep_rows_hi(tile, r, quads):
                    for q in quads:
                        act.wait_ge(x_turned, 4 * tile + q + 1)
                        act.activation(quad(xT_hi, r, q), bank(t_ps, q % 2), ACT.Copy).then_inc(x_hi, 1)

                p1 = pairs(act, 1)
                keep_rows_hi(0, 0, range(4))
                with act.If(p1 > 0):
                    keep_rows_hi(1, 1, range(4))
                for u in range(AHEAD):
                    split_hi(0, u)

                def body(g):
                    here, nx, nx2 = (pairs(act, g + i) for i in range(3))
                    for u in range(AHEAD, UN - 1):
                        split_hi(g, u)
                    unit_used(act, g, UIN - 1)
                    c.hold(act)

                    def activate(n):
                        for r in range(n):
                            act.activation(sg[:, r, :], gu_ps[:, 2 * r, :], ACT.Silu).then_inc(silu_done, 1)
                        keep_rows_hi(g + here + n, 0, (0, 1))
                        for r in range(n):
                            act.wait_ge(a_turned, g + here + r + 1)
                            act.activation(aT_hi[:, r], bank(y_ps, r), ACT.Copy).then_inc(a_hi, 1)
                        keep_rows_hi(g + here + n, 0, (2, 3))

                    by_size(act, here, nx, activate)
                    with act.If(nx < nx2):
                        keep_rows_hi(g + nx + 2, 1, range(4))
                    split_hi(g, UN - 1)
                    act.wait_ge(y_free, g + 1)
                    act.wait_ge(row_idx_ready, g + 1)
                    c.hold(act)

                    def keep(n):
                        for b in range(UOUT):
                            keep_y(act, 0, g, here, n, b, lambda out, ps, w: act.activation(out, ps, ACT.Copy, scale=w))
                            split_hi(g + 1, b)

                    by_size(act, here, nx, keep)

                groups(act, body)

            @block.vector
            def _(dve):
                def split_lo(g, u):
                    r, s = u % RAW, u % SPL
                    dve.wait_ge(hi_done, UN * g + u + 1)
                    dve.tensor_tensor(w_lo[:, s, :], raw[:, r, :], w_hi[:, s, :], ALU.subtract).then_inc(lo_done[r], 1)

                def keep_rows_lo(tile, r, quads):
                    for q in quads:
                        dve.wait_ge(x_hi, 4 * tile + q + 1)
                        dve.tensor_tensor(quad(xT_lo, r, q), bank(t_ps, q % 2), quad(xT_hi, r, q), ALU.subtract).then_inc(x_kept, 1)

                def field(g, f):
                    return table[:, ds(2 * g, 2), f:f + 1].rearrange("p a b -> p (a b)")

                p1 = pairs(dve, 1)
                dve.wait_ge(table_loaded, 16)
                dve.tensor_copy(gather_idx[:], field(0, 0)).then_inc(idx_ready, 1)
                dve.wait_ge(x_loaded, 16 * p1 + 16)
                dve.tensor_copy(gather_idx[:], field(1, 0)).then_inc(idx_ready, 1)
                keep_rows_lo(0, 0, range(4))
                with dve.If(p1 > 0):
                    keep_rows_lo(1, 1, range(4))
                for u in range(AHEAD):
                    split_lo(0, u)

                def body(g):
                    here, nx, nx2 = (pairs(dve, g + i) for i in range(3))
                    for u in range(AHEAD, UN - 1):
                        split_lo(g, u)

                    def activate(n):
                        for r in range(n):
                            dve.wait_ge(silu_done, g + here + r + 1)
                            dve.tensor_tensor(act_rows[:, r, :], sg[:, r, :], gu_ps[:, 2 * r + 1, :], ALU.mult).then_inc(act_ready, 1)
                        keep_rows_lo(g + here + n, 0, (0, 1))
                        for r in range(n):
                            dve.wait_ge(a_hi, g + here + r + 1)
                            dve.tensor_tensor(aT_lo[:, r], bank(y_ps, r), aT_hi[:, r], ALU.subtract).then_inc(a_kept, 1)
                        keep_rows_lo(g + here + n, 0, (2, 3))

                    by_size(dve, here, nx, activate)
                    with dve.If(nx < nx2):
                        keep_rows_lo(g + nx + 2, 1, range(4))
                    dve.wait_ge(x_loaded, 16 * (g + nx2 + 2))
                    dve.tensor_copy(gather_idx[:], field(g + 2, 0)).then_inc(idx_ready, 1)
                    dve.wait_ge(y_free, g + 1)
                    dve.wait_ge(y_kept[0], 2 * (g + here) + 1)
                    dve.tensor_copy(row_idx[:], field(g, 1))
                    dve.tensor_copy(wcol[:].bitcast(I32), field(g, 2)).then_inc(row_idx_ready, 1)
                    split_lo(g, UN - 1)
                    dve.wait_ge(row_idx_ready, g + 1)
                    c.hold(dve)

                    def keep(n):
                        for b in range(UOUT):
                            keep_y(dve, 1, g, here, n, b, lambda out, ps, w: dve.tensor_scalar(out, ps, w, None, ALU.mult))
                            split_lo(g + 1, b)

                    by_size(dve, here, nx, keep)

                groups(dve, body)


def phase_final(c):
    nc, io, sem = c.nc, c.io, c.sem
    SL = 3
    with ExitStack() as mem:
        def sb(name, shape, dt=F32):
            return mem.enter_context(nc.sbuf_tensor(name, shape, dt))

        x, r0, r1 = (sb(f"f_{n}", [P, SL, D]) for n in ("x", "r0", "r1"))
        g, junk = sb("f_g", [P, D]), sb("f_junk", [P, D])
        ssq, rstd = sb("f_ssq", [P, SL]), sb("f_rstd", [P, SL])
        loaded, stored = c.sems("f_loaded", SL), c.sems("f_stored", SL)
        g_loaded, step, summed = sem("f_g_loaded"), sem("f_step"), sem("f_summed")
        squared, root_done, rstd_done, ready = sem("f_squared"), sem("f_root_done"), sem("f_rstd_done"), sem("f_ready")
        with nc.Block() as block:

            @block.sync
            def _(sp):
                sp.dma_start(g[:], io.norm_final.to_broadcast([P, D])).then_inc(g_loaded, 16)
                with sp.Fori(0, NT // SL) as i:
                    for s in range(SL):
                        t = i * SL + s
                        sp.wait_ge(stored[s], 16 * i + 1)
                        sp.dma_start(x[:, s, :], io.x1[ds(t * P, P), :]).then_inc(loaded[s], 16)
                        sp.dma_start(r0[:, s, :], io.expert_rows[ds(t * P, P), :]).then_inc(loaded[s], 16)
                        sp.dma_start(r1[:, s, :], io.expert_rows[ds(t * P + TOK, P), :]).then_inc(loaded[s], 16)

            @block.vector
            def _(dve):
                def add(s, i, t):
                    dve.wait_ge(loaded[s], 48 * (i + 1))
                    dve.tensor_tensor(r0[:, s, :], r0[:, s, :], r1[:, s, :], ALU.add).then_inc(step, 1)
                    dve.wait_ge(step, t + 1)
                    dve.tensor_tensor(x[:, s, :], x[:, s, :], r0[:, s, :], ALU.add).then_inc(summed, 1)

                def scale(s, t):
                    dve.wait_ge(root_done, t + 1)
                    dve.reciprocal(rstd[:, s:s + 1], ssq[:, s:s + 1]).then_inc(rstd_done, 1)
                    dve.wait_ge(rstd_done, t + 1)
                    dve.scalar_tensor_tensor(x[:, s, :], x[:, s, :], rstd[:, s:s + 1], g[:], ALU.mult, ALU.mult).then_inc(ready, 1)

                dve.wait_ge(g_loaded, 16)
                add(0, 0, 0)
                with dve.Fori(0, NT // SL - 1) as i:
                    for s in range(SL):
                        t = i * SL + s
                        add((s + 1) % SL, i + (s + 1) // SL, t + 1)
                        scale(s, t)
                for s in range(SL):
                    t = NT - SL + s
                    if s + 1 < SL:
                        add(s + 1, NT // SL - 1, t + 1)
                    scale(s, t)

            @block.scalar
            def _(act):
                c.start_at_one(act, *stored)
                with act.Fori(0, NT // SL) as i:
                    for s in range(SL):
                        t = i * SL + s
                        act.wait_ge(summed, t + 1)
                        act.activation(junk[:], x[:, s, :], ACT.Square, accum_out=ssq[:, s:s + 1]).then_inc(squared, 1)
                        act.wait_ge(squared, t + 1)
                        act.activation(ssq[:, s:s + 1], ssq[:, s:s + 1], ACT.Sqrt, bias=c.eps[:], scale=1.0 / D).then_inc(root_done, 1)
                        act.wait_ge(ready, t + 1)
                        act.dma_start(io.y_all[ds(t * P, P), :], x[:, s, :]).then_inc(stored[s], 16)
                for s in range(SL):
                    act.wait_ge(stored[s], 16 * (NT // SL) + 1)



class Dram:

    def __init__(self, x, cache_k, cache_v, small, norm_mix, w_in, lam, head_norm, w_out, norm_ffn, w_router, b_router,
                 w_ei, w_eo, norm_final, y_all, k_all, v_all, conv_all):
        self.x, self.cache_k, self.cache_v, self.small = x, cache_k, cache_v, small
        self.norm_mix, self.w_in, self.lam, self.head_norm, self.w_out = norm_mix, w_in, lam, head_norm, w_out
        self.norm_ffn, self.w_router, self.b_router, self.w_ei, self.w_eo = norm_ffn, w_router, b_router, w_ei, w_eo
        self.norm_final, self.y_all, self.k_all, self.v_all, self.conv_all = norm_final, y_all, k_all, v_all, conv_all


def build(nc, io):
    io.chunks = nc.dram_tensor("chunks", (3 * CH, P, TOK), F32).ap()
    io.o_new = nc.dram_tensor("o_new", (STREAMS * NEW, DC), F32).ap()
    io.x1 = nc.dram_tensor("x1", (TOK, D), F32).ap()
    io.h2 = nc.dram_tensor("h2", (TOK, D), F32).ap()
    io.slots = nc.dram_tensor("slots", (SLOT_GROUPS * GROUP, 4), I32).ap()
    io.expert_rows = nc.dram_tensor("expert_rows", (TOPK * TOK, D), F32).ap()
    with ExitStack() as stack:
        c = Ctx(nc, io)

        def sb(name, shape, dt=F32):
            return stack.enter_context(nc.sbuf_tensor(name, shape, dt))

        c.ident = sb("ident", [P, P])
        c.eps = sb("eps", [P, 1])
        c.taps = sb("taps", [P, CH, 2 * STREAMS + 3])
        c.neglam = sb("neglam", [P, 1])
        c.hn = sb("hn", [P, VD])
        c.group_expert = sb("group_expert", [1, SLOT_GROUPS], I32)
        c.group_count = sb("group_count", [1, 1], I32)
        c.group_pairs = sb("group_pairs", [1, SLOT_GROUPS], I32)
        with ExitStack() as mem:
            hT_hi = mem.enter_context(nc.sbuf_tensor("hT_hi", [P, KT, TOK], F32R))
            hT_lo = mem.enter_context(nc.sbuf_tensor("hT_lo", [P, KT, TOK], F32R))
            phase_norm(c, hT_hi, hT_lo)
            phase_project(c, hT_hi, hT_lo)
        with ExitStack() as mem:
            def cat(name):
                return mem.enter_context(nc.sbuf_tensor(name, [P, CH, TOK], F32R))

            o_hi, o_lo = cat("o_hi"), cat("o_lo")
            phase_decode(c, o_hi, o_lo)
            a_hi, a_lo = cat("a_hi"), cat("a_lo")
            phase_attend(c, a_hi, a_lo, o_hi, o_lo)
            phase_mix_out(c, a_hi, a_lo, o_hi, o_lo)
        c.clear_semaphores()
        phase_route(c)
        phase_experts(c)
        phase_final(c)


def kernel(x_prompt, x_sample, cache_k, cache_v, state_conv, norm_mix, w_in, conv_w, lambda_q1, lambda_k1, lambda_q2,
           lambda_k2, head_norm, w_out, norm_ffn, w_router_group, b_router_group, w_router_expert, b_router_expert,
           w_expert_in, w_expert_out, norm_final):
    import concourse.bacc as bacc
    from concourse.bass_utils import run_bass_kernel_spmd

    a = np.asarray
    arrays = dict(
        x=np.concatenate([a(x_prompt)[0], a(x_sample).reshape(STREAMS * NEW, D)]),
        cache_k=a(cache_k).reshape(STREAMS, PAST, DC),
        cache_v=a(cache_v).reshape(STREAMS, PAST, DC),
        small=np.concatenate([a(state_conv).reshape(2 * STREAMS, DC), a(conv_w).reshape(3, DC)]),
        norm_mix=a(norm_mix).reshape(1, D),
        w_in=a(w_in)[0],
        lam=np.concatenate([a(v).reshape(1, DH) for v in (lambda_q1, lambda_k1, lambda_q2, lambda_k2)], axis=1),
        head_norm=a(head_norm).reshape(1, VD),
        w_out=a(w_out)[0],
        norm_ffn=a(norm_ffn).reshape(1, D),
        w_router=np.concatenate([a(w_router_group)[0], a(w_router_expert)[0]], axis=1),
        b_router=np.concatenate([a(b_router_group), a(b_router_expert)], axis=1),
        w_ei=a(w_expert_in)[0],
        w_eo=a(w_expert_out)[0],
        norm_final=a(norm_final).reshape(1, D),
    )
    nc = bacc.Bacc("TRN2", target_bir_lowering=False, num_devices=1)
    tensors = {}
    for name in arrays:
        arrays[name] = np.ascontiguousarray(arrays[name])
        tensors[name] = nc.dram_tensor(name, arrays[name].shape, F32, kind="ExternalInput").ap()
    outs = dict(y_all=(TOK, D), k_all=(TOK, DC), v_all=(TOK, DC), conv_all=(2 + 2 * STREAMS, DC))
    for name, shape in outs.items():
        tensors[name] = nc.dram_tensor(name, shape, F32, kind="ExternalOutput").ap()
    build(nc, Dram(**tensors))
    got = run_bass_kernel_spmd(nc, [arrays], core_ids=[0]).results[0]
    y, k, v, conv = (got[name] for name in outs)
    return (
        y[:PROMPT].reshape(1, PROMPT, D), y[PROMPT:].reshape(STREAMS, NEW, D),
        k[:PROMPT].reshape(1, 1, PROMPT, HEADS, 2, DH), v[:PROMPT].reshape(1, 1, PROMPT, HEADS, VD),
        conv[:2].reshape(1, 1, 2, DC),
        k[PROMPT:].reshape(1, STREAMS, NEW, HEADS, 2, DH), v[PROMPT:].reshape(1, STREAMS, NEW, HEADS, VD),
        conv[2:].reshape(1, STREAMS, 2, DC),
    )
```

```python
from contextlib import ExitStack

import numpy as np
import concourse.bass as bass
from concourse import mybir

F32 = mybir.dt.float32
F32R = mybir.dt.float32r
I32 = mybir.dt.int32
U32 = mybir.dt.uint32
ALU = mybir.AluOpType
ACT = mybir.ActivationFunctionType
AX = mybir.AxisListType
ds = bass.ds

P = 128
D = 2048
PROMPT = 1024
STREAMS = 8
NEW = 16
PAST = 512
TOK = PROMPT + STREAMS * NEW
NT = TOK // P
KT = D // P
HALF = KT // 2
NB = 3
BLK = TOK // NB
DC = D // 2
CH = DC // P
HEADS = 8
DH = 64
VD = 128
SCALE = DH ** -0.5
LAM_INIT = 0.8 - 0.6
EPS = 1e-6
MASKED = -1e30
GROUPS = 4
PER = 8
EXPERTS = GROUPS * PER
TOPK = 2
DE = 512
NR = GROUPS + EXPERTS
GROUP = 2 * P
MAXG = TOPK * TOK // GROUP + EXPERTS - 1
SLOT_GROUPS = MAXG + 3
BIG = 1e30
NO_ROW = 1 << 20


SL = 3
RAW = 6
AHEAD = 4


class Ctx:

    def __init__(self, nc, io):
        self.nc, self.io, self.in_use = nc, io, []
        self.passed = nc.alloc_semaphore("passed")

    def sem(self, name):
        self.in_use.append(self.nc.alloc_semaphore(name))
        return self.in_use[-1]

    def clear_semaphores(self):
        self.nc.clear_and_free_semaphores(self.in_use)
        self.nc.all_engine_barrier()
        self.in_use = []

    def start_at_one(self, eng, *sems):
        for sem in sems:
            eng.sem_inc(sem, 1)

    def hold(self, eng):
        eng.sem_inc(self.passed, 1)

    def sems(self, name, n):
        return [self.sem(f"{name}{i}") for i in range(n)]


def one_ahead(eng, front, back):
    front(0, 0, 0)
    with eng.Fori(0, NT // SL - 1) as i:
        for s in range(SL):
            front((s + 1) % SL, i + (s + 1) // SL, i * SL + s + 1)
            back(s, i * SL + s)
    for s in range(SL):
        if s + 1 < SL:
            front(s + 1, NT // SL - 1, NT - SL + s + 1)
        back(s, NT - SL + s)


def phase_norm(c, hT_hi, hT_lo):
    nc, io, sem = c.nc, c.io, c.sem
    with ExitStack() as mem:
        x = mem.enter_context(nc.sbuf_tensor("n_x", [P, SL, D], F32))
        g = mem.enter_context(nc.sbuf_tensor("n_g", [P, D], F32))
        ssq = mem.enter_context(nc.sbuf_tensor("n_ssq", [P, SL], F32))
        rstd = mem.enter_context(nc.sbuf_tensor("n_rstd", [P, SL], F32))
        small = mem.enter_context(nc.sbuf_tensor("n_small", [19, DC], F32))
        junk = mem.enter_context(nc.psum_tensor("n_junk", [P, D], F32))
        tp = mem.enter_context(nc.psum_tensor("n_tp", [P, 4, 512], F32))
        x_loaded = c.sems("n_x_loaded", SL)
        x_done = c.sems("n_x_done", SL)
        g_loaded, squared, ms_done = sem("n_g_loaded"), sem("n_squared"), sem("n_ms_done")
        small_loaded, small_turned, small_kept = sem("n_small_loaded"), sem("n_small_turned"), sem("n_small_kept")
        rstd_done, h_ready, turned = sem("n_rstd_done"), sem("n_h_ready"), sem("n_turned")
        hi_done, lo_done, ident0, ident_ready = sem("n_hi_done"), sem("n_lo_done"), sem("n_ident0"), sem("n_ident_ready")
        lam_loaded, lam_step = sem("n_lam_loaded"), sem("n_lam_step")
        lam_exp = sem("n_lam_exp")
        lamb = mem.enter_context(nc.sbuf_tensor("n_lamb", [P, 4, DH], F32))
        lw = mem.enter_context(nc.sbuf_tensor("n_lw", [P, 8], F32))
        with nc.Block() as block:

            @block.sync
            def _(sp):
                sp.dma_start(g[:], io.norm_mix.to_broadcast([P, D])).then_inc(g_loaded, 16)
                with sp.Fori(0, NT // SL) as i:
                    for s in range(SL):
                        sp.wait_ge(x_done[s], i + 1)
                        sp.dma_start(x[:, s, :], io.x[ds((i * SL + s) * P, P), :]).then_inc(x_loaded[s], 16)
                sp.dma_start(small[:], io.small).then_inc(small_loaded, 16)
                sp.dma_start(lamb[:].rearrange("p a b -> p (a b)"), io.lam.to_broadcast([P, 4 * DH])).then_inc(lam_loaded, 16)
                sp.dma_start(c.hn[:], io.head_norm.to_broadcast([P, VD])).then_inc(lam_loaded, 16)

            @block.gpsimd
            def _(pool):
                pool.memset(c.ident[:], 0.0).then_inc(ident0, 1)
                pool.wait_ge(ident0, 1)
                pool.affine_select(out=c.ident[:], in_=c.ident[:], compare_op=ALU.not_equal, fill=1.0, base=0,
                                   pattern=[[-1, P]], channel_multiplier=1).then_inc(ident_ready, 1)
                pool.memset(c.eps[:], EPS).then_inc(ident_ready, 1)

            @block.scalar
            def _(act):
                def root(s, i, t):
                    act.wait_ge(x_loaded[s], 16 * (i + 1))
                    act.wait_ge(rstd_done, t + 1)
                    act.activation(junk[:], x[:, s, :], ACT.Square, accum_out=ssq[:, s:s + 1]).then_inc(squared, 1)
                    act.wait_ge(squared, t + 1)
                    act.activation(ssq[:, s:s + 1], ssq[:, s:s + 1], ACT.Sqrt, bias=c.eps[:], scale=1.0 / D).then_inc(ms_done, 1)

                def keep_hi(s, t):
                    for q in range(4):
                        act.wait_ge(turned, 4 * t + q + 1)
                        act.activation(hT_hi[:, 4 * q:4 * q + 4, ds(t * P, P)],
                                       tp[:, q, :].rearrange("p (a b) -> p a b", a=4), ACT.Copy).then_inc(hi_done, 1)

                act.wait_ge(ident_ready, 2)
                one_ahead(act, root, keep_hi)
                act.wait_ge(lam_step, 2)
                act.activation(lw[:, 2:4], lw[:, 0:2], ACT.Exp).then_inc(lam_exp, 1)

            @block.vector
            def _(dve):
                dve.wait_ge(g_loaded, 16)
                def scale(s, i, t):
                    dve.wait_ge(ms_done, t + 1)
                    dve.reciprocal(rstd[:, s:s + 1], ssq[:, s:s + 1]).then_inc(rstd_done, 1)
                    dve.wait_ge(rstd_done, t + 2)
                    dve.scalar_tensor_tensor(x[:, s, :], x[:, s, :], rstd[:, s:s + 1], g[:], ALU.mult,
                                             ALU.mult).then_inc(h_ready, 1)

                def keep_lo(s, t):
                    for q in range(4):
                        dve.wait_ge(hi_done, 4 * t + q + 1)
                        dve.tensor_tensor(hT_lo[:, 4 * q:4 * q + 4, ds(t * P, P)],
                                          tp[:, q, :].rearrange("p (a b) -> p a b", a=4),
                                          hT_hi[:, 4 * q:4 * q + 4, ds(t * P, P)], ALU.subtract).then_inc(lo_done, 1)

                one_ahead(dve, scale, keep_lo)
                dve.wait_ge(small_turned, 1)
                dve.tensor_copy(c.taps[:], tp[:, 0, 0:CH * 19].rearrange("p (a b) -> p a b", a=CH)).then_inc(small_kept, 1)
                dve.wait_ge(lam_loaded, 32)
                lv = lamb[:].rearrange("p (m a) d -> p m a d", m=2)
                dve.tensor_tensor(lv[:, :, 0, :], lv[:, :, 0, :], lv[:, :, 1, :], ALU.mult).then_inc(lam_step, 1)
                dve.wait_ge(lam_step, 1)
                dve.tensor_reduce(lw[:, 0:2], lv[:, :, 0, :], AX.X, ALU.add).then_inc(lam_step, 1)
                dve.wait_ge(lam_exp, 1)
                dve.scalar_tensor_tensor(c.neglam[:], lw[:, 3:4], -LAM_INIT, lw[:, 2:3], ALU.add, ALU.subtract).then_inc(lam_step, 1)
                dve.tensor_scalar(c.hn[:], c.hn[:], 1.0 - LAM_INIT, None, ALU.mult).then_inc(lam_step, 1)

            @block.tensor
            def _(pe):
                c.start_at_one(pe, *x_done, rstd_done, lo_done)
                pe.wait_ge(ident_ready, 1)
                with pe.Fori(0, NT // SL) as i:
                    for s in range(SL):
                        t = i * SL + s
                        pe.wait_ge(h_ready, t + 1)
                        for q in range(4):
                            pe.wait_ge(lo_done, 4 * t + 1)
                            for j in range(4):
                                k = 4 * q + j
                                mm = pe.transpose(tp[:, q, j * P:(j + 1) * P], x[:, s, k * P:(k + 1) * P], c.ident[:])
                            mm.then_inc(turned, 1)
                        pe.wait_ge(turned, 4 * t + 4)
                        pe.sem_inc(x_done[s], 1)
                pe.wait_ge(small_loaded, 16)
                pe.wait_ge(lo_done, 4 * NT + 1)
                for j in range(CH):
                    mm = pe.transpose(tp[:, 0, j * 19:(j + 1) * 19], small[:, j * P:(j + 1) * P], c.ident[0:19, 0:19])
                mm.then_inc(small_turned, 1)


def weight_chunks(c, tag, w_raw, w_hi, w_lo):
    loaded, split = c.sems(f"{tag}_w_loaded", 2), c.sems(f"{tag}_w_split", 2)
    hi_done, half0_used = c.sem(f"{tag}_w_hi_done"), c.sem(f"{tag}_half0_used")
    z_done, z_kept = c.sems(f"{tag}_z_done", NB), c.sems(f"{tag}_z_kept", NB)

    def load(sp, n, w_cols):
        for half in range(2):
            sp.wait_ge(split[half], n + 1)
            c.hold(sp)
            sp.dma_start(w_raw[:, half * HALF:(half + 1) * HALF, :], w_cols(half)).then_inc(loaded[half], 16)

    def split_chunk(pool, n):
        for half in range(2):
            part = slice(half * HALF, (half + 1) * HALF)
            pool.wait_ge(loaded[half], 16 * (n + 1))
            pool.wait_ge(half0_used if half == 0 else z_done[NB - 1], n + 1)
            c.hold(pool)
            pool.tensor_copy(w_hi[:, part, :], w_raw[:, part, :]).then_inc(hi_done, 1)
            pool.wait_ge(hi_done, 2 * n + half + 1)
            pool.tensor_tensor(w_lo[:, part, :], w_raw[:, part, :], w_hi[:, part, :], ALU.subtract).then_inc(split[half], 1)

    def products(pe, n, half, z, x_hi, x_lo):
        pe.wait_ge(split[half], n + 2)
        for b in range(NB):
            if half == 0:
                pe.wait_ge(z_kept[b], n + 1)
            cols = slice(b * BLK, (b + 1) * BLK)
            for j in range(HALF):
                k = half * HALF + j
                xk = k % x_hi.shape[1]
                out = z[:, b, 0:BLK]
                pe.matmul(out, w_hi[:, k, :], x_hi[:, xk, cols], start=(k == 0), stop=False)
                pe.matmul(out, w_hi[:, k, :], x_lo[:, xk, cols], start=False, stop=False)
                mm = pe.matmul(out, w_lo[:, k, :], x_hi[:, xk, cols], start=False, stop=(k == KT - 1))
            if half == 1:
                mm.then_inc(z_done[b], 1)
        if half == 0:
            mm.then_inc(half0_used, 1)

    return load, split_chunk, products, z_done, z_kept, (*split, half0_used, *z_done, *z_kept)


def phase_project(c, hT_hi, hT_lo):
    nc, io, sem = c.nc, c.io, c.sem
    NCONV = 3 * CH
    with ExitStack() as mem:
        def sb(name, shape, dt=F32):
            return mem.enter_context(nc.sbuf_tensor(name, shape, dt))

        w_raw = sb("p_w_raw", [P, KT, P])
        w_hi = sb("p_w_hi", [P, KT, P], F32R)
        w_lo = sb("p_w_lo", [P, KT, P], F32R)
        e = sb("p_e", [P, TOK])
        xs = sb("p_xs", [P, TOK])
        up = sb("p_up", [P, 2 + PROMPT])
        us = sb("p_us", [P, STREAMS, 2 + NEW])
        tail = sb("p_tail", [P, CH, 2 + 2 * STREAMS])
        rows = sb("p_rows", [P, NT, P])
        tail_rows = sb("p_tail_rows", [2 + 2 * STREAMS, DC])
        z = mem.enter_context(nc.psum_tensor("p_z", [P, NB, 512], F32))
        tp = mem.enter_context(nc.psum_tensor("p_tp", [P, NB, 512], F32))
        load, split_chunk, products, z_done, z_kept, first_counts = weight_chunks(c, "p", w_raw, w_hi, w_lo)
        zeroed, step = sem("p_zeroed"), sem("p_conv_step")
        e_ready, e_stored = sem("p_e_ready"), sem("p_e_stored")
        e_turned, rows_ready, rows_stored = sem("p_e_turned"), sem("p_rows_ready"), sem("p_rows_stored")
        tail_turned, tail_kept, tail_stored = sem("p_tail_turned"), sem("p_tail_kept"), sem("p_tail_stored")

        w = io.w_in.rearrange("(h k p) n -> h p k n", h=2, p=P)
        NQ = NCONV + CH
        N = NQ + 2 * CH
        tr = slice(0, 3 * P)

        with nc.Block() as block:

            @block.sync
            def _(sp):
                with sp.Fori(0, CH) as t:
                    for r, kind in enumerate((2, 1, 0)):
                        load(sp, t * 3 + r, lambda half: w[half, :, :, ds(t * P + kind * DC, P)])
                with sp.Fori(0, 3 * CH) as t:
                    load(sp, t + NCONV, lambda half: w[half, :, :, ds(t * P + 3 * DC, P)])

            @block.gpsimd
            def _(pool):
                pool.memset(up[:, 0:2], 0.0).then_inc(zeroed, 1)
                with pool.Fori(0, N) as n:
                    split_chunk(pool, n)

            @block.tensor
            def _(pe):
                c.start_at_one(pe, *first_counts, e_stored, rows_stored, rows_ready)
                def turn_back(m):
                    pe.wait_ge(e_ready, m + 1 + 2 * CH)
                    for b in range(NB):
                        for j in range(NB):
                            mm = pe.transpose(tp[:, b, j * P:(j + 1) * P], e[:, (b * NB + j) * P:(b * NB + j + 1) * P],
                                              c.ident[:])
                        mm.then_inc(e_turned, 1)

                with pe.Fori(0, NQ) as n:
                    products(pe, n, 0, z, hT_hi, hT_lo)
                    products(pe, n, 1, z, hT_hi, hT_lo)
                products(pe, NQ, 0, z, hT_hi, hT_lo)
                products(pe, NQ, 1, z, hT_hi, hT_lo)
                with pe.Fori(1, 2 * CH) as m:
                    products(pe, m + NQ, 0, z, hT_hi, hT_lo)
                    pe.wait_ge(rows_ready, m)
                    turn_back(m - 1)
                    products(pe, m + NQ, 1, z, hT_hi, hT_lo)
                pe.wait_ge(rows_ready, 2 * CH)
                turn_back(2 * CH - 1)
                pe.wait_ge(rows_ready, 2 * CH + 1)
                for j in range(CH):
                    mm = pe.transpose(tp[0:2 + 2 * STREAMS, j // 4, (j % 4) * P:(j % 4 + 1) * P], tail[:, j, :], c.ident[:])
                mm.then_inc(tail_turned, 1)

            @block.vector
            def _(dve):
                cut = PROMPT - 2 * BLK
                ys = xs[:, PROMPT:TOK].rearrange("p (s r) -> p s r", s=STREAMS)
                es = slice(2, 2 + NEW)
                STEPS = 10
                dve.wait_ge(zeroed, 1)
                with dve.Fori(0, CH) as t:
                    for b in range(NB):
                        dve.wait_ge(z_done[b], t * 3 + 2)
                        dve.tensor_copy(xs[:, b * BLK:(b + 1) * BLK], z[:, b, 0:BLK]).then_inc(z_kept[b], 1)
                    dve.tensor_copy(us[:, :, 0:2], c.taps[:, ds(t, 1), 0:2 * STREAMS].rearrange(
                        "p a (s r) -> p (a s) r", s=STREAMS)).then_inc(step, 1)
                    dve.wait_ge(z_kept[2], t * 3 + 2)
                    for b in range(2):
                        dve.wait_ge(z_done[b], t * 3 + 3)
                        dve.tensor_tensor(up[:, 2 + b * BLK:2 + (b + 1) * BLK], z[:, b, 0:BLK],
                                          xs[:, b * BLK:(b + 1) * BLK], ALU.mult).then_inc(z_kept[b], 1)
                    dve.wait_ge(z_done[2], t * 3 + 3)
                    dve.tensor_tensor(up[:, 2 + 2 * BLK:2 + PROMPT], z[:, 2, 0:cut], xs[:, 2 * BLK:PROMPT],
                                      ALU.mult).then_inc(step, 1)
                    dve.tensor_tensor(us[:, :, es], z[:, 2, cut:BLK].rearrange("p (s r) -> p s r", s=STREAMS), ys,
                                      ALU.mult).then_inc(z_kept[2], 1)
                    dve.wait_ge(z_kept[2], t * 3 + 3)
                    dve.wait_ge(z_kept[1], t * 3 + 3)
                    dve.wait_ge(step, t * STEPS + 2)
                    dve.tensor_copy(tail[:, ds(t, 1), 0:2].rearrange("p a b -> p (a b)"), up[:, PROMPT:PROMPT + 2]).then_inc(step, 1)
                    dve.tensor_copy(tail[:, ds(t, 1), 2:2 + 2 * STREAMS].rearrange("p a (s r) -> p (a s) r", s=STREAMS),
                                    us[:, :, NEW:NEW + 2]).then_inc(step, 1)
                    def tap(j):
                        return c.taps[:, ds(t, 1), 2 * STREAMS + j:2 * STREAMS + j + 1].rearrange("p a b -> p (a b)")
                    dve.tensor_scalar(xs[:, 0:PROMPT], up[:, 0:PROMPT], tap(0), None, ALU.mult).then_inc(step, 1)
                    dve.tensor_scalar(ys, us[:, :, 0:NEW], tap(0), None, ALU.mult).then_inc(step, 1)
                    for j in (1, 2):
                        dve.wait_ge(step, t * STEPS + 4 + 2 * j)
                        dve.scalar_tensor_tensor(xs[:, 0:PROMPT], up[:, j:j + PROMPT], tap(j), xs[:, 0:PROMPT], ALU.mult,
                                                 ALU.add).then_inc(step, 1)
                        dve.scalar_tensor_tensor(ys, us[:, :, j:j + NEW], tap(j), ys, ALU.mult, ALU.add).then_inc(step, 1)
                    dve.wait_ge(step, t * STEPS + STEPS)
                    dve.wait_ge(e_stored, 16 * t + 1)
                    for b in range(NB):
                        dve.wait_ge(z_done[b], t * 3 + 4)
                        dve.tensor_tensor(e[:, b * BLK:(b + 1) * BLK], z[:, b, 0:BLK], xs[:, b * BLK:(b + 1) * BLK],
                                          ALU.mult).then_inc(z_kept[b], 1)
                    dve.wait_ge(z_kept[2], t * 3 + 4)
                    dve.sem_inc(e_ready, 1)
                with dve.Fori(0, CH) as t:
                    dve.wait_ge(e_stored, 16 * (t + CH) + 1)
                    for b in range(NB):
                        dve.wait_ge(z_done[b], t + NCONV + 2)
                        dve.tensor_scalar(e[:, b * BLK:(b + 1) * BLK], z[:, b, 0:BLK], SCALE, None, ALU.mult).then_inc(z_kept[b], 1)
                    dve.wait_ge(z_kept[2], t + NCONV + 2)
                    dve.sem_inc(e_ready, 1)

                def keep_rows(m):
                    dve.wait_ge(rows_stored, 16 * m + 1)
                    for b in range(NB):
                        dve.wait_ge(e_turned, NB * m + b + 1)
                        cp = dve.tensor_copy(rows[:, b * NB:(b + 1) * NB, :],
                                             tp[:, b, tr].rearrange("p (a q) -> p a q", a=NB))
                    cp.then_inc(rows_ready, 1)

                def keep_e(m, stored):
                    dve.wait_ge(e_stored, stored + 1)
                    for b in range(NB):
                        dve.wait_ge(z_done[b], m + NQ + 2)
                        dve.tensor_copy(e[:, b * BLK:(b + 1) * BLK], z[:, b, 0:BLK]).then_inc(z_kept[b], 1)
                    dve.wait_ge(z_kept[2], m + NQ + 2)
                    dve.sem_inc(e_ready, 1)

                keep_e(0, 16 * 2 * CH)
                with dve.Fori(1, CH + 1) as m:
                    keep_rows(m - 1)
                    keep_e(m, (m + 2 * CH) * 16)
                with dve.Fori(CH + 1, 2 * CH) as m:
                    keep_rows(m - 1)
                    keep_e(m, 16 * 3 * CH)
                keep_rows(2 * CH - 1)
                dve.wait_ge(tail_turned, 1)
                dve.tensor_copy(tail_rows[:].rearrange("p (a q) -> p a q", a=2), tp[0:2 + 2 * STREAMS, 0:2, :]).then_inc(tail_kept, 1)

            @block.scalar
            def _(act):
                with act.Fori(0, 2 * CH) as t:
                    act.wait_ge(e_ready, t + 1)
                    act.dma_start(io.chunks[ds(t, 1), :, :].rearrange("a p n -> (a p) n"), e[:]).then_inc(e_stored, 16)

                def store_rows(dram, m, done):
                    act.wait_ge(rows_ready, done + 2)
                    act.dma_start(dram.rearrange("(t p) n -> p t n", p=P)[:, :, ds(m * P, P)], rows[:]).then_inc(rows_stored, 16)

                with act.Fori(0, CH) as m:
                    act.wait_ge(e_ready, m + 2 * CH + 1)
                    act.dma_start(io.chunks[ds(m + 2 * CH, 1), :, :].rearrange("a p n -> (a p) n"), e[:]).then_inc(e_stored, 16)
                    store_rows(io.k_all, m, m)
                with act.Fori(0, CH) as m:
                    store_rows(io.v_all, m, m + CH)
                act.wait_ge(tail_kept, 1)
                act.dma_start(io.conv_all, tail_rows[:]).then_inc(tail_stored, 16)
                act.wait_ge(tail_stored, 16)
                act.wait_ge(rows_stored, 16 * 2 * CH + 1)
                act.wait_ge(e_stored, 16 * 3 * CH + 1)


def head_norm(dve, o, ssq, rstd, step, root_ready):
    dve.wait_ge(root_ready, 1)
    dve.reciprocal(rstd[:], ssq[:]).then_inc(step, 1)
    dve.wait_ge(step, 3)
    dve.tensor_tensor(o, o, rstd[:].unsqueeze(2).to_broadcast([P, HEADS, VD]), ALU.mult).then_inc(step, 1)
    dve.wait_ge(step, 4)


def norm_sums(dve, o, square, ssq, step):
    dve.tensor_tensor(square, o, o, ALU.mult).then_inc(step, 1)
    dve.wait_ge(step, 1)
    dve.tensor_reduce(ssq[:], square, AX.X, ALU.add).then_inc(step, 1)


def phase_decode(c):
    nc, io, sem = c.nc, c.io, c.sem
    HG = 4
    KEYS = PAST + NEW
    PT = PAST // P
    with ExitStack() as mem:
        def sb(name, shape, dt=F32):
            return mem.enter_context(nc.sbuf_tensor(name, shape, dt))

        k = sb("d_k", [P, 2, PT, DC])
        v = sb("d_v", [P, 2, PT, DC])
        vn = sb("d_vn", [NEW, 2, DC])
        kT = sb("d_kT", [P, 2, HEADS, KEYS])
        qs = sb("d_q", [P, HEADS, P])
        qx = sb("d_qx", [P, HEADS, P])
        pr = sb("d_pr", [P, 2, KEYS])
        mixer, mixl = sb("d_mixer", [P, HG * NEW]), sb("d_mixl", [P, 2, HG * NEW])
        at = sb("d_at", [P, PT + 1, HG * NEW])
        orow = sb("d_orow", [NEW, DC])
        nb, l, rl = (sb(f"d_{n}", [P, 2]) for n in ("nb", "l", "rl"))
        t_ps = mem.enter_context(nc.psum_tensor("d_t", [P, 2, 512], F32))
        s_ps = mem.enter_context(nc.psum_tensor("d_s", [P, 2, 1024], F32))
        at_ps = mem.enter_context(nc.psum_tensor("d_at_ps", [P, 512], F32))
        o_ps = mem.enter_context(nc.psum_tensor("d_o_ps", [P, 512], F32))
        k_loaded, v_loaded, kn_loaded = (c.sems(f"d_{n}_loaded", 2) for n in ("k", "v", "kn"))
        q_loaded = sem("d_q_loaded")
        k_turned, kT_ready = sem("d_k_turned"), c.sems("d_kT_ready", 2)
        qx_zeroed, qx_ready, mixer_step = sem("d_qx_zeroed"), sem("d_qx_ready"), sem("d_mixer_step")
        scores_done, step, exp_done, mixl_ready = sem("d_scores_done"), sem("d_step"), sem("d_exp_done"), sem("d_mixl_ready")
        at_done, at_kept, o_done, o_kept, o_stored = sem("d_at_done"), sem("d_at_kept"), sem("d_o_done"), sem("d_o_kept"), sem("d_o_stored")
        bias_ready = sem("d_bias_ready")
        G = HEADS // HG

        def by_stream(eng, stream):
            with eng.Fori(0, STREAMS // 2 - 1) as i:
                for s in range(2):
                    stream(i, s, True)
            stream(STREAMS // 2 - 1, 0, True)
            stream(STREAMS // 2 - 1, 1, False)

        with nc.Block() as block:

            @block.sync
            def _(sp):
                sp.dma_start(qs[:], io.chunks[CH:2 * CH, :, PROMPT:TOK].rearrange("h p n -> p h n")).then_inc(q_loaded, 16)

                def load_keys(b, s):
                    sp.dma_start(k[:, s], io.cache_k[ds(b, 1), :, :].rearrange("a (t p) n -> p (a t) n", p=P)).then_inc(k_loaded[s], 16)

                def load_new_keys(b, s):
                    sp.dma_start(kT[:, s, :, PAST:KEYS], io.chunks[2 * CH:3 * CH, :, ds(b * NEW + PROMPT, NEW)].rearrange(
                        "h p n -> p h n")).then_inc(kn_loaded[s], 16)

                def load_values(b, s):
                    sp.dma_start(v[:, s], io.cache_v[ds(b, 1), :, :].rearrange("a (t p) n -> p (a t) n", p=P)).then_inc(v_loaded[s], 16)
                    sp.dma_start(vn[:, s, :], io.v_all[ds(b * NEW + PROMPT, NEW), :]).then_inc(v_loaded[s], 16)

                for b in range(2):
                    load_keys(b, b)
                    load_new_keys(b, b)
                    load_values(b, b)
                with sp.Fori(1, STREAMS // 2) as i:
                    for s in range(2):
                        b = 2 * i + s
                        sp.wait_ge(k_turned, HEADS * (b - 1) + 1)
                        load_keys(b, s)
                        sp.wait_ge(scores_done, G * (b - 1) + 1)
                        load_new_keys(b, s)
                        sp.wait_ge(o_done, G * (b - 1) + 1)
                        load_values(b, s)
                sp.wait_ge(o_stored, 16 * STREAMS + 1)

            @block.gpsimd
            def _(pool):
                pool.memset(qx[:], 0.0).then_inc(qx_zeroed, 1)

            @block.tensor
            def _(pe):
                c.start_at_one(pe, k_turned, scores_done, o_done, *kT_ready, exp_done, at_kept, o_kept, at_done, o_stored)

                def turn_keys(i, s, heads):
                    b = 2 * i + s
                    for h in heads:
                        if h == 0:
                            pe.wait_ge(k_loaded[s], 16 * (i + 1))
                        pe.wait_ge(kT_ready[h % 2], b * (HEADS // 2) + h // 2 + 1)
                        for t in range(PT):
                            mm = pe.transpose(t_ps[:, h % 2, t * P:(t + 1) * P], k[:, s, t, h * VD:(h + 1) * VD], c.ident[:])
                        mm.then_inc(k_turned, 1)

                def scores(b, s, hg):
                    pe.wait_ge(qx_ready, b * G + hg + 1)
                    for lo, hi in ((0, PAST), (PAST, KEYS)):
                        for j in range(HG):
                            h = hg * HG + j
                            mm = pe.matmul(s_ps[:, hg, lo:hi], qx[:, h, :], kT[:, s, h, lo:hi], start=(j == 0), stop=(j == HG - 1))
                    mm.then_inc(scores_done, 1)

                def mix(b, hg):
                    pe.wait_ge(mixl_ready, b * G + hg + 1)
                    pe.wait_ge(at_kept, b * G + hg + 1)
                    for t in range(PT + 1):
                        w = min(P, KEYS - t * P)
                        mm = pe.matmul(at_ps[0:w, t * HG * NEW:(t + 1) * HG * NEW], pr[:, hg, t * P:t * P + w], mixl[:, hg, :],
                                       start=True, stop=True)
                    mm.then_inc(at_done, 1)

                def values(b, i, s, hg):
                    pe.wait_ge(at_kept, b * G + hg + 2)
                    pe.wait_ge(o_kept, b * G + hg + 1)
                    if hg == 0:
                        pe.wait_ge(v_loaded[s], 32 * (i + 1))
                    for j in range(HG):
                        cols = slice((hg * HG + j) * VD, (hg * HG + j + 1) * VD)
                        for t in range(PT + 1):
                            w = min(P, KEYS - t * P)
                            rhs = v[:, s, t, cols] if t < PT else vn[:, s, cols]
                            mm = pe.matmul(o_ps[0:NEW, j * VD:(j + 1) * VD], at[0:w, t, j * NEW:(j + 1) * NEW], rhs,
                                           start=(t == 0), stop=(t == PT))
                    mm.then_inc(o_done, 1)

                def stream(i, s, more):
                    b = 2 * i + s
                    nx = (i + s, 1 - s)
                    pe.wait_ge(exp_done, b * G + 1)
                    for part in range(2):
                        pe.wait_ge(kT_ready[part], (b + 1) * (HEADS // 2) + 1)
                    pe.wait_ge(kn_loaded[s], 16 * (i + 1))
                    scores(b, s, 0)
                    scores(b, s, 1)
                    if more:
                        turn_keys(*nx, range(0, 4))
                    mix(b, 0)
                    if more:
                        turn_keys(*nx, range(4, 6))
                    values(b, i, s, 0)
                    mix(b, 1)
                    if more:
                        turn_keys(*nx, range(6, 8))
                    values(b, i, s, 1)

                turn_keys(0, 0, range(HEADS))
                by_stream(pe, stream)

            @block.vector
            def _(dve):
                idv = c.ident[:].rearrange("p (h m q) -> p h m q", h=HG, m=2)
                mv = mixer[:].rearrange("p (h q) -> p h q", h=HG)
                dve.tensor_scalar(mv, idv[:, :, 1, :], c.neglam[:], None, ALU.mult).then_inc(mixer_step, 1)
                dve.wait_ge(mixer_step, 1)
                dve.tensor_tensor(mv, mv, idv[:, :, 0, :], ALU.add).then_inc(mixer_step, 1)
                dve.wait_ge(mixer_step, 2)
                dve.wait_ge(qx_zeroed, 1)
                dve.wait_ge(q_loaded, 16)
                def spread_queries(b):
                    dve.wait_ge(scores_done, b * G + 1)
                    for h in range(HEADS):
                        for m in range(2):
                            part, col = slice(m * DH, (m + 1) * DH), (2 * (h % HG) + m) * NEW
                            cp = dve.tensor_copy(qx[part, h, col:col + NEW], qs[part, h, ds(b * NEW, NEW)])
                        if h % HG == HG - 1:
                            cp.then_inc(qx_ready, 1)

                def keep_keys(b, s, heads):
                    for h in heads:
                        dve.wait_ge(k_turned, b * HEADS + h + 2)
                        dve.tensor_copy(kT[:, s, h, 0:PAST], t_ps[:, 1, :]).then_inc(kT_ready[1], 1)

                def bias(b, hg):
                    dve.wait_ge(scores_done, b * G + hg + 2)
                    dve.tensor_reduce(nb[:, hg:hg + 1], s_ps[:, hg, 0:KEYS], AX.X, ALU.max, negate=True).then_inc(bias_ready, 1)

                def over_sum(b, hg):
                    n = b * G + hg
                    dve.wait_ge(exp_done, n + 2)
                    dve.reciprocal(rl[:, hg:hg + 1], l[:, hg:hg + 1]).then_inc(step, 1)
                    dve.wait_ge(step, n + 1)
                    dve.tensor_scalar(mixl[:, hg, :], mixer[:], rl[:, hg:hg + 1], None, ALU.mult).then_inc(mixl_ready, 1)

                def keep_mixed(b, hg):
                    dve.wait_ge(at_done, b * G + hg + 2)
                    w = PT * HG * NEW
                    dve.tensor_copy(at[:, 0:PT, :].rearrange("p a b -> p (a b)"), at_ps[:, 0:w])
                    dve.tensor_copy(at[0:NEW, PT, :], at_ps[0:NEW, w:w + HG * NEW]).then_inc(at_kept, 1)

                def stream(i, s, more):
                    b, nx = 2 * i + s, 1 - s
                    bias(b, 0)
                    bias(b, 1)
                    over_sum(b, 0)
                    if more:
                        keep_keys(b + 1, nx, (1, 3))
                    over_sum(b, 1)
                    keep_mixed(b, 0)
                    if more:
                        spread_queries(b + 1)
                        keep_keys(b + 1, nx, (5,))
                    keep_mixed(b, 1)
                    if more:
                        keep_keys(b + 1, nx, (7,))

                spread_queries(0)
                keep_keys(0, 0, range(1, HEADS, 2))
                by_stream(dve, stream)

            @block.scalar
            def _(act):
                def keep_keys(b, s, heads):
                    for h in heads:
                        act.wait_ge(k_turned, b * HEADS + h + 2)
                        act.activation(kT[:, s, h, 0:PAST], t_ps[:, 0, :], ACT.Copy).then_inc(kT_ready[0], 1)

                def exps(b, hg):
                    act.wait_ge(bias_ready, b * G + hg + 1)
                    act.wait_ge(at_done, b * G + 1)
                    act.activation(pr[:, hg, :], s_ps[:, hg, 0:KEYS], ACT.Exp, bias=nb[:, hg:hg + 1],
                                   accum_out=l[:, hg:hg + 1]).then_inc(exp_done, 1)

                def keep_rows(b, hg):
                    act.wait_ge(o_done, b * G + hg + 2)
                    if hg == 0:
                        act.wait_ge(o_stored, 16 * b + 1)
                    act.activation(orow[:, hg * 512:(hg + 1) * 512], o_ps[0:NEW, :], ACT.Copy).then_inc(o_kept, 1)

                def stream(i, s, more):
                    b, nx = 2 * i + s, 1 - s
                    exps(b, 0)
                    exps(b, 1)
                    if more:
                        keep_keys(b + 1, nx, (0, 2, 4))
                    keep_rows(b, 0)
                    if more:
                        keep_keys(b + 1, nx, (6,))
                    keep_rows(b, 1)
                    act.wait_ge(o_kept, G * (b + 1) + 1)
                    act.dma_start(io.o_new[ds(b * NEW, NEW), :], orow[:]).then_inc(o_stored, 16)

                keep_keys(0, 0, range(0, HEADS, 2))
                by_stream(act, stream)


def phase_attend(c, a_hi, a_lo, o_hi, o_lo):
    nc, io, sem = c.nc, c.io, c.sem
    QT = PROMPT // P
    with ExitStack() as mem:
        def sb(name, shape, dt=F32):
            return mem.enter_context(nc.sbuf_tensor(name, shape, dt))

        q = sb("a_q", [P, 2, PROMPT])
        k = sb("a_k", [P, 2, PROMPT])
        v = sb("a_v", [P, 2, QT, VD])
        pr = sb("a_pr", [P, 2, 2, PROMPT])
        at = sb("a_at", [P, 2, PROMPT])
        o = sb("a_o", [P, 2, QT, VD])
        nb, l, rl = (sb(f"a_{n}", [P, 2, 2]) for n in ("nb", "l", "rl"))
        cf = sb("a_cf", [P, 1])
        mask_q, mask_k = sb("a_mask_q", [P, P]), sb("a_mask_k", [P, P // 2])
        ssq, rstd = sb("a_ssq", [P, QT]), sb("a_rstd", [P, QT])
        a_raw = sb("a_raw", [P, TOK])
        square = a_raw[:, 0:QT * VD].rearrange("p (a b) -> p a b", a=QT)
        s_ps = mem.enter_context(nc.psum_tensor("a_s", [P, 2, PROMPT], F32))
        t_ps = mem.enter_context(nc.psum_tensor("a_t", [P, 2, 512], F32))
        o_ps = mem.enter_context(nc.psum_tensor("a_o_ps", [P, 2, 512], F32))
        head_loaded, head_used = c.sems("a_head_loaded", 2), c.sems("a_head_used", 2)
        scores_done, exp_done, bias_ready = c.sems("a_scores_done", 2), c.sems("a_exp_done", 2), c.sems("a_bias_ready", 2)
        step, mixed, mask_step = sem("a_step"), sem("a_mixed"), sem("a_mask_step")
        turned, t_kept = c.sems("a_turned", 2), c.sems("a_t_kept", 2)
        at_ready, pv_done, o_kept = sem("a_at_ready"), sem("a_pv_done"), sem("a_o_kept")
        sums_ready, root_ready, rstd_ready, scaled, normed = (sem(f"a_{n}") for n in ("sums_ready", "root_ready", "rstd_ready", "scaled", "normed"))
        squared, out_hi, out_done = sem("a_squared"), sem("a_out_hi"), sem("a_out_done")
        raw_loaded, split_hi, split_lo = sem("a_raw_loaded"), sem("a_split_hi"), sem("a_split_lo")
        so, so_square = (pr[:, slot, 1, :].rearrange("p (a b) -> p a b", a=HEADS) for slot in range(2))
        so_ssq, so_rstd = sb("a_so_ssq", [P, HEADS]), sb("a_so_rstd", [P, HEADS])
        so_loaded, so_step, so_root, so_normed, so_hi = (sem(f"a_so_{n}") for n in ("loaded", "step", "root", "normed", "hi"))
        STEPS = 2

        TURNS = {7: (0, 1), 0: (2,), 1: (3,), 2: (4,), 3: (5,), 4: (6, 7), 5: (8, 9), 6: (10, 11), "out": (12, 13),
                 "streams": (2, 3), "last out": (4, 5)}
        SUMS_STEP, ROOT_STEP, INVERSE_STEP, OUT_STEP = 4, 5, 6, 7

        def bank_use(h, turn):
            missing = 1 if isinstance(h, int) and h == 0 else 2
            return turn % 2, 7 * h + turn // 2 - missing

        def blocks(i, n):
            return range(4 * n, min(4 * n + 4, i + 1))

        def pair(body, eng):
            body(0, True)
            with eng.Fori(1, HEADS // 2) as it:
                body(it, False)

        with nc.Block() as block:

            @block.gpsimd
            def _(pool):
                pool.memset(mask_k[:], 1.0).then_inc(mask_step, 1)
                pool.memset(mask_q[:], 0.0).then_inc(mask_step, 1)
                pool.wait_ge(mask_step, 2)
                for m in range(2):
                    pool.memset(mask_q[m * DH:m * DH + 1, 0:P // 2], MASKED).then_inc(mask_step, 1)
                pool.wait_ge(mask_step, 4)
                with pool.Fori(0, HEADS // 2) as it:
                    for s in range(2):
                        h = 2 * it + s
                        pool.dma_start(a_raw[:], io.chunks[ds(h, 1), :, :].rearrange("a p n -> (a p) n")).then_inc(raw_loaded, 16)
                        pool.wait_ge(raw_loaded, 16 * (h + 1))
                        c.hold(pool)
                        hi = a_hi[:, ds(h, 1), :].rearrange("p a b -> p (a b)")
                        pool.tensor_copy(hi, a_raw[:]).then_inc(split_hi, 1)
                        pool.wait_ge(split_hi, h + 1)
                        pool.tensor_tensor(a_lo[:, ds(h, 1), :].rearrange("p a b -> p (a b)"), a_raw[:], hi, ALU.subtract).then_inc(split_lo, 1)
                        pool.wait_ge(o_kept, QT * (h + 1))
                        pool.wait_ge(split_lo, h + 2)
                        pool.tensor_tensor(square, o[:, s], o[:, s], ALU.mult).then_inc(squared, 1)
                        pool.wait_ge(rstd_ready, h + 1)
                        pool.tensor_tensor(o[:, s], o[:, s], rstd[:].unsqueeze(2).to_broadcast([P, QT, VD]), ALU.mult).then_inc(scaled, 1)
                        pool.wait_ge(scaled, h + 1)
                        pool.tensor_tensor(o[:, s], o[:, s], c.hn[:].unsqueeze(1).to_broadcast([P, QT, VD]), ALU.mult).then_inc(normed, 1)

            @block.sync
            def _(sp):
                with sp.Fori(0, HEADS // 2) as it:
                    for s in range(2):
                        h = 2 * it + s
                        sp.wait_ge(head_used[s], it + 1)
                        c.hold(sp)
                        sp.dma_start(q[:, s, :], io.chunks[ds(h + CH, 1), :, 0:PROMPT].rearrange("a p n -> (a p) n")).then_inc(head_loaded[s], 16)
                        sp.dma_start(k[:, s, :], io.chunks[ds(h + 2 * CH, 1), :, 0:PROMPT].rearrange("a p n -> (a p) n")).then_inc(head_loaded[s], 16)
                        sp.dma_start(v[:, s, :, :], io.v_all[0:PROMPT, ds(h * VD, VD)].rearrange("(t p) e -> p t e", p=P)).then_inc(head_loaded[s], 16)
                sp.wait_ge(mixed, HEADS * QT)
                sp.dma_start(so, io.o_new.rearrange("p (a b) -> p a b", a=HEADS)).then_inc(so_loaded, 16)

            @block.tensor
            def _(pe):
                c.start_at_one(pe, *head_used, *exp_done, *t_kept, split_lo)

                def scores(s, i, g):
                    w = P * (i + 1)
                    for m in range(2):
                        part = slice(m * DH, (m + 1) * DH)
                        pe.wait_ge(exp_done[m], g + 1)
                        for b in range(0, P * (i + 1), 512):
                            e = min(b + 512, P * (i + 1))
                            mm = pe.matmul(s_ps[:, m, b:e], q[part, s, i * P:(i + 1) * P], k[part, s, b:e], start=True, stop=e < w)
                        mm = pe.matmul(s_ps[:, m, w - P // 2:w], mask_q[part, :], mask_k[part, :], start=False, stop=True)
                        mm.then_inc(scores_done[m], 1)

                def turn(i, h, g):
                    pe.wait_ge(mixed, g + 1)
                    for n, at_turn in enumerate(TURNS[i]):
                        bank, before = bank_use(h, at_turn)
                        pe.wait_ge(t_kept[bank], before + 1)
                        for j in blocks(i, n):
                            mm = pe.transpose(t_ps[:, bank, (j % 4) * P:(j % 4 + 1) * P], pr[:, i % 2, 0, j * P:(j + 1) * P],
                                              c.ident[:])
                        mm.then_inc(turned[bank], 1)

                def weigh(s, i, g):
                    pe.wait_ge(at_ready, g + 1)
                    for j in range(i + 1):
                        mm = pe.matmul(o_ps[:, i % 2, 0:VD], at[:, i % 2, j * P:(j + 1) * P], v[:, s, j, :], start=(j == 0), stop=(j == i))
                    mm.then_inc(pv_done, 1)

                def turn_out(h, s, turns=TURNS["out"]):
                    pe.wait_ge(normed, h)
                    for n, at_turn in enumerate(turns):
                        bank, before = bank_use(h, at_turn)
                        pe.wait_ge(t_kept[bank], before + 1)
                        for j in range(4):
                            mm = pe.transpose(t_ps[:, bank, j * P:(j + 1) * P], o[:, s, 4 * n + j, :], c.ident[:])
                        mm.then_inc(turned[bank], 1)

                def body(it, first):
                    for s in range(2):
                        h = 2 * it + s
                        start = first and s == 0
                        pe.wait_ge(head_loaded[s], 48 * (it + 1))
                        for i in range(QT):
                            g = h * QT + i
                            scores(s, i, g)
                            if not (start and i < 2):
                                weigh(s if i >= 2 else 1 - s, (i - 2) % QT, g - 2)
                            if i == 1 and not start:
                                pe.wait_ge(pv_done, g - 1)
                                pe.sem_inc(head_used[1 - s], 1)
                            if not (start and i == 0):
                                turn((i - 1) % QT, h, g - 1)
                            if i == OUT_STEP and not start:
                                turn_out(h, 1 - s)

                pe.wait_ge(mask_step, 4)
                pair(body, pe)
                n = HEADS * QT
                weigh(1, QT - 2, n - 2)
                turn(QT - 1, HEADS, n - 1)
                weigh(1, QT - 1, n - 1)
                pe.wait_ge(so_normed, 1)
                for m, at_turn in enumerate(TURNS["streams"]):
                    bank, before = bank_use(HEADS, at_turn)
                    pe.wait_ge(t_kept[bank], before + 1)
                    for j in range(4):
                        mm = pe.transpose(t_ps[:, bank, j * P:(j + 1) * P], so[:, 4 * m + j, :], c.ident[:])
                    mm.then_inc(turned[bank], 1)
                turn_out(HEADS, 1, TURNS["last out"])

            @block.vector
            def _(dve):
                def bias(i, g):
                    for m in range(2):
                        dve.wait_ge(scores_done[m], g + 1)
                        dve.tensor_reduce(nb[:, i % 2, m:m + 1], s_ps[:, m, 0:P * (i + 1)], AX.X, ALU.max,
                                          negate=True).then_inc(bias_ready[m], 1)

                def mix(i, g, kept):
                    w, s = P * (i + 1), i % 2
                    if kept:
                        dve.wait_ge(o_kept, g - 1)
                    for m in range(2):
                        dve.wait_ge(exp_done[m], g + 2)
                    dve.reciprocal(rl[:, s, :], l[:, s, :]).then_inc(step, 1)
                    dve.wait_ge(step, STEPS * g + 1)
                    dve.tensor_scalar(cf[:], rl[:, s, 1:2], l[:, s, 0:1], c.neglam[:], ALU.mult, ALU.mult).then_inc(step, 1)
                    dve.wait_ge(step, STEPS * g + 2)
                    dve.scalar_tensor_tensor(pr[:, s, 0, 0:w], pr[:, s, 1, 0:w], cf[:], pr[:, s, 0, 0:w], ALU.mult, ALU.add).then_inc(mixed, 1)

                def keep_o(i, g, s, turned_out=None):
                    dve.wait_ge(pv_done, g + 1)
                    if turned_out is not None:
                        dve.wait_ge(out_done, turned_out)
                    dve.tensor_scalar(o[:, s, i, :], o_ps[:, i % 2, 0:VD], rl[:, i % 2, 0:1], None, ALU.mult).then_inc(o_kept, 1)

                def sums(h):
                    dve.wait_ge(squared, h)
                    dve.tensor_reduce(ssq[:], square, AX.X, ALU.add).then_inc(sums_ready, 1)

                def inverse(h):
                    dve.wait_ge(root_ready, h)
                    dve.reciprocal(rstd[:], ssq[:]).then_inc(rstd_ready, 1)

                def out_lo(h, turns=TURNS["out"]):
                    for n, at_turn in enumerate(turns):
                        bank, _ = bank_use(0, at_turn)
                        part = slice(n * 512, (n + 1) * 512)
                        dve.wait_ge(out_hi, 2 * h - 1 + n)
                        dve.tensor_tensor(o_lo[:, ds(h - 1, 1), part].rearrange("p a b -> p (a b)"), t_ps[:, bank, :],
                                          o_hi[:, ds(h - 1, 1), part].rearrange("p a b -> p (a b)"), ALU.subtract).then_inc(t_kept[bank], 1)

                def body(it, first):
                    for s in range(2):
                        h = 2 * it + s
                        start = first and s == 0
                        for i in range(QT):
                            g = h * QT + i
                            bias(i, g)
                            if not (start and i < 2):
                                keep_o((i - 2) % QT, g - 2, s if i >= 2 else 1 - s, h - 1 if i == 2 and not first else None)
                            if i == INVERSE_STEP and not start:
                                inverse(h)
                            mix(i, g, not (start and i < 2))
                            if not start:
                                if i == SUMS_STEP:
                                    sums(h)
                                if i == OUT_STEP:
                                    out_lo(h)

                pair(body, dve)
                n = HEADS * QT
                keep_o(QT - 2, n - 2, 1)
                keep_o(QT - 1, n - 1, 1)
                dve.wait_ge(so_loaded, 16)
                norm_sums(dve, so, so_square, so_ssq, so_step)
                sums(HEADS)
                inverse(HEADS)
                head_norm(dve, so, so_ssq, so_rstd, so_step, so_root)
                dve.tensor_tensor(so, so, c.hn[:].unsqueeze(1).to_broadcast([P, HEADS, VD]), ALU.mult).then_inc(so_normed, 1)
                for m, at_turn in enumerate(TURNS["streams"]):
                    bank, _ = bank_use(0, at_turn)
                    heads = slice(4 * m, 4 * m + 4)
                    dve.wait_ge(so_hi, m + 1)
                    dve.tensor_tensor(o_lo[:, heads, PROMPT:TOK], t_ps[:, bank, :].rearrange("p (h n) -> p h n", h=4),
                                      o_hi[:, heads, PROMPT:TOK], ALU.subtract).then_inc(t_kept[bank], 1)
                out_lo(HEADS, TURNS["last out"])

            @block.scalar
            def _(act):
                def exponentials(i, g):
                    w, s = P * (i + 1), i % 2
                    for m in range(2):
                        act.wait_ge(bias_ready[m], g + 1)
                        act.activation(pr[:, s, m, 0:w], s_ps[:, m, 0:w], ACT.Exp, bias=nb[:, s, m:m + 1],
                                       accum_out=l[:, s, m:m + 1]).then_inc(exp_done[m], 1)

                def keep_at(i, h):
                    for n, at_turn in enumerate(TURNS[i]):
                        bank, before = bank_use(h, at_turn)
                        act.wait_ge(turned[bank], before + 1)
                        w = P * len(blocks(i, n))
                        act.activation(at[:, i % 2, n * 512:n * 512 + w], t_ps[:, bank, 0:w], ACT.Copy).then_inc(t_kept[bank], 1)
                    act.wait_ge(t_kept[bank], before + 2)
                    act.sem_inc(at_ready, 1)

                def root(h):
                    act.wait_ge(sums_ready, h)
                    act.activation(ssq[:], ssq[:], ACT.Sqrt, bias=c.eps[:], scale=1.0 / VD).then_inc(root_ready, 1)

                def keep_out(h, turns=TURNS["out"]):
                    for n, at_turn in enumerate(turns):
                        bank, before = bank_use(h, at_turn)
                        act.wait_ge(turned[bank], before + 1)
                        act.activation(o_hi[:, ds(h - 1, 1), n * 512:(n + 1) * 512].rearrange("p a b -> p (a b)"),
                                       t_ps[:, bank, :], ACT.Copy).then_inc(out_hi, 1)
                    act.wait_ge(out_hi, 2 * h)
                    act.sem_inc(out_done, 1)

                def body(it, first):
                    for s in range(2):
                        h = 2 * it + s
                        start = first and s == 0
                        for i in range(QT):
                            g = h * QT + i
                            exponentials(i, g)
                            if i == ROOT_STEP and not start:
                                root(h)
                            if not (start and i == 0):
                                keep_at((i - 1) % QT, h)
                            if i == OUT_STEP and not start:
                                keep_out(h)

                pair(body, act)
                keep_at(QT - 1, HEADS)
                act.wait_ge(so_step, 2)
                act.activation(so_ssq[:], so_ssq[:], ACT.Sqrt, bias=c.eps[:], scale=1.0 / VD).then_inc(so_root, 1)
                root(HEADS)
                for m, at_turn in enumerate(TURNS["streams"]):
                    bank, before = bank_use(HEADS, at_turn)
                    act.wait_ge(turned[bank], before + 1)
                    act.activation(o_hi[:, 4 * m:4 * m + 4, PROMPT:TOK], t_ps[:, bank, :].rearrange("p (h n) -> p h n", h=4),
                                   ACT.Copy).then_inc(so_hi, 1)
                keep_out(HEADS, TURNS["last out"])


def phase_mix_out(c, a_hi, a_lo, o_hi, o_lo):
    nc, io, sem = c.nc, c.io, c.sem
    with ExitStack() as mem:
        def sb(name, shape, dt=F32):
            return mem.enter_context(nc.sbuf_tensor(name, shape, dt))

        w_raw = sb("m_w_raw", [P, KT, P])
        w_hi = sb("m_w_hi", [P, KT, P], F32R)
        w_lo = sb("m_w_lo", [P, KT, P], F32R)
        e = sb("m_e", [P, TOK])
        x = sb("m_x", [P, NT, P])
        rows = sb("m_rows", [P, NT, P])
        z = mem.enter_context(nc.psum_tensor("m_z", [P, NB, 512], F32))
        tp = mem.enter_context(nc.psum_tensor("m_tp", [P, NB, 512], F32))
        load, split_chunk, products, z_done, z_kept, first_counts = weight_chunks(c, "m", w_raw, w_hi, w_lo)
        e_ready, e_turned = sem("m_e_ready"), sem("m_e_turned")
        x_loaded, rows_ready, rows_stored = sem("m_x_loaded"), sem("m_rows_ready"), sem("m_rows_stored")
        w = io.w_out.rearrange("(h k p) n -> h p k n", h=2, p=P)
        x_cols = io.x.rearrange("(t p) n -> p t n", p=P)
        x1_cols = io.x1.rearrange("(t p) n -> p t n", p=P)

        with nc.Block() as block:

            @block.sync
            def _(sp):
                with sp.Fori(0, KT) as n:
                    load(sp, n, lambda half: w[half, :, :, ds(n * P, P)])

            @block.gpsimd
            def _(pool):
                with pool.Fori(0, KT) as n:
                    split_chunk(pool, n)

            @block.tensor
            def _(pe):
                c.start_at_one(pe, *first_counts, rows_stored, rows_ready)
                def turn_back(m):
                    pe.wait_ge(e_ready, m + 1)
                    pe.wait_ge(rows_ready, m + 1)
                    for b in range(NB):
                        for j in range(NB):
                            mm = pe.transpose(tp[:, b, j * P:(j + 1) * P], e[:, (b * NB + j) * P:(b * NB + j + 1) * P],
                                              c.ident[:])
                        mm.then_inc(e_turned, 1)

                products(pe, 0, 0, z, a_hi, a_lo)
                products(pe, 0, 1, z, o_hi, o_lo)
                with pe.Fori(1, KT) as n:
                    products(pe, n, 0, z, a_hi, a_lo)
                    turn_back(n - 1)
                    products(pe, n, 1, z, o_hi, o_lo)
                turn_back(KT - 1)

            @block.vector
            def _(dve):
                def keep_e(n):
                    for b in range(NB):
                        dve.wait_ge(z_done[b], n + 2)
                        dve.tensor_copy(e[:, b * BLK:(b + 1) * BLK], z[:, b, 0:BLK]).then_inc(z_kept[b], 1)
                    dve.wait_ge(z_kept[2], n + 2)
                    dve.sem_inc(e_ready, 1)

                def add_rows(m):
                    dve.wait_ge(x_loaded, 16 * (m + 1))
                    dve.wait_ge(rows_stored, 16 * m + 1)
                    for b in range(NB):
                        dve.wait_ge(e_turned, NB * m + b + 1)
                        add = dve.tensor_tensor(rows[:, b * NB:(b + 1) * NB, :],
                                                tp[:, b, 0:NB * P].rearrange("p (a q) -> p a q", a=NB),
                                                x[:, b * NB:(b + 1) * NB, :], ALU.add)
                    add.then_inc(rows_ready, 1)

                keep_e(0)
                with dve.Fori(1, KT) as n:
                    add_rows(n - 1)
                    keep_e(n)
                add_rows(KT - 1)

            @block.scalar
            def _(act):
                with act.Fori(0, KT) as n:
                    act.wait_ge(rows_ready, n + 1)
                    act.dma_start(x[:], x_cols[:, :, ds(n * P, P)]).then_inc(x_loaded, 16)
                    act.wait_ge(rows_ready, n + 2)
                    act.dma_start(x1_cols[:, :, ds(n * P, P)], rows[:]).then_inc(rows_stored, 16)
                act.wait_ge(rows_stored, 16 * KT + 1)


UIN, UOUT = KT // 2, D // 512


def load_unit(c, eng, raw, raw_loaded, expert, u):
    r = u % RAW
    if u < UIN:
        w = c.io.w_ei.rearrange("e (u a p) n -> e u p a n", a=2, p=P)[ds(expert, 1), u, :, :, :].rearrange("e p a n -> (e p) a n")
    else:
        w = c.io.w_eo.rearrange("e (k p) (b n) -> e b p k n", p=P, n=512)[ds(expert, 1), u - UIN, :, :, :].rearrange("e p k n -> (e p) k n")
    eng.dma_start(raw[:, r, :].rearrange("p (a n) -> p a n", a=w.shape[1]), w).then_inc(raw_loaded[r], 16)


def phase_route(c, raw, raw_loaded):
    nc, io, sem = c.nc, c.io, c.sem
    NP = TOPK * NT
    with ExitStack() as mem:
        def sb(name, shape, dt=F32):
            return mem.enter_context(nc.sbuf_tensor(name, shape, dt))

        x = sb("r_x", [P, SL, D])
        g = sb("r_g", [P, D])
        xT = sb("r_xT", [P, KT, P])
        wr = sb("r_w", [P, KT, NR])
        br = sb("r_b", [P, NR])
        ssq, rstd = sb("r_ssq", [P, SL]), sb("r_rstd", [P, SL])
        junk = sb("r_junk", [P, D])
        lg = sb("r_lg", [P, NT, NR])
        tri, ones = sb("r_tri", [P, P]), sb("r_ones", [P, P])
        ints = sb("r_ints", [P, 64], I32)
        nums = sb("r_nums", [P, 64])
        thr_i, thr = sb("r_thr_i", [P, NT], I32), sb("r_thr", [P, NT])
        gm, gs, m1, m2, e1, e2, ex, wsum = (sb(f"r_{n}", [P, NT]) for n in ("gm", "gs", "m1", "m2", "e1", "e2", "ex", "wsum"))
        d4, x4, oh4 = (sb(f"r_{n}", [P, NT, GROUPS]) for n in ("d4", "x4", "oh4"))
        le, eq, oh1, oh2, both, carry, place = (sb(f"r_{n}", [P, NT, EXPERTS]) for n in ("le", "eq", "oh1", "oh2", "both", "carry", "place"))
        count, groups, end, start = (sb(f"r_{n}", [P, EXPERTS]) for n in ("count", "groups", "end", "start"))
        over = sb("r_over", [P, EXPERTS, NT])
        pos_f, pos = sb("r_pos_f", [P, NP]), sb("r_pos", [P, NP], U32)
        rows = sb("r_rows", [P, NP, 4], I32)
        empty = sb("r_empty", [P, 2 * SLOT_GROUPS, 4], I32)
        done_by, begun = (sb(f"r_{n}", [1, SLOT_GROUPS, EXPERTS]) for n in ("done_by", "begun"))
        first_slot, second_slots, group_f, paired = (sb(f"r_{n}", [1, SLOT_GROUPS]) for n in ("first_slot", "second_slots", "group_f", "paired"))
        slots_end = sb("r_slots_end", [1, EXPERTS])
        tp = mem.enter_context(nc.psum_tensor("r_tp", [P, 4, 512], F32))
        lg_ps = mem.enter_context(nc.psum_tensor("r_lg_ps", [P, 512], F32))
        cum_ps = mem.enter_context(nc.psum_tensor("r_cum", [P, 2, 512], F32))
        x_loaded, x_turned, h_stored = c.sems("r_x_loaded", SL), c.sems("r_x_turned", SL), c.sems("r_h_stored", SL)
        params, squared, root_done, rstd_done = sem("r_params"), sem("r_squared"), sem("r_root_done"), sem("r_rstd_done")
        h_ready, turned, kept_a, kept_v = sem("r_h_ready"), sem("r_turned"), sem("r_kept_a"), sem("r_kept_v")
        logits_done, logits_kept = sem("r_logits_done"), sem("r_logits_kept")
        consts, step, gaps_ready, exps_done = sem("r_consts"), sem("r_step"), sem("r_gaps_ready"), sem("r_exps_done")
        chosen, summed = sem("r_chosen"), sem("r_summed")
        plan_ready, emptied, slots_ready, slots_stored = sem("r_plan_ready"), sem("r_emptied"), sem("r_slots_ready"), sem("r_slots_stored")

        with nc.Block() as block:

            @block.sync
            def _(sp):
                sp.dma_start(g[:], io.norm_ffn.to_broadcast([P, D])).then_inc(params, 16)
                sp.dma_start(wr[:], io.w_router.rearrange("(k p) n -> p k n", p=P)).then_inc(params, 16)
                sp.dma_start(br[:], io.b_router.to_broadcast([P, NR])).then_inc(params, 16)
                with sp.Fori(0, NT // SL) as i:
                    for s in range(SL):
                        sp.wait_ge(x_turned[s], i + 1)
                        c.hold(sp)
                        sp.wait_ge(h_stored[s], 16 * i + 1)
                        c.hold(sp)
                        sp.dma_start(x[:, s, :], io.x1[ds((i * SL + s) * P, P), :]).then_inc(x_loaded[s], 16)
                sp.wait_ge(plan_ready, 1)
                first = sp.value_load(c.group_expert[0:1, 0:1], min_val=0, max_val=EXPERTS - 1)
                for u in range(AHEAD):
                    load_unit(c, sp, raw, raw_loaded, first, u)

            @block.gpsimd
            def _(pool):
                pool.memset(tri[:], 1.0).then_inc(consts, 1)
                pool.memset(ones[:], 1.0).then_inc(consts, 1)
                pool.memset(empty[:], 0).then_inc(consts, 1)
                pool.memset(rows[:], 0).then_inc(consts, 1)
                pool.iota(ints[:], pattern=[[1, 64]], base=0, channel_multiplier=0).then_inc(consts, 1)
                pool.iota(thr_i[:], pattern=[[GROUP, NT]], base=0, channel_multiplier=0).then_inc(consts, 1)
                pool.wait_ge(consts, 6)
                pool.affine_select(out=tri[:], in_=tri[:], compare_op=ALU.is_gt, fill=0.0, base=0, pattern=[[1, P]],
                                   channel_multiplier=-1).then_inc(consts, 1)
                pool.memset(empty[:, :, 0:2], NO_ROW).then_inc(consts, 1)
                for k in range(TOPK):
                    pool.iota(rows[:, k * NT:(k + 1) * NT, 0], pattern=[[P, NT]], base=0, channel_multiplier=1).then_inc(consts, 1)
                    pool.iota(rows[:, k * NT:(k + 1) * NT, 1], pattern=[[P, NT]], base=k * TOK, channel_multiplier=1).then_inc(consts, 1)
                pool.wait_ge(consts, 12)
                pool.dma_start(io.slots.rearrange("(p t) f -> p (t f)", p=P), empty[:].rearrange("p t f -> p (t f)")).then_inc(emptied, 16)
                pool.wait_ge(emptied, 16)
                pool.wait_ge(slots_ready, 1)
                for n in range(NP):
                    pool.indirect_dma_start(out=io.slots, out_offset=bass.IndirectOffsetOnAxis(ap=pos[:, n:n + 1], axis=0),
                                            in_=rows[:, n, :], in_offset=None).then_inc(slots_stored, 16)
                pool.wait_ge(slots_stored, 16 * NP)

            @block.scalar
            def _(act):
                def root(s, i, t):
                    act.wait_ge(x_loaded[s], 16 * (i + 1))
                    act.wait_ge(rstd_done, t + 1)
                    act.activation(junk[:], x[:, s, :], ACT.Square, accum_out=ssq[:, s:s + 1]).then_inc(squared, 1)
                    act.wait_ge(squared, t + 1)
                    act.activation(ssq[:, s:s + 1], ssq[:, s:s + 1], ACT.Sqrt, bias=c.eps[:], scale=1.0 / D).then_inc(root_done, 1)

                def keep(s, t):
                    act.wait_ge(h_ready, t + 1)
                    act.dma_start(io.h2[ds(t * P, P), :], x[:, s, :]).then_inc(h_stored[s], 16)
                    for q in (0, 2):
                        act.wait_ge(turned, 4 * t + q + 1)
                        act.activation(xT[:, 4 * q:4 * q + 4, :], tp[:, q, :].rearrange("p (a b) -> p a b", a=4),
                                       ACT.Copy).then_inc(kept_a, 1)

                one_ahead(act, root, keep)
                act.wait_ge(gaps_ready, 1)
                act.activation(x4[:], d4[:], ACT.Exp).then_inc(exps_done, 1)
                act.wait_ge(gaps_ready, 2)
                act.activation(ex[:], wsum[:], ACT.Exp).then_inc(exps_done, 1)
                for s in range(SL):
                    act.wait_ge(h_stored[s], 16 * (NT // SL) + 1)

            @block.tensor
            def _(pe):
                c.start_at_one(pe, *x_turned, *h_stored, rstd_done, logits_kept)
                pe.wait_ge(params, 48)
                with pe.Fori(0, NT // SL) as i:
                    for s in range(SL):
                        t = i * SL + s
                        pe.wait_ge(h_ready, t + 1)
                        for q in range(4):
                            for j in range(4):
                                k = 4 * q + j
                                mm = pe.transpose(tp[:, q, j * P:(j + 1) * P], x[:, s, k * P:(k + 1) * P], c.ident[:])
                            mm.then_inc(turned, 1)
                        pe.wait_ge(turned, 4 * t + 4)
                        pe.sem_inc(x_turned[s], 1)
                        pe.wait_ge(kept_a, 2 * t + 2)
                        pe.wait_ge(kept_v, 2 * t + 2)
                        pe.wait_ge(logits_kept, t + 1)
                        for k in range(KT):
                            mm = pe.matmul(lg_ps[:, 0:NR], xT[:, k, :], wr[:, k, :], start=(k == 0), stop=(k == KT - 1))
                        mm.then_inc(logits_done, 1)
                pe.wait_ge(chosen, 1)
                pe.wait_ge(consts, 7)
                n = NT * EXPERTS
                pe.matmul(cum_ps[:, 0, 0:n], tri[:], both[:].rearrange("p t e -> p (t e)"), start=True, stop=True)
                pe.matmul(cum_ps[:, 1, 0:n], ones[:], both[:].rearrange("p t e -> p (t e)"), start=True, stop=True).then_inc(summed, 1)

            @block.vector
            def _(dve):
                dve.wait_ge(params, 48)

                def scale(s, i, t):
                    dve.wait_ge(root_done, t + 1)
                    dve.reciprocal(rstd[:, s:s + 1], ssq[:, s:s + 1]).then_inc(rstd_done, 1)
                    dve.wait_ge(rstd_done, t + 2)
                    dve.scalar_tensor_tensor(x[:, s, :], x[:, s, :], rstd[:, s:s + 1], g[:], ALU.mult, ALU.mult).then_inc(h_ready, 1)

                def keep(s, t):
                    for q in (1, 3):
                        dve.wait_ge(turned, 4 * t + q + 1)
                        dve.tensor_copy(xT[:, 4 * q:4 * q + 4, :], tp[:, q, :].rearrange("p (a b) -> p a b", a=4)).then_inc(kept_v, 1)
                    dve.wait_ge(logits_done, t + 1)
                    dve.tensor_tensor(lg[:, ds(t, 1), :].rearrange("p a b -> p (a b)"), lg_ps[:, 0:NR], br[:], ALU.add).then_inc(logits_kept, 1)

                one_ahead(dve, scale, keep)

                steps = [0]

                def then(ins):
                    steps[0] += 1
                    ins.then_inc(step, 1)
                    dve.wait_ge(step, steps[0])

                def tt(out, a, b, op):
                    then(dve.tensor_tensor(out, a, b, op))

                def over_last(v, n):
                    return v.unsqueeze(2).to_broadcast([P, NT, n])

                def over_tiles(v, n):
                    return v.unsqueeze(1).to_broadcast([P, NT, n])

                dve.wait_ge(logits_kept, NT + 1)
                dve.wait_ge(consts, 12)
                then(dve.tensor_copy(nums[:], ints[:]))
                then(dve.tensor_copy(thr[:], thr_i[:]))
                e_no = nums[:, 0:EXPERTS]

                def first_best(best, index, onehot, scores, n):
                    then(dve.tensor_reduce(best, scores, AX.X, ALU.max))
                    tt(onehot, scores, over_last(best, n), ALU.is_equal)
                    then(dve.tensor_scalar(onehot, onehot, -64.0, 64.0, ALU.mult, ALU.add))
                    tt(onehot, onehot, over_tiles(e_no[:, 0:n], n), ALU.add)
                    then(dve.tensor_reduce(index, onehot, AX.X, ALU.min))
                    tt(onehot, over_tiles(e_no[:, 0:n], n), over_last(index, n), ALU.is_equal)

                first_best(gm[:], e1[:], oh4[:], lg[:, :, 0:GROUPS], GROUPS)
                dve.tensor_tensor(d4[:], lg[:, :, 0:GROUPS], over_last(gm[:], GROUPS), ALU.subtract).then_inc(gaps_ready, 1)
                then(dve.tensor_scalar(oh4[:], oh4[:], -1.0, BIG, ALU.add, ALU.mult))
                tt(le[:].rearrange("p t (g e) -> p t g e", g=GROUPS), lg[:, :, GROUPS:NR].rearrange("p t (g e) -> p t g e", g=GROUPS),
                   oh4[:].unsqueeze(3).to_broadcast([P, NT, GROUPS, PER]), ALU.add)
                first_best(m1[:], e1[:], oh1[:], le[:], EXPERTS)
                then(dve.scalar_tensor_tensor(le[:], oh1[:], -2 * BIG, le[:], ALU.mult, ALU.add))
                first_best(m2[:], e2[:], oh2[:], le[:], EXPERTS)
                dve.tensor_tensor(wsum[:], m2[:], m1[:], ALU.subtract).then_inc(gaps_ready, 1)
                dve.tensor_tensor(both[:], oh1[:], oh2[:], ALU.add).then_inc(chosen, 1)
                dve.wait_ge(exps_done, 2)
                then(dve.tensor_reduce(gs[:], x4[:], AX.X, ALU.add))
                then(dve.tensor_scalar(wsum[:], ex[:], 1.0, None, ALU.add))
                tt(gs[:], gs[:], wsum[:], ALU.mult)
                wv = rows[:].bitcast(F32)
                then(dve.reciprocal(gs[:], gs[:]))
                then(dve.tensor_copy(wv[:, 0:NT, 2], gs[:]))
                tt(wv[:, NT:NP, 2], gs[:], ex[:], ALU.mult)
                dve.wait_ge(summed, 1)
                before = cum_ps[:, 0, 0:NT * EXPERTS].rearrange("p (t e) -> p t e", t=NT)
                total = cum_ps[:, 1, 0:NT * EXPERTS].rearrange("p (t e) -> p t e", t=NT)
                then(dve.memset(carry[:, 0, :], 0.0))
                for t in range(1, NT):
                    tt(carry[:, t, :], carry[:, t - 1, :], total[:, t - 1, :], ALU.add)
                tt(count[:], carry[:, NT - 1, :], total[:, NT - 1, :], ALU.add)
                tt(over[:], count[:].unsqueeze(2).to_broadcast([P, EXPERTS, NT]), thr[:].unsqueeze(1).to_broadcast([P, EXPERTS, NT]), ALU.is_gt)
                then(dve.tensor_reduce(groups[:], over[:], AX.X, ALU.add))
                then(dve.tensor_tensor_scan(end[:], ones[:, 0:EXPERTS], groups[:], 0.0, ALU.mult, ALU.add))
                tt(start[:], end[:], groups[:], ALU.subtract)
                then(dve.tensor_scalar(start[:], start[:], float(GROUP), None, ALU.mult))
                tt(place[:], carry[:], before, ALU.add)
                tt(place[:], place[:], over_tiles(start[:], EXPERTS), ALU.add)
                tt(eq[:], place[:], oh1[:], ALU.mult)
                then(dve.tensor_reduce(pos_f[:, 0:NT], eq[:], AX.X, ALU.add))
                tt(eq[:], place[:], oh2[:], ALU.mult)
                then(dve.tensor_reduce(pos_f[:, NT:NP], eq[:], AX.X, ALU.add))
                dve.tensor_copy(pos[:], pos_f[:]).then_inc(slots_ready, 1)
                def by_group(v):
                    return v.unsqueeze(2).to_broadcast([1, SLOT_GROUPS, EXPERTS])

                def by_expert(v):
                    return v.unsqueeze(1).to_broadcast([1, SLOT_GROUPS, EXPERTS])

                group_no = nums[0:1, 0:SLOT_GROUPS]
                tt(done_by[:], by_expert(end[0:1, :]), by_group(group_no), ALU.is_le)
                then(dve.tensor_reduce(group_f[:], done_by[:], AX.X, ALU.add))
                then(dve.tensor_scalar(c.group_expert[:], group_f[:], EXPERTS - 1.0, None, ALU.min))
                then(dve.tensor_copy(c.group_count[:], end[0:1, EXPERTS - 1:EXPERTS]))
                dve.sem_inc(plan_ready, 1)
                then(dve.tensor_scalar(first_slot[:], group_no, float(GROUP), None, ALU.mult))
                then(dve.tensor_scalar(second_slots[:], first_slot[:], float(P), None, ALU.add))
                tt(slots_end[:], start[0:1, :], count[0:1, :], ALU.add)
                tt(begun[:], by_expert(start[0:1, :]), by_group(first_slot[:]), ALU.is_le)
                tt(done_by[:], by_expert(slots_end[:]), by_group(second_slots[:]), ALU.is_gt)
                tt(begun[:], begun[:], done_by[:], ALU.mult)
                then(dve.tensor_reduce(paired[:], begun[:], AX.X, ALU.add))
                then(dve.tensor_tensor_scan(group_f[:], ones[0:1, 0:SLOT_GROUPS], paired[:], 0.0, ALU.mult, ALU.add))
                tt(group_f[:], group_f[:], paired[:], ALU.subtract)
                then(dve.tensor_copy(c.group_pairs[:], group_f[:]))


def phase_experts(c, raw, raw_loaded):
    nc, io, sem = c.nc, c.io, c.sem
    UN = UIN + UOUT
    KE = DE // P
    SPL = 4
    with ExitStack() as mem:
        def sb(name, shape, dt=F32):
            return mem.enter_context(nc.sbuf_tensor(name, shape, dt))

        w_hi = sb("e_w_hi", [P, SPL, D], F32R)
        w_lo = sb("e_w_lo", [P, SPL, D], F32R)
        x = sb("e_x", [P, 2, D])
        xT_hi, xT_lo = sb("e_xT_hi", [P, 2, KT, P], F32R), sb("e_xT_lo", [P, 2, KT, P], F32R)
        sg, act_rows = sb("e_sg", [P, 2, DE]), sb("e_act", [P, 2, DE])
        aT_hi, aT_lo = sb("e_aT_hi", [P, 2, KE, P], F32R), sb("e_aT_lo", [P, 2, KE, P], F32R)
        y = sb("e_y", [P, 2, D])
        table = sb("e_table", [P, 2 * SLOT_GROUPS, 4], I32)
        gather_idx, row_idx = sb("e_gather_idx", [P, 2], I32), sb("e_row_idx", [P, 2], I32)
        wcol = sb("e_wcol", [P, 2])
        act_warm, warmed = sb("e_act_warm", [P, 1]), sem("e_warmed")
        gu_ps = mem.enter_context(nc.psum_tensor("e_gu", [P, 4, 512], F32))
        t_ps = mem.enter_context(nc.psum_tensor("e_t", [P, 2, 512], F32))
        y_ps = mem.enter_context(nc.psum_tensor("e_y_ps", [P, 2, 512], F32))
        first_loaded, table_loaded, x_cleared = sem("e_first_loaded"), sem("e_table_loaded"), sem("e_x_cleared")
        lo_done = c.sems("e_lo_done", RAW)
        hi_done, used = sem("e_hi_done"), c.sems("e_used", SPL)
        idx_ready, row_idx_ready = sem("e_idx_ready"), sem("e_row_idx_ready")
        x_loaded, x_turned, x_hi, x_kept = sem("e_x_loaded"), sem("e_x_turned"), sem("e_x_hi"), sem("e_x_kept")
        a_turned, a_hi, a_kept = sem("e_a_turned"), sem("e_a_hi"), sem("e_a_kept")
        silu_done, act_ready = sem("e_silu_done"), sem("e_act_ready")
        first_done, y_kept, y_stored = sem("e_first_done"), c.sems("e_y_kept", 2), sem("e_y_stored")
        y_free = sem("e_y_free")

        def group_count(eng):
            return eng.value_load(c.group_count[0:1, 0:1], min_val=1, max_val=MAXG)

        def groups(eng, count, body):
            with eng.Fori(0, MAXG) as g:
                with eng.If(g < count):
                    body(g)

        def pairs(eng, g):
            return eng.value_load(c.group_pairs[0:1, ds(g, 1)], min_val=0, max_val=MAXG)

        def by_size(eng, before, after, part):
            with eng.If(before < after):
                part(2)
            with eng.If(before == after):
                part(1)

        with nc.Block() as block:

            @block.sync
            def _(sp):
                def load(g, ex, u):
                    r = u % RAW
                    sp.wait_ge(lo_done[r], 2 * g + u // RAW + 1)
                    load_unit(c, sp, raw, raw_loaded, ex, u)

                slot_tiles = io.slots.rearrange("(t p) f -> p t f", p=P)
                sp.dma_start(table[:, 0:4, :], slot_tiles[:, 0:4, :]).then_inc(first_loaded, 16)
                sp.dma_start(table[:, 4:, :], slot_tiles[:, 4:, :]).then_inc(table_loaded, 16)
                first = sp.value_load(c.group_expert[0:1, 0:1], min_val=0, max_val=EXPERTS - 1)
                for u in range(AHEAD, RAW):
                    load_unit(c, sp, raw, raw_loaded, first, u)

                count = group_count(sp)

                def body(g):
                    ex = sp.value_load(c.group_expert[0:1, ds(g, 1)], min_val=0, max_val=EXPERTS - 1)
                    for u in range(RAW, UN):
                        load(g, ex, u)
                    nx = sp.value_load(c.group_expert[0:1, ds(g + 1, 1)], min_val=0, max_val=EXPERTS - 1)
                    for u in range(AHEAD):
                        load(g + 1, nx, u)
                    with sp.If(g + 1 < count):
                        for u in range(AHEAD, RAW):
                            load(g + 1, nx, u)

                groups(sp, count, body)

            @block.gpsimd
            def _(pool):
                def gather_tile(r):
                    pool.indirect_dma_start(out=x[:, r, :], out_offset=None, in_=io.h2, in_offset=bass.IndirectOffsetOnAxis(
                        ap=gather_idx[:, r:r + 1].bitcast(U32), axis=0), bounds_check=TOK - 1, oob_is_err=False).then_inc(x_loaded, 16)

                def gather(g, before, after):
                    pool.wait_ge(idx_ready, g + 1)
                    c.hold(pool)
                    gather_tile(0)
                    with pool.If(before < after):
                        gather_tile(1)

                pool.memset(x[:], 0.0).then_inc(x_cleared, 1)
                pool.wait_ge(x_cleared, 1)
                count = group_count(pool)
                p0, p1, p2 = (pairs(pool, g) for g in range(3))
                gather(0, p0, p1)
                pool.wait_ge(x_turned, 4 * p1 + 4)
                gather(1, p1, p2)

                def body(g):
                    here, nx, nx2, nx3 = (pairs(pool, g + i) for i in range(4))
                    pool.wait_ge(x_turned, 4 * (g + nx2 + 2))
                    gather(g + 2, nx2, nx3)

                    def scatter(n):
                        for eng in range(2):
                            pool.wait_ge(y_kept[eng], 2 * (g + here + n) + 1)
                        c.hold(pool)
                        for r in range(n):
                            pool.indirect_dma_start(out=io.expert_rows, out_offset=bass.IndirectOffsetOnAxis(
                                ap=row_idx[:, r:r + 1].bitcast(U32), axis=0), in_=y[:, r, :], in_offset=None,
                                bounds_check=TOPK * TOK - 1, oob_is_err=False).then_inc(y_stored, 16)

                    by_size(pool, here, nx, scatter)
                    pool.wait_ge(y_stored, 16 * (g + nx + 1))
                    pool.sem_inc(y_free, 1)

                groups(pool, count, body)
                all_pairs = pairs(pool, MAXG)
                pool.wait_ge(y_stored, 16 * (count + all_pairs))
                pool.wait_ge(x_loaded, 16 * (count + all_pairs + 2))

            @block.tensor
            def _(pe):
                c.start_at_one(pe, *lo_done, act_ready, *y_kept, *used, y_free)

                def turn_rows(tile, r, quads):
                    for q in quads:
                        if q >= 2:
                            pe.wait_ge(x_kept, 4 * tile + q - 1)
                        for j in range(4):
                            k = 4 * q + j
                            mm = pe.transpose(t_ps[:, q % 2, j * P:(j + 1) * P], x[:, r, k * P:(k + 1) * P], c.ident[:])
                        mm.then_inc(x_turned, 1)

                count, p1 = group_count(pe), pairs(pe, 1)
                pe.wait_ge(x_loaded, 16 * p1 + 16)
                turn_rows(0, 0, range(4))
                with pe.If(p1 > 0):
                    pe.wait_ge(x_kept, 4)
                    turn_rows(1, 1, range(4))

                def body(g):
                    here, nx, nx2 = (pairs(pe, g + i) for i in range(3))

                    def gate_up(n):
                        pe.wait_ge(x_kept, 4 * (g + here + n))
                        pe.wait_ge(act_ready, g + here + 1)
                        for u in range(UIN):
                            s = u % SPL
                            pe.wait_ge(lo_done[u % RAW], 2 * g + u // RAW + 2)
                            for a in range(2):
                                k = 2 * u + a
                                for r in range(n):
                                    for x_part, w_part, last in ((xT_hi, w_hi, False), (xT_hi, w_lo, False), (xT_lo, w_hi, True)):
                                        for b in range(2):
                                            mm = pe.matmul(gu_ps[:, 2 * r + b, :], x_part[:, r, k, :],
                                                           w_part[:, s, a * 1024 + b * 512:a * 1024 + b * 512 + 512],
                                                           start=(k == 0 and x_part is xT_hi and w_part is w_hi), stop=(k == KT - 1 and last))
                            mm.then_inc(used[s], 1)
                        pe.wait_ge(x_loaded, 16 * (g + nx2 + 2))
                        tile = g + here + n
                        turn_rows(tile, 0, (0, 1))
                        for r in range(n):
                            pe.wait_ge(act_ready, g + here + r + 2)
                            pe.wait_ge(y_kept[r], 2 * (g + here) + 1)
                            for k in range(KE):
                                mm = pe.transpose(y_ps[:, r, k * P:(k + 1) * P], act_rows[:, r, k * P:(k + 1) * P], c.ident[:])
                            mm.then_inc(a_turned, 1)
                        turn_rows(tile, 0, (2, 3))

                    by_size(pe, here, nx, gate_up)
                    with pe.If(nx < nx2):
                        tile = g + nx + 2
                        pe.wait_ge(x_kept, 4 * tile)
                        turn_rows(tile, 1, range(4))

                    def out_rows(n):
                        for b in range(UOUT):
                            u = UIN + b
                            s = u % SPL
                            pe.wait_ge(lo_done[u % RAW], 2 * g + u // RAW + 2)
                            for r in range(n):
                                m = b * n + r
                                if b == 0:
                                    pe.wait_ge(a_kept, g + here + r + 1)
                                pe.wait_ge(y_kept[m % 2], 2 * (g + here) + m // 2 + 1)
                                for k in range(KE):
                                    for a_part, w_part, last in ((aT_hi, w_hi, False), (aT_hi, w_lo, False), (aT_lo, w_hi, True)):
                                        mm = pe.matmul(y_ps[:, m % 2, :], a_part[:, r, k, :], w_part[:, s, k * 512:(k + 1) * 512],
                                                       start=(k == 0 and a_part is aT_hi and w_part is w_hi), stop=(k == KE - 1 and last))
                                mm.then_inc(used[s] if r == n - 1 else first_done, 1)

                    by_size(pe, here, nx, out_rows)

                groups(pe, count, body)

            def unit_used(eng, g, u):
                eng.wait_ge(used[u % SPL], 3 * g + u // SPL + 2)

            def keep_y(eng, which, g, here, n, b, keep):
                for r in range(n):
                    m = b * n + r
                    if m % 2 == which:
                        if r == n - 1:
                            unit_used(eng, g, UIN + b)
                        else:
                            eng.wait_ge(first_done, 4 * here + b + 1)
                        keep(y[:, r, b * 512:(b + 1) * 512], y_ps[:, m % 2, :], wcol[:, r:r + 1]).then_inc(y_kept[which], 1)

            def quad(part, r, q):
                return part[:, r, 4 * q:4 * q + 4, :]

            def bank(ps, b):
                return ps[:, b, :].rearrange("p (a b) -> p a b", a=4)

            @block.scalar
            def _(act):
                def split_hi(g, u):
                    r, s = u % RAW, u % SPL
                    act.wait_ge(raw_loaded[r], 32 * g + 16 * (u // RAW) + 16)
                    act.wait_ge(used[s], 3 * g + u // SPL + 1)
                    act.activation(w_hi[:, s, :], raw[:, r, :], ACT.Copy).then_inc(hi_done, 1)

                def keep_rows_hi(tile, r, quads):
                    for q in quads:
                        act.wait_ge(x_turned, 4 * tile + q + 1)
                        act.activation(quad(xT_hi, r, q), bank(t_ps, q % 2), ACT.Copy).then_inc(x_hi, 1)

                count, p1 = group_count(act), pairs(act, 1)
                act.activation(act_warm[:], c.eps[:], ACT.Silu).then_inc(warmed, 1)
                for u in range(AHEAD):
                    split_hi(0, u)
                keep_rows_hi(0, 0, range(4))
                with act.If(p1 > 0):
                    keep_rows_hi(1, 1, range(4))

                def body(g):
                    here, nx, nx2 = (pairs(act, g + i) for i in range(3))
                    for u in range(AHEAD, UN - 1):
                        split_hi(g, u)
                    unit_used(act, g, UIN - 1)
                    c.hold(act)

                    def activate(n):
                        for r in range(n):
                            act.activation(sg[:, r, :], gu_ps[:, 2 * r, :], ACT.Silu).then_inc(silu_done, 1)
                        keep_rows_hi(g + here + n, 0, (0, 1))
                        for r in range(n):
                            act.wait_ge(a_turned, g + here + r + 1)
                            act.activation(aT_hi[:, r], bank(y_ps, r), ACT.Copy).then_inc(a_hi, 1)
                        keep_rows_hi(g + here + n, 0, (2, 3))

                    by_size(act, here, nx, activate)
                    with act.If(nx < nx2):
                        keep_rows_hi(g + nx + 2, 1, range(4))
                    split_hi(g, UN - 1)
                    act.wait_ge(y_free, g + 1)
                    act.wait_ge(row_idx_ready, g + 1)
                    c.hold(act)

                    def keep(n):
                        for b in range(UOUT):
                            keep_y(act, 0, g, here, n, b, lambda out, ps, w: act.activation(out, ps, ACT.Copy, scale=w))
                            split_hi(g + 1, b)

                    by_size(act, here, nx, keep)

                groups(act, count, body)

            @block.vector
            def _(dve):
                def split_lo(g, u):
                    r, s = u % RAW, u % SPL
                    dve.wait_ge(hi_done, UN * g + u + 1)
                    dve.tensor_tensor(w_lo[:, s, :], raw[:, r, :], w_hi[:, s, :], ALU.subtract).then_inc(lo_done[r], 1)

                def keep_rows_lo(tile, r, quads):
                    for q in quads:
                        dve.wait_ge(x_hi, 4 * tile + q + 1)
                        dve.tensor_tensor(quad(xT_lo, r, q), bank(t_ps, q % 2), quad(xT_hi, r, q), ALU.subtract).then_inc(x_kept, 1)

                def field(g, f):
                    return table[:, ds(2 * g, 2), f:f + 1].rearrange("p a b -> p (a b)")

                count, p1 = group_count(dve), pairs(dve, 1)
                dve.wait_ge(first_loaded, 16)
                dve.tensor_copy(gather_idx[:], field(0, 0)).then_inc(idx_ready, 1)
                for u in range(AHEAD):
                    split_lo(0, u)
                dve.wait_ge(table_loaded, 16)
                dve.wait_ge(x_loaded, 16 * p1 + 16)
                dve.tensor_copy(gather_idx[:], field(1, 0)).then_inc(idx_ready, 1)
                keep_rows_lo(0, 0, range(4))
                with dve.If(p1 > 0):
                    keep_rows_lo(1, 1, range(4))

                def body(g):
                    here, nx, nx2 = (pairs(dve, g + i) for i in range(3))
                    for u in range(AHEAD, UN - 1):
                        split_lo(g, u)

                    def activate(n):
                        for r in range(n):
                            dve.wait_ge(silu_done, g + here + r + 1)
                            dve.tensor_tensor(act_rows[:, r, :], sg[:, r, :], gu_ps[:, 2 * r + 1, :], ALU.mult).then_inc(act_ready, 1)
                        keep_rows_lo(g + here + n, 0, (0, 1))
                        for r in range(n):
                            dve.wait_ge(a_hi, g + here + r + 1)
                            dve.tensor_tensor(aT_lo[:, r], bank(y_ps, r), aT_hi[:, r], ALU.subtract).then_inc(a_kept, 1)
                        keep_rows_lo(g + here + n, 0, (2, 3))

                    by_size(dve, here, nx, activate)
                    with dve.If(nx < nx2):
                        keep_rows_lo(g + nx + 2, 1, range(4))
                    dve.wait_ge(x_loaded, 16 * (g + nx2 + 2))
                    dve.tensor_copy(gather_idx[:], field(g + 2, 0)).then_inc(idx_ready, 1)
                    dve.wait_ge(y_free, g + 1)
                    dve.wait_ge(y_kept[0], 2 * (g + here) + 1)
                    dve.tensor_copy(row_idx[:], field(g, 1))
                    dve.tensor_copy(wcol[:].bitcast(I32), field(g, 2)).then_inc(row_idx_ready, 1)
                    split_lo(g, UN - 1)
                    dve.wait_ge(row_idx_ready, g + 1)
                    c.hold(dve)

                    def keep(n):
                        for b in range(UOUT):
                            keep_y(dve, 1, g, here, n, b, lambda out, ps, w: dve.tensor_scalar(out, ps, w, None, ALU.mult))
                            split_lo(g + 1, b)

                    by_size(dve, here, nx, keep)

                groups(dve, count, body)


def phase_final(c):
    nc, io, sem = c.nc, c.io, c.sem
    with ExitStack() as mem:
        def sb(name, shape, dt=F32):
            return mem.enter_context(nc.sbuf_tensor(name, shape, dt))

        x, r0, r1 = (sb(f"f_{n}", [P, SL, D]) for n in ("x", "r0", "r1"))
        g, junk = sb("f_g", [P, D]), sb("f_junk", [P, D])
        ssq, rstd = sb("f_ssq", [P, SL]), sb("f_rstd", [P, SL])
        loaded, stored = c.sems("f_loaded", SL), c.sems("f_stored", SL)
        g_loaded, step, summed = sem("f_g_loaded"), sem("f_step"), sem("f_summed")
        squared, root_done, rstd_done, ready = sem("f_squared"), sem("f_root_done"), sem("f_rstd_done"), sem("f_ready")
        with nc.Block() as block:

            @block.sync
            def _(sp):
                sp.dma_start(g[:], io.norm_final.to_broadcast([P, D])).then_inc(g_loaded, 16)
                with sp.Fori(0, NT // SL) as i:
                    for s in range(SL):
                        t = i * SL + s
                        sp.wait_ge(stored[s], 16 * i + 1)
                        sp.dma_start(x[:, s, :], io.x1[ds(t * P, P), :]).then_inc(loaded[s], 16)
                        sp.dma_start(r0[:, s, :], io.expert_rows[ds(t * P, P), :]).then_inc(loaded[s], 16)
                        sp.dma_start(r1[:, s, :], io.expert_rows[ds(t * P + TOK, P), :]).then_inc(loaded[s], 16)

            @block.vector
            def _(dve):
                def add(s, i, t):
                    dve.wait_ge(loaded[s], 48 * (i + 1))
                    dve.tensor_tensor(r0[:, s, :], r0[:, s, :], r1[:, s, :], ALU.add).then_inc(step, 1)
                    dve.wait_ge(step, t + 1)
                    dve.tensor_tensor(x[:, s, :], x[:, s, :], r0[:, s, :], ALU.add).then_inc(summed, 1)

                def scale(s, t):
                    dve.wait_ge(root_done, t + 1)
                    dve.reciprocal(rstd[:, s:s + 1], ssq[:, s:s + 1]).then_inc(rstd_done, 1)
                    dve.wait_ge(rstd_done, t + 1)
                    dve.scalar_tensor_tensor(x[:, s, :], x[:, s, :], rstd[:, s:s + 1], g[:], ALU.mult, ALU.mult).then_inc(ready, 1)

                dve.wait_ge(g_loaded, 16)
                add(0, 0, 0)
                with dve.Fori(0, NT // SL - 1) as i:
                    for s in range(SL):
                        t = i * SL + s
                        add((s + 1) % SL, i + (s + 1) // SL, t + 1)
                        scale(s, t)
                for s in range(SL):
                    t = NT - SL + s
                    if s + 1 < SL:
                        add(s + 1, NT // SL - 1, t + 1)
                    scale(s, t)

            @block.scalar
            def _(act):
                c.start_at_one(act, *stored)
                with act.Fori(0, NT // SL) as i:
                    for s in range(SL):
                        t = i * SL + s
                        act.wait_ge(summed, t + 1)
                        act.activation(junk[:], x[:, s, :], ACT.Square, accum_out=ssq[:, s:s + 1]).then_inc(squared, 1)
                        act.wait_ge(squared, t + 1)
                        act.activation(ssq[:, s:s + 1], ssq[:, s:s + 1], ACT.Sqrt, bias=c.eps[:], scale=1.0 / D).then_inc(root_done, 1)
                        act.wait_ge(ready, t + 1)
                        act.dma_start(io.y_all[ds(t * P, P), :], x[:, s, :]).then_inc(stored[s], 16)
                for s in range(SL):
                    act.wait_ge(stored[s], 16 * (NT // SL) + 1)



class Dram:

    def __init__(self, x, cache_k, cache_v, small, norm_mix, w_in, lam, head_norm, w_out, norm_ffn, w_router, b_router,
                 w_ei, w_eo, norm_final, y_all, k_all, v_all, conv_all):
        self.x, self.cache_k, self.cache_v, self.small = x, cache_k, cache_v, small
        self.norm_mix, self.w_in, self.lam, self.head_norm, self.w_out = norm_mix, w_in, lam, head_norm, w_out
        self.norm_ffn, self.w_router, self.b_router, self.w_ei, self.w_eo = norm_ffn, w_router, b_router, w_ei, w_eo
        self.norm_final, self.y_all, self.k_all, self.v_all, self.conv_all = norm_final, y_all, k_all, v_all, conv_all


def build(nc, io):
    io.chunks = nc.dram_tensor("chunks", (3 * CH, P, TOK), F32).ap()
    io.o_new = nc.dram_tensor("o_new", (STREAMS * NEW, DC), F32).ap()
    io.x1 = nc.dram_tensor("x1", (TOK, D), F32).ap()
    io.h2 = nc.dram_tensor("h2", (TOK, D), F32).ap()
    io.slots = nc.dram_tensor("slots", (SLOT_GROUPS * GROUP, 4), I32).ap()
    io.expert_rows = nc.dram_tensor("expert_rows", (TOPK * TOK, D), F32).ap()
    with ExitStack() as stack:
        c = Ctx(nc, io)

        def sb(name, shape, dt=F32):
            return stack.enter_context(nc.sbuf_tensor(name, shape, dt))

        c.ident = sb("ident", [P, P])
        c.eps = sb("eps", [P, 1])
        c.taps = sb("taps", [P, CH, 2 * STREAMS + 3])
        c.neglam = sb("neglam", [P, 1])
        c.hn = sb("hn", [P, VD])
        c.group_expert = sb("group_expert", [1, SLOT_GROUPS], I32)
        c.group_count = sb("group_count", [1, 1], I32)
        c.group_pairs = sb("group_pairs", [1, SLOT_GROUPS], I32)
        with ExitStack() as mem:
            hT_hi = mem.enter_context(nc.sbuf_tensor("hT_hi", [P, KT, TOK], F32R))
            hT_lo = mem.enter_context(nc.sbuf_tensor("hT_lo", [P, KT, TOK], F32R))
            phase_norm(c, hT_hi, hT_lo)
            phase_project(c, hT_hi, hT_lo)
        with ExitStack() as mem:
            def cat(name):
                return mem.enter_context(nc.sbuf_tensor(name, [P, CH, TOK], F32R))

            o_hi, o_lo = cat("o_hi"), cat("o_lo")
            phase_decode(c)
            a_hi, a_lo = cat("a_hi"), cat("a_lo")
            phase_attend(c, a_hi, a_lo, o_hi, o_lo)
            phase_mix_out(c, a_hi, a_lo, o_hi, o_lo)
        c.clear_semaphores()
        with ExitStack() as mem:
            raw = mem.enter_context(nc.sbuf_tensor("expert_raw", [P, RAW, D], F32))
            raw_loaded = c.sems("raw_loaded", RAW)
            phase_route(c, raw, raw_loaded)
            phase_experts(c, raw, raw_loaded)
        phase_final(c)


def kernel(x_prompt, x_sample, cache_k, cache_v, state_conv, norm_mix, w_in, conv_w, lambda_q1, lambda_k1, lambda_q2,
           lambda_k2, head_norm, w_out, norm_ffn, w_router_group, b_router_group, w_router_expert, b_router_expert,
           w_expert_in, w_expert_out, norm_final):
    import concourse.bacc as bacc
    from concourse.bass_utils import run_bass_kernel_spmd

    a = np.asarray
    arrays = dict(
        x=np.concatenate([a(x_prompt)[0], a(x_sample).reshape(STREAMS * NEW, D)]),
        cache_k=a(cache_k).reshape(STREAMS, PAST, DC),
        cache_v=a(cache_v).reshape(STREAMS, PAST, DC),
        small=np.concatenate([a(state_conv).reshape(2 * STREAMS, DC), a(conv_w).reshape(3, DC)]),
        norm_mix=a(norm_mix).reshape(1, D),
        w_in=a(w_in)[0],
        lam=np.concatenate([a(v).reshape(1, DH) for v in (lambda_q1, lambda_k1, lambda_q2, lambda_k2)], axis=1),
        head_norm=a(head_norm).reshape(1, VD),
        w_out=a(w_out)[0],
        norm_ffn=a(norm_ffn).reshape(1, D),
        w_router=np.concatenate([a(w_router_group)[0], a(w_router_expert)[0]], axis=1),
        b_router=np.concatenate([a(b_router_group), a(b_router_expert)], axis=1),
        w_ei=a(w_expert_in)[0],
        w_eo=a(w_expert_out)[0],
        norm_final=a(norm_final).reshape(1, D),
    )
    nc = bacc.Bacc("TRN2", target_bir_lowering=False, num_devices=1)
    tensors = {}
    for name in arrays:
        arrays[name] = np.ascontiguousarray(arrays[name])
        tensors[name] = nc.dram_tensor(name, arrays[name].shape, F32, kind="ExternalInput").ap()
    outs = dict(y_all=(TOK, D), k_all=(TOK, DC), v_all=(TOK, DC), conv_all=(2 + 2 * STREAMS, DC))
    for name, shape in outs.items():
        tensors[name] = nc.dram_tensor(name, shape, F32, kind="ExternalOutput").ap()
    build(nc, Dram(**tensors))
    got = run_bass_kernel_spmd(nc, [arrays], core_ids=[0]).results[0]
    y, k, v, conv = (got[name] for name in outs)
    return (
        y[:PROMPT].reshape(1, PROMPT, D), y[PROMPT:].reshape(STREAMS, NEW, D),
        k[:PROMPT].reshape(1, 1, PROMPT, HEADS, 2, DH), v[:PROMPT].reshape(1, 1, PROMPT, HEADS, VD),
        conv[:2].reshape(1, 1, 2, DC),
        k[PROMPT:].reshape(1, STREAMS, NEW, HEADS, 2, DH), v[PROMPT:].reshape(1, STREAMS, NEW, HEADS, VD),
        conv[2:].reshape(1, STREAMS, 2, DC),
    )
```
